# Optimizing a Trainium2 kernel written in Bass

```python
import math
import jax, jax.numpy as jnp
from jax import lax
import numpy as np
import jax
import jax.numpy as jnp

D_MODEL = 1024
BATCH = 1
SEQ = 256
DEPTH = 1

CHUNK = 64
D_MIX = 2 * D_MODEL
SSD_WIDTH = D_MIX // 2
SSD_HEAD_DIM = 64
SSD_HEADS = SSD_WIDTH // SSD_HEAD_DIM
SSD_GROUPS = 2
SSD_HPG = SSD_HEADS // SSD_GROUPS
SSD_STATE = 128
SSD_CONV = 4
SSD_CONV_CH = SSD_WIDTH + 2 * SSD_GROUPS * SSD_STATE
SC_WIDTH = D_MIX - SSD_WIDTH
SC_GROUP_DIM = 64
SC_GROUPS = SC_WIDTH // SC_GROUP_DIM
SC_CONV = 3
IN_COLS = SSD_WIDTH + SSD_CONV_CH + SSD_HEADS + 3 * SC_WIDTH
N_EXPERT_GROUPS = 4
EXPERTS_PER_GROUP = 8
N_EXPERTS = N_EXPERT_GROUPS * EXPERTS_PER_GROUP
TOP_K_IN_GROUP = 2
D_FF_EXPERT = D_MODEL // 2
EXPERT_BLOCK = 128
EPS = 1e-6


def rmsnorm(x, g):
    xf = x.astype(jnp.float32)
    y = xf * lax.rsqrt(jnp.mean(xf * xf, axis=-1, keepdims=True) + EPS)
    return (y * g.astype(jnp.float32)).astype(x.dtype)

def grouped_rmsnorm(x, g, n_groups):
    shp = x.shape
    xf = x.astype(jnp.float32).reshape(*shp[:-1], n_groups, shp[-1] // n_groups)
    y = xf * lax.rsqrt(jnp.mean(xf * xf, axis=-1, keepdims=True) + EPS)
    return (y.reshape(shp) * g.astype(jnp.float32)).astype(x.dtype)

def causal_depthwise_conv(x, w):
    k = w.shape[0]
    return lax.conv_general_dilated(
        x, w[:, None, :].astype(x.dtype), window_strides=(1,), padding=[(k - 1, 0)],
        dimension_numbers=("NWC", "WIO", "NWC"), feature_group_count=x.shape[-1])

def ssd_chunked_scan(x, dt, a, bmat, cmat):
    bsz, seqlen = x.shape[0], x.shape[1]
    nc = seqlen // CHUNK
    f32 = jnp.float32
    xdt = (x.astype(f32) * dt[..., None]).reshape(bsz, nc, CHUNK, SSD_GROUPS, SSD_HPG, SSD_HEAD_DIM)
    bc = bmat.astype(f32).reshape(bsz, nc, CHUNK, SSD_GROUPS, SSD_STATE)
    cc = cmat.astype(f32).reshape(bsz, nc, CHUNK, SSD_GROUPS, SSD_STATE)
    a_dt = (dt * a.astype(f32)).reshape(bsz, nc, CHUNK, SSD_GROUPS, SSD_HPG)
    ac = jnp.cumsum(a_dt, axis=2).transpose(0, 1, 3, 4, 2)
    seg = ac[..., :, None] - ac[..., None, :]
    causal = jnp.tril(jnp.ones((CHUNK, CHUNK), dtype=bool))
    decay_in = jnp.exp(jnp.where(causal, seg, -jnp.inf))
    cb = jnp.einsum("bclgn,bcsgn->bcgls", cc, bc)
    y_diag = jnp.einsum("bcgls,bcgrls,bcsgrp->bclgrp", cb, decay_in, xdt)
    decay_to_end = jnp.exp(ac[..., -1:] - ac)
    states = jnp.einsum("bclgn,bcgrl,bclgrp->bcgrpn", bc, decay_to_end, xdt)
    chunk_decay = jnp.exp(ac[..., -1])

    def step(carry, inp):
        st, dec = inp
        return carry * dec[..., None, None] + st, carry

    init = jnp.zeros((bsz, SSD_GROUPS, SSD_HPG, SSD_HEAD_DIM, SSD_STATE), f32)
    _, prev = lax.scan(step, init, (jnp.moveaxis(states, 1, 0), jnp.moveaxis(chunk_decay, 1, 0)))
    prev = jnp.moveaxis(prev, 0, 1)
    y_off = jnp.einsum("bclgn,bcgrpn,bcgrl->bclgrp", cc, prev, jnp.exp(ac))
    return (y_diag + y_off).reshape(bsz, seqlen, SSD_HEADS, SSD_HEAD_DIM)

def hybrid_mixer(hn, w_in, ssd_conv_w, ssd_conv_b, dt_bias, a_log, d_skip, ssd_norm,
                 sc_conv_w, sc_norm, w_out):
    bsz, seqlen, _ = hn.shape
    proj = hn @ w_in
    o1 = SSD_WIDTH
    o2 = o1 + SSD_CONV_CH
    o3 = o2 + SSD_HEADS
    o4 = o3 + SC_WIDTH
    o5 = o4 + SC_WIDTH
    z, xbc, dt_raw, sc_b, sc_c, sc_v = jnp.split(proj, [o1, o2, o3, o4, o5], axis=-1)
    xbc = jax.nn.silu(causal_depthwise_conv(xbc, ssd_conv_w) + ssd_conv_b)
    xs, bm, cm = jnp.split(xbc, [SSD_WIDTH, SSD_WIDTH + SSD_GROUPS * SSD_STATE], axis=-1)
    dt = jax.nn.softplus(dt_raw.astype(jnp.float32) + dt_bias.astype(jnp.float32))
    a = -jnp.exp(a_log.astype(jnp.float32))
    xh = xs.reshape(bsz, seqlen, SSD_HEADS, SSD_HEAD_DIM)
    y = ssd_chunked_scan(xh, dt, a,
                         bm.reshape(bsz, seqlen, SSD_GROUPS, SSD_STATE),
                         cm.reshape(bsz, seqlen, SSD_GROUPS, SSD_STATE))
    y = y + d_skip.astype(jnp.float32)[:, None] * xh.astype(jnp.float32)
    y = y.reshape(bsz, seqlen, SSD_WIDTH).astype(hn.dtype)
    ssd_out = grouped_rmsnorm(y * jax.nn.silu(z), ssd_norm, SSD_GROUPS)
    sc = sc_b * causal_depthwise_conv(sc_c * sc_v, sc_conv_w)
    sc_out = grouped_rmsnorm(sc, sc_norm, SC_GROUPS)
    return jnp.concatenate([ssd_out, sc_out], axis=-1) @ w_out

def hierarchical_moe(hn, w_router_group, w_router_expert, w_gate, w_up, w_down):
    bsz, seqlen, d = hn.shape
    tokens = hn.reshape(-1, d)
    n = tokens.shape[0]
    g_logits = (tokens @ w_router_group).astype(jnp.float32)
    g_probs = jax.nn.softmax(g_logits, axis=-1)
    g_idx = jnp.argmax(g_logits, axis=-1)
    g_w = jnp.take_along_axis(g_probs, g_idx[:, None], axis=1)
    e_logits = jnp.einsum("nd,gde->nge", tokens, w_router_expert).astype(jnp.float32)
    e_sel = jnp.take_along_axis(e_logits, g_idx[:, None, None], axis=1)[:, 0]
    top_v, top_i = lax.top_k(e_sel, TOP_K_IN_GROUP)
    gates = g_w * jax.nn.softmax(top_v, axis=-1)
    expert_id = (g_idx[:, None] * EXPERTS_PER_GROUP + top_i).reshape(-1).astype(jnp.int32)
    token_id = jnp.repeat(jnp.arange(n, dtype=jnp.int32), TOP_K_IN_GROUP)
    gate_flat = gates.reshape(-1)
    m = n * TOP_K_IN_GROUP
    order = jnp.argsort(expert_id)
    sorted_e = expert_id[order]
    counts = jnp.bincount(expert_id, length=N_EXPERTS)
    padded_counts = ((counts + EXPERT_BLOCK - 1) // EXPERT_BLOCK) * EXPERT_BLOCK
    padded_end = jnp.cumsum(padded_counts)
    padded_start = padded_end - padded_counts
    start = jnp.cumsum(counts) - counts
    rank = jnp.arange(m, dtype=jnp.int32) - start[sorted_e]
    dest = padded_start[sorted_e] + rank
    p_rows = ((m + N_EXPERTS * EXPERT_BLOCK + EXPERT_BLOCK - 1) // EXPERT_BLOCK) * EXPERT_BLOCK
    n_blocks = p_rows // EXPERT_BLOCK
    row_token = jnp.zeros((p_rows,), jnp.int32).at[dest].set(token_id[order])
    row_gate = jnp.zeros((p_rows,), jnp.float32).at[dest].set(gate_flat[order])
    block_expert = jnp.clip(
        jnp.searchsorted(padded_end, jnp.arange(n_blocks) * EXPERT_BLOCK, side="right"),
        0, N_EXPERTS - 1).astype(jnp.int32)
    xs = tokens[row_token].reshape(n_blocks, EXPERT_BLOCK, d)

    def run_block(args):
        xb, e = args
        return (jax.nn.silu(xb @ w_gate[e]) * (xb @ w_up[e])) @ w_down[e]

    ys = lax.map(run_block, (xs, block_expert)).reshape(p_rows, d)
    out = jnp.zeros((n, d), jnp.float32).at[row_token].add(ys.astype(jnp.float32) * row_gate[:, None])
    return out.reshape(bsz, seqlen, d).astype(hn.dtype)

def first_inputs(seed: int = 0) -> dict:
    key = jax.random.key(seed)
    ks = jax.random.split(key, 24)
    f32 = jnp.float32

    def nrm(k, shape, scale):
        return jax.random.normal(k, shape, f32) * scale

    x = nrm(ks[0], (BATCH, SEQ, D_MODEL), 1.0)
    norm_mix = 1.0 + nrm(ks[1], (DEPTH, D_MODEL), 0.02)
    w_in = nrm(ks[2], (DEPTH, D_MODEL, IN_COLS), D_MODEL ** -0.5)
    ssd_conv_w = nrm(ks[3], (DEPTH, SSD_CONV, SSD_CONV_CH), SSD_CONV ** -0.5)
    ssd_conv_b = nrm(ks[4], (DEPTH, SSD_CONV_CH), 0.01)
    dt0 = jnp.exp(jax.random.uniform(ks[5], (DEPTH, SSD_HEADS), f32,
                                     minval=math.log(1e-3), maxval=math.log(1e-1)))
    dt_bias = dt0 + jnp.log(-jnp.expm1(-dt0))
    a_log = jnp.log(jax.random.uniform(ks[6], (DEPTH, SSD_HEADS), f32, minval=1.0, maxval=16.0))
    d_skip = 1.0 + nrm(ks[7], (DEPTH, SSD_HEADS), 0.1)
    ssd_norm = 1.0 + nrm(ks[8], (DEPTH, SSD_WIDTH), 0.02)
    sc_conv_w = nrm(ks[9], (DEPTH, SC_CONV, SC_WIDTH), SC_CONV ** -0.5)
    sc_norm = 1.0 + nrm(ks[10], (DEPTH, SC_WIDTH), 0.02)
    w_out = nrm(ks[11], (DEPTH, D_MIX, D_MODEL), D_MIX ** -0.5)
    norm_ffn = 1.0 + nrm(ks[12], (DEPTH, D_MODEL), 0.02)
    w_router_group = nrm(ks[13], (DEPTH, D_MODEL, N_EXPERT_GROUPS), D_MODEL ** -0.5)
    w_router_expert = nrm(ks[14], (DEPTH, N_EXPERT_GROUPS, D_MODEL, EXPERTS_PER_GROUP), D_MODEL ** -0.5)
    w_gate = nrm(ks[15], (DEPTH, N_EXPERTS, D_MODEL, D_FF_EXPERT), D_MODEL ** -0.5)
    w_up = nrm(ks[16], (DEPTH, N_EXPERTS, D_MODEL, D_FF_EXPERT), D_MODEL ** -0.5)
    w_down = nrm(ks[17], (DEPTH, N_EXPERTS, D_FF_EXPERT, D_MODEL), D_FF_EXPERT ** -0.5)
    final_norm = 1.0 + nrm(ks[18], (D_MODEL,), 0.02)
    return {"x": x, "norm_mix": norm_mix, "w_in": w_in, "ssd_conv_w": ssd_conv_w,
            "ssd_conv_b": ssd_conv_b, "dt_bias": dt_bias, "a_log": a_log, "d_skip": d_skip,
            "ssd_norm": ssd_norm, "sc_conv_w": sc_conv_w, "sc_norm": sc_norm, "w_out": w_out,
            "norm_ffn": norm_ffn, "w_router_group": w_router_group,
            "w_router_expert": w_router_expert, "w_gate": w_gate, "w_up": w_up,
            "w_down": w_down, "final_norm": final_norm}

def first_block(x, norm_mix, w_in, ssd_conv_w, ssd_conv_b, dt_bias, a_log, d_skip, ssd_norm,
              sc_conv_w, sc_norm, w_out, norm_ffn, w_router_group, w_router_expert,
              w_gate, w_up, w_down, final_norm):
    h = x
    for i in range(DEPTH):
        hn = rmsnorm(h, norm_mix[i])
        h = h + hybrid_mixer(hn, w_in[i], ssd_conv_w[i], ssd_conv_b[i], dt_bias[i], a_log[i],
                             d_skip[i], ssd_norm[i], sc_conv_w[i], sc_norm[i], w_out[i])
        hn = rmsnorm(h, norm_ffn[i])
        h = h + hierarchical_moe(hn, w_router_group[i], w_router_expert[i],
                                 w_gate[i], w_up[i], w_down[i])
    return rmsnorm(h, final_norm)


DEPTH_2 = 4

N_MIXERS = 3
N_FOX_LAYERS = (DEPTH_2 + 2) // 3
N_GLA_LAYERS = (DEPTH_2 + 1) // 3
N_GDN_LAYERS = DEPTH_2 // 3
RMS_EPS = 1e-6

FOX_HEADS = 8
FOX_HEAD_DIM = D_MODEL // FOX_HEADS
FOX_WIDTH = FOX_HEADS * FOX_HEAD_DIM
FOX_BLOCK = 128
FOX_FGATE_BIAS = 3.0
FOX_IN_DIM = 4 * FOX_WIDTH + FOX_HEADS

GLA_HEADS = 4
GLA_KEY_DIM = D_MODEL // 2 // GLA_HEADS
GLA_VAL_DIM = D_MODEL // GLA_HEADS
GLA_WIDTH = GLA_HEADS * GLA_VAL_DIM
GLA_RANK = 16
GLA_TAU = 16.0
GLA_CHUNK = 64
GLA_IN_DIM = 2 * GLA_HEADS * GLA_KEY_DIM + 2 * GLA_WIDTH + GLA_RANK

GDN_QK_HEADS = 4
GDN_V_HEADS = 8
GDN_HEAD_DIM = D_MODEL // GDN_V_HEADS
GDN_WIDTH = GDN_V_HEADS * GDN_HEAD_DIM
GDN_CONV = 4
GDN_CHUNK = 64
GDN_CONV_DIM = 2 * GDN_QK_HEADS * GDN_HEAD_DIM + GDN_WIDTH
GDN_IN_DIM = GDN_CONV_DIM + GDN_WIDTH + 2 * GDN_V_HEADS


def rms_norm(x, w):
    xf = x.astype(jnp.float32)
    y = xf * lax.rsqrt(jnp.mean(xf * xf, axis=-1, keepdims=True) + RMS_EPS)
    return (y * w.astype(jnp.float32)).astype(x.dtype)

def l2_norm(x):
    xf = x.astype(jnp.float32)
    return xf * lax.rsqrt(jnp.sum(xf * xf, axis=-1, keepdims=True) + RMS_EPS)

def to_chunks(t, chunk):
    b, s, h = t.shape[:3]
    t = t.reshape((b, s // chunk, chunk, h) + t.shape[3:])
    return jnp.moveaxis(t, 3, 1)

def from_chunks(t):
    b, h, nc, l, d = t.shape
    return jnp.moveaxis(t, 1, 3).reshape(b, nc * l, h, d)

def causal_conv(u, w):
    k, c = w.shape
    return lax.conv_general_dilated(u, w[:, None, :].astype(u.dtype), window_strides=(1,), padding=[(k - 1, 0)], dimension_numbers=('NWC', 'WIO', 'NWC'), feature_group_count=c)

def fox_mixer(xn, w_in, b_f, q_gain, k_gain, w_out):
    bsz, s, _ = xn.shape
    h, dh = FOX_HEADS, FOX_HEAD_DIM
    q, k, v, z, f_logit = jnp.split(xn @ w_in, [FOX_WIDTH, 2 * FOX_WIDTH, 3 * FOX_WIDTH, 4 * FOX_WIDTH], axis=-1)
    q = rms_norm(q.reshape(bsz, s, h, dh), q_gain).transpose(0, 2, 1, 3)
    k = rms_norm(k.reshape(bsz, s, h, dh), k_gain).transpose(0, 2, 1, 3)
    v = v.reshape(bsz, s, h, dh).transpose(0, 2, 1, 3)
    log_f = jax.nn.log_sigmoid((f_logit + b_f).astype(jnp.float32))
    cum = jnp.cumsum(log_f, axis=1).transpose(0, 2, 1)
    nb = s // FOX_BLOCK
    q_blocks = q.reshape(bsz, h, nb, FOX_BLOCK, dh).transpose(2, 0, 1, 3, 4)
    c_blocks = cum.reshape(bsz, h, nb, FOX_BLOCK).transpose(2, 0, 1, 3)
    pos_blocks = jnp.arange(s).reshape(nb, FOX_BLOCK)
    key_pos = jnp.arange(s)
    scale = dh ** -0.5

    def attend_block(blk):
        qb, cb, pb = blk
        logits = jnp.einsum('bhqd,bhkd->bhqk', qb, k).astype(jnp.float32) * scale + (cb[..., :, None] - cum[..., None, :])
        logits = jnp.where(pb[:, None] >= key_pos[None, :], logits, -jnp.inf)
        p = jax.nn.softmax(logits, axis=-1).astype(v.dtype)
        return jnp.einsum('bhqk,bhkd->bhqd', p, v)

    o = lax.map(attend_block, (q_blocks, c_blocks, pos_blocks))
    o = o.transpose(1, 0, 3, 2, 4).reshape(bsz, s, FOX_WIDTH)
    return (o * jax.nn.silu(z)) @ w_out

def gla_mixer(xn, w_in, w_gate_up, b_gate, o_gain, w_out):
    bsz, s, _ = xn.shape
    h, dk, dv, L = GLA_HEADS, GLA_KEY_DIM, GLA_VAL_DIM, GLA_CHUNK
    f32 = jnp.float32
    qk_w = h * dk
    q, k, v, z, g_low = jnp.split(xn @ w_in, [qk_w, 2 * qk_w, 2 * qk_w + GLA_WIDTH, 2 * qk_w + 2 * GLA_WIDTH], axis=-1)
    log_a = jax.nn.log_sigmoid((g_low @ w_gate_up + b_gate).astype(f32)) / GLA_TAU
    qc = to_chunks(q.reshape(bsz, s, h, dk).astype(f32) * dk ** -0.5, L)
    kc = to_chunks(k.reshape(bsz, s, h, dk).astype(f32), L)
    vc = to_chunks(v.reshape(bsz, s, h, dv).astype(f32), L)
    ac = to_chunks(log_a.reshape(bsz, s, h, dk), L)
    bcum = jnp.cumsum(ac, axis=3)
    b_last = bcum[..., -1:, :]
    q_dec = qc * jnp.exp(bcum)
    k_inv = kc * jnp.exp(-bcum)
    k_dec = kc * jnp.exp(b_last - bcum)
    causal = jnp.tril(jnp.ones((L, L), dtype=bool))
    attn = jnp.where(causal, jnp.einsum('bhnld,bhnmd->bhnlm', q_dec, k_inv), 0.0)
    o_intra = jnp.einsum('bhnlm,bhnmv->bhnlv', attn, vc)

    def step(state, inp):
        qd, kd, vv, dec = inp
        o = jnp.einsum('bhld,bhdv->bhlv', qd, state)
        state = state * dec[..., :, None] + jnp.einsum('bhld,bhlv->bhdv', kd, vv)
        return state, o

    xs = (jnp.moveaxis(q_dec, 2, 0), jnp.moveaxis(k_dec, 2, 0), jnp.moveaxis(vc, 2, 0), jnp.moveaxis(jnp.exp(b_last[..., 0, :]), 2, 0))
    state0 = jnp.zeros((bsz, h, dk, dv), f32)
    _, o_inter = lax.scan(step, state0, xs)
    o = o_intra + jnp.moveaxis(o_inter, 0, 2)
    o = rms_norm(from_chunks(o), o_gain).reshape(bsz, s, GLA_WIDTH).astype(xn.dtype)
    return (o * jax.nn.silu(z)) @ w_out

def gdn_mixer(xn, w_in, conv_w, a_log, dt_bias, o_gain, w_out):
    bsz, s, _ = xn.shape
    hq, hv, d, L = GDN_QK_HEADS, GDN_V_HEADS, GDN_HEAD_DIM, GDN_CHUNK
    f32 = jnp.float32
    qkv, z, a, b = jnp.split(xn @ w_in, [GDN_CONV_DIM, GDN_CONV_DIM + GDN_WIDTH, GDN_CONV_DIM + GDN_WIDTH + hv], axis=-1)
    qkv = jax.nn.silu(causal_conv(qkv, conv_w))
    q, k, v = jnp.split(qkv, [hq * d, 2 * hq * d], axis=-1)
    rep = hv // hq
    q = jnp.repeat(l2_norm(q.reshape(bsz, s, hq, d)), rep, axis=2) * d ** -0.5
    k = jnp.repeat(l2_norm(k.reshape(bsz, s, hq, d)), rep, axis=2)
    v = v.reshape(bsz, s, hv, d).astype(f32)
    beta = jax.nn.sigmoid(b.astype(f32))
    g = -jnp.exp(a_log) * jax.nn.softplus(a.astype(f32) + dt_bias)
    qc, kc, vc = to_chunks(q, L), to_chunks(k, L), to_chunks(v, L)
    bc = to_chunks(beta, L)
    gc = jnp.cumsum(to_chunks(g, L), axis=-1)
    causal = jnp.tril(jnp.ones((L, L), dtype=bool))
    strict = jnp.tril(jnp.ones((L, L), dtype=bool), k=-1)
    diff = gc[..., :, None] - gc[..., None, :]
    decay = jnp.where(causal, jnp.exp(jnp.where(causal, diff, 0.0)), 0.0)
    kb = kc * bc[..., None]
    vb = vc * bc[..., None]
    tri = jnp.where(strict, jnp.einsum('bhnld,bhnmd->bhnlm', kb, kc) * decay, 0.0) + jnp.eye(L, dtype=f32)
    u = lax.linalg.triangular_solve(tri, vb, left_side=True, lower=True)
    w = lax.linalg.triangular_solve(tri, kb * jnp.exp(gc)[..., None], left_side=True, lower=True)
    qk = jnp.einsum('bhnld,bhnmd->bhnlm', qc, kc) * decay
    q_dec = qc * jnp.exp(gc)[..., None]
    g_last = gc[..., -1]
    k_dec = kc * jnp.exp(g_last[..., None] - gc)[..., None]

    def step(state, inp):
        uu, ww, qkk, qd, kd, dec = inp
        v_new = uu - jnp.einsum('bhld,bhdv->bhlv', ww, state)
        o = jnp.einsum('bhld,bhdv->bhlv', qd, state) + jnp.einsum('bhlm,bhmv->bhlv', qkk, v_new)
        state = state * dec[..., None, None] + jnp.einsum('bhld,bhlv->bhdv', kd, v_new)
        return state, o

    xs = tuple(jnp.moveaxis(t, 2, 0) for t in (u, w, qk, q_dec, k_dec, jnp.exp(g_last)))
    state0 = jnp.zeros((bsz, hv, d, d), f32)
    _, o_inter = lax.scan(step, state0, xs)
    o = from_chunks(jnp.moveaxis(o_inter, 0, 2))
    o = rms_norm(o, o_gain).reshape(bsz, s, GDN_WIDTH).astype(xn.dtype)
    return (o * jax.nn.silu(z)) @ w_out

def second_inputs(seed: int = 0) -> dict:
    key = jax.random.key(seed)
    ks = jax.random.split(key, 20)
    f32 = jnp.float32

    def nrm(k, shape, scale):
        return jax.random.normal(k, shape, f32) * scale

    x = nrm(ks[0], (BATCH, SEQ, D_MODEL), 1.0)
    norm_w = 1.0 + nrm(ks[1], (DEPTH_2, D_MODEL), 0.02)
    fox_w_in = nrm(ks[2], (N_FOX_LAYERS, D_MODEL, FOX_IN_DIM), D_MODEL ** -0.5)
    fox_b_f = FOX_FGATE_BIAS + nrm(ks[3], (N_FOX_LAYERS, FOX_HEADS), 0.5)
    fox_q_gain = 1.0 + nrm(ks[4], (N_FOX_LAYERS, FOX_HEAD_DIM), 0.02)
    fox_k_gain = 1.0 + nrm(ks[5], (N_FOX_LAYERS, FOX_HEAD_DIM), 0.02)
    fox_w_out = nrm(ks[6], (N_FOX_LAYERS, FOX_WIDTH, D_MODEL), FOX_WIDTH ** -0.5)
    gla_w_in = nrm(ks[7], (N_GLA_LAYERS, D_MODEL, GLA_IN_DIM), D_MODEL ** -0.5)
    gla_w_gate_up = nrm(ks[8], (N_GLA_LAYERS, GLA_RANK, GLA_HEADS * GLA_KEY_DIM), GLA_RANK ** -0.5)
    gla_b_gate = nrm(ks[9], (N_GLA_LAYERS, GLA_HEADS * GLA_KEY_DIM), 0.1)
    gla_o_gain = 1.0 + nrm(ks[10], (N_GLA_LAYERS, GLA_VAL_DIM), 0.02)
    gla_w_out = nrm(ks[11], (N_GLA_LAYERS, GLA_WIDTH, D_MODEL), GLA_WIDTH ** -0.5)
    gdn_w_in = nrm(ks[12], (N_GDN_LAYERS, D_MODEL, GDN_IN_DIM), D_MODEL ** -0.5)
    gdn_conv_w = nrm(ks[13], (N_GDN_LAYERS, GDN_CONV, GDN_CONV_DIM), GDN_CONV ** -0.5)
    gdn_a_log = jnp.log(jax.random.uniform(ks[14], (N_GDN_LAYERS, GDN_V_HEADS), f32, minval=1.0, maxval=16.0))
    dt = jnp.exp(jax.random.uniform(ks[15], (N_GDN_LAYERS, GDN_V_HEADS), f32, minval=math.log(1e-3), maxval=math.log(1e-1)))
    gdn_dt_bias = dt + jnp.log(-jnp.expm1(-dt))
    gdn_o_gain = 1.0 + nrm(ks[16], (N_GDN_LAYERS, GDN_HEAD_DIM), 0.02)
    gdn_w_out = nrm(ks[17], (N_GDN_LAYERS, GDN_WIDTH, D_MODEL), GDN_WIDTH ** -0.5)
    return {'x': x, 'norm_w': norm_w,
            'fox_w_in': fox_w_in, 'fox_b_f': fox_b_f, 'fox_q_gain': fox_q_gain, 'fox_k_gain': fox_k_gain, 'fox_w_out': fox_w_out,
            'gla_w_in': gla_w_in, 'gla_w_gate_up': gla_w_gate_up, 'gla_b_gate': gla_b_gate, 'gla_o_gain': gla_o_gain, 'gla_w_out': gla_w_out,
            'gdn_w_in': gdn_w_in, 'gdn_conv_w': gdn_conv_w, 'gdn_a_log': gdn_a_log, 'gdn_dt_bias': gdn_dt_bias, 'gdn_o_gain': gdn_o_gain, 'gdn_w_out': gdn_w_out}

def second_block(x, norm_w, fox_w_in, fox_b_f, fox_q_gain, fox_k_gain, fox_w_out, gla_w_in, gla_w_gate_up, gla_b_gate, gla_o_gain, gla_w_out, gdn_w_in, gdn_conv_w, gdn_a_log, gdn_dt_bias, gdn_o_gain, gdn_w_out):
    for layer in range(DEPTH_2):
        xn = rms_norm(x, norm_w[layer])
        kind, idx = layer % N_MIXERS, layer // N_MIXERS
        if kind == 0:
            y = fox_mixer(xn, fox_w_in[idx], fox_b_f[idx], fox_q_gain[idx], fox_k_gain[idx], fox_w_out[idx])
        elif kind == 1:
            y = gla_mixer(xn, gla_w_in[idx], gla_w_gate_up[idx], gla_b_gate[idx], gla_o_gain[idx], gla_w_out[idx])
        else:
            y = gdn_mixer(xn, gdn_w_in[idx], gdn_conv_w[idx], gdn_a_log[idx], gdn_dt_bias[idx], gdn_o_gain[idx], gdn_w_out[idx])
        x = x + y.astype(x.dtype)
    return x


def setup_inputs(seed=0):
    out = dict(first_inputs(seed))
    for name, value in second_inputs(seed + 1).items():
        if name != "x":
            out[name + "_2"] = value
    return out


def reference(
    x, norm_mix, w_in, ssd_conv_w, ssd_conv_b, dt_bias, a_log, d_skip, ssd_norm, sc_conv_w,
    sc_norm, w_out, norm_ffn, w_router_group, w_router_expert, w_gate, w_up, w_down, final_norm,
    norm_w_2, fox_w_in_2, fox_b_f_2, fox_q_gain_2, fox_k_gain_2, fox_w_out_2, gla_w_in_2,
    gla_w_gate_up_2, gla_b_gate_2, gla_o_gain_2, gla_w_out_2, gdn_w_in_2, gdn_conv_w_2,
    gdn_a_log_2, gdn_dt_bias_2, gdn_o_gain_2, gdn_w_out_2,
):
    x = first_block(
        x, norm_mix, w_in, ssd_conv_w, ssd_conv_b, dt_bias, a_log, d_skip, ssd_norm, sc_conv_w,
        sc_norm, w_out, norm_ffn, w_router_group, w_router_expert, w_gate, w_up, w_down,
        final_norm,
    )
    return second_block(
        x, norm_w_2, fox_w_in_2, fox_b_f_2, fox_q_gain_2, fox_k_gain_2, fox_w_out_2, gla_w_in_2,
        gla_w_gate_up_2, gla_b_gate_2, gla_o_gain_2, gla_w_out_2, gdn_w_in_2, gdn_conv_w_2,
        gdn_a_log_2, gdn_dt_bias_2, gdn_o_gain_2, gdn_w_out_2,
    )


_drawn_inputs = setup_inputs


def setup_inputs(seed=0):
    import zlib

    import numpy as np

    out = dict(_drawn_inputs(seed))
    spreads = {}
    factors = {'fox_q_gain_2': 8.0, 'fox_k_gain_2': 8.0, 'gla_o_gain_2': 4.555, 'gdn_o_gain_2': 5.685}
    for name, (base, spread) in spreads.items():
        noise = np.random.default_rng([zlib.crc32(name.encode()), seed]).standard_normal(out[name].shape)
        drawn = base * np.exp(spread * noise) if base else spread * noise
        out[name] = jnp.asarray(drawn.astype(out[name].dtype))
    for name, factor in factors.items():
        out[name] = (out[name] * factor).astype(out[name].dtype)
    return out
```

```python
from contextlib import ExitStack

import concourse.bass as bass
from concourse import mybir

F32 = mybir.dt.float32
I32 = mybir.dt.int32
ALU = mybir.AluOpType
ACT = mybir.ActivationFunctionType
AX = mybir.AxisListType

P = 128
T = 256
NT = T // P
D = 1024
KD = D // P
BLK = 512
EPS = 1e-6
RSQRT_SEED = 1597463007.0

SLOTS = 6
SLOT = KD * BLK

SSD_H, SSD_N = 16, 128
SSD_W, SSD_XBC = 1024, 1536
FOX_H = 8
GLA_H, GLA_DK, GLA_DV, GLA_CH = 4, 128, 256, 64
GDN_QH, GDN_VH = 4, 8
NG, EPG = 4, 8
NE = NG * EPG
QUAD = 4
CAP = P // QUAD
NQ = NE // QUAD
FF = 512
STEPS_UP, STEPS_DOWN = KD, FF // P
MOE_STEPS = STEPS_UP + STEPS_DOWN

VEC_A = [("ssd_conv_w", 48), ("ssd_conv_b", 12), ("ssd_norm", 8), ("sc_conv_w", 24), ("sc_norm", 8),
         ("norm_mix", 8), ("norm_ffn", 8), ("fox_q_gain", 2), ("fox_k_gain", 2), ("gla_o_gain", 2),
         ("gla_b_gate", 4), ("gdn_o_gain", 1)]
VEC_B = [("norm_w", 32), ("gdn_conv_w", 64)]
NA = sum(n for _, n in VEC_A)
NB = sum(n for _, n in VEC_B)
VCOL = {}
for _tab, _start in ((VEC_A, 0), (VEC_B, P)):
    for _name, _n in _tab:
        VCOL[_name] = _start
        _start += _n

LAYERS = ["ssd", "fox0", "gla", "gdn", "fox1"]
PROJ_BLOCKS = {"ssd": 11, "fox0": 8, "gla": 6, "gdn": 6, "fox1": 8}
PROJ_BASE, _n = {}, 0
for _l in LAYERS:
    PROJ_BASE[_l] = _n
    _n += 2 * PROJ_BLOCKS[_l]

RING_BASE, _n = {}, 0
for _l in LAYERS:
    RING_BASE[_l] = _n
    _n += PROJ_BLOCKS[_l]
    RING_BASE[_l + "_out"] = _n
    _n += 4 if _l == "ssd" else 2
    if _l == "ssd":
        RING_BASE["moe"] = _n
        _n += NQ * MOE_STEPS

ROWN = {}
_n = 0
for _name, _tiles in (("sc", 8), ("ssd", 8), ("fox0", 16), ("gla", 8), ("gdn_qk", 8), ("gdn_o", 8), ("fox1", 16)):
    ROWN[_name] = (len(ROWN), _n, _tiles)
    _n += _tiles

SOFT_USE = {"ssd": 1, "fox0": 2, "gdn": 3, "fox1": 4}
ROW_USE = {"ssd": 1, "fox0": 2, "gdn": 3, "fox1": 4}
SUM_BANK = {name: 1 if name == "ssd" else 4 for name in ROWN}

X_BEFORE = {"moe": 4, "fox0": 6, "gla": 10, "gdn": 14, "fox1": 18, "end": 22}
NORMS = ["ssd", "moe", "fox0", "gla", "gdn", "fox1"]
SQS = ["ssd", "moe", "final", "fox0", "gla", "gdn", "fox1"]


def build(nc, x_in, norm_mix, w_in, ssd_conv_w, ssd_conv_b, dt_bias, a_log, d_skip, ssd_norm, sc_conv_w,
          sc_norm, w_out, norm_ffn, w_router_group, w_router_expert, w_gate, w_up, w_down, final_norm,
          norm_w, fox_w_in, fox_b_f, fox_q_gain, fox_k_gain, fox_w_out, gla_w_in, gla_w_gate_up, gla_b_gate,
          gla_o_gain, gla_w_out, gdn_w_in, gdn_conv_w, gdn_a_log, gdn_dt_bias, gdn_o_gain, gdn_w_out, out,
          upto="all"):
    ctx = ExitStack()
    with ctx:
        def sb(name, shape, dt=F32):
            return ctx.enter_context(nc.sbuf_tensor(name, shape, dt))

        def sem(name):
            return ctx.enter_context(nc.semaphore(name))

        ring = sb("ring", [P, SLOTS, SLOT])
        x_res = sb("x_res", [P, NT, D])
        hn = sb("hn", [P, NT, D])
        hnT = sb("hnT", [P, KD, T])
        cm = sb("cm", [P, 44, T])
        vtm = sb("vtm", [P, NT, D])
        sq = sb("sq", [P, 2, 4, T])
        rowsel = sb("rowsel", [16, 16, P])
        onehot = sb("onehot", [P, 32])
        colsel64 = sb("colsel64", [P, 8, 16])
        ident = sb("ident", [P, P])
        ones = sb("ones", [P, P])
        qgain = sb("qgain", [P, 1])
        upper = sb("upper", [P, P])
        supper = sb("supper", [P, P])
        slower = sb("slower", [P, P])
        upper64 = sb("upper64", [P, P])
        lastrow = sb("lastrow", [P, P])
        negmask = sb("negmask", [P, 2, P])
        iota_i = sb("iota_i", [P, CAP], I32)
        iota = sb("iota", [P, CAP])
        vec = sb("vec", [P, 2 * P])
        ss = sb("ss", [P, 8])
        w_dt = sb("w_dt", [P, KD, SSD_H])
        w_f = sb("w_f", [P, 2, KD, FOX_H])
        w_low = sb("w_low", [P, KD, 16])
        w_ab = sb("w_ab", [P, KD, 16])
        w_rt = sb("w_rt", [P, KD, NG + NE])
        w_gup = sb("w_gup", [16, BLK])
        cols = sb("cols", [16, 8])
        ncols = sb("ncols", [16, 2])
        dsk = sb("dsk", [P, 8])
        rrow = sb("rrow", [16, 3, T])
        rows = sb("rows", [16, 4, T])
        tok = sb("tok", [P, 8, 16])
        count_i = sb("count_i", [1, 1], I32)

        bank = [ctx.enter_context(nc.psum_tensor(f"bank{i}", [P, 512], F32)) for i in range(8)]

        cmf = cm[:].rearrange("p a b -> p (a b)")
        hnTf = hnT[:].rearrange("p a b -> p (a b)")

        def tiles(a, n, inner=T):
            return cmf[:, a * T:(a + n) * T].rearrange("p (n i) -> p n i", i=inner)

        def b2(i):
            return bank[i][:].rearrange("p (a b) -> p a b", b=T)

        def b4(i):
            return bank[i][:].rearrange("p (a b) -> p a b", b=P)

        s = {n: sem(n) for n in (
            "x_loaded", "vec_loaded", "small_loaded", "fnorm_loaded", "out_stored", "ring_used",
            "pool_chain", "consts_ready", "cv_ready",
            "dve_chain", "act_chain", "moe_chain", "pass_chain", "sp_turn",
            "vec_turned", "vec_ready", "cols_ready",
            "ss_ready", "xn_ready", "turned", "hnT_act", "hnT_dve", "x_ready",
            "proj_done", "proj_copied", "small_done",
            "sq_ready", "sq_summed", "rownorm_ready", "spread_done", "spread_used",
            "outT_ready", "outp_done",
            "lin_ready", "tanh_ready", "z_tanh", "z_ready",
            "row_arg", "qk_ready", "row_ln", "row_ready", "row_turned", "col_ready",
            "ssd_conv_done", "ssd_xt_done", "ssd_xt_used", "ssd_g_done", "ssd_bc", "ssd_seg", "ssd_exp",
            "ssd_m", "ssd_y", "ssd_dte_arg", "ssd_dte", "ssd_xdte", "ssd_state", "ssd_state_used", "ssd_yready",
            "rt_done", "rt_arg", "rt_exp", "rt_mask", "rt_rank", "rt_passes", "moe_sel", "moe_sg", "moe_gath", "moe_xg", "moe_tanh",
            "moe_h", "moe_gt", "moe_gtc", "moe_ht", "moe_htc", "moe_ya", "moe_yd", "moe_scat", "moe_acc", "moe_done",
            
            "fox_s", "fox_l", "fox_e", "fox_p", "fox_t", "fox_tc", "fox_o", "fox_oc",
            "gla_low", "gla_gate", "gla_arg", "gla_ln", "gla_dec", "gla_exp", "gla_qk", "gla_at", "gla_atc", "gla_kt",
            "gla_ktc", "gla_st", "gla_stc", "gla_o", "gla_oc",
            "gdn_row_free", "gdn_beta_exp", "gdn_last", "gdn_col_arg", "gdn_col_exp", "gdn_conv_done", "gdn_qk_ready",
            "gdn_xt", "gdn_xtc", "gdn_kt", "gdn_ktc", "gdn_bc", "gdn_arg", "gdn_exp", "gdn_x", "gdn_turned", "gdn_q_ready",
            "gdn_qt_ready", "gdn_power", "gdn_r", "gdn_r_ready", "gdn_uw", "gdn_u_ready", "gdn_w_ready", "gdn_s",
            "gdn_s_ready", "gdn_ws", "gdn_new", "gdn_o", "gdn_oc",
        )}
        ready = [sem(f"slot_ready{i}") for i in range(SLOTS)]
        ov_ready, ov_used = sem("ov_ready"), sem("ov_used")

        earlier = sb("earlier", [P, 8, 8])

        def column(r, R):
            return onehot[:, 15 - r:15 - r + R]

        def tf(a, n):
            return cmf[:, a * T:(a + n) * T]

        used_floats = [0]

        def view(*shape):
            size = 1
            for k in shape:
                size *= k
            a = cmf[:, used_floats[0]:used_floats[0] + size]
            used_floats[0] += size
            if len(shape) == 2:
                return a.rearrange("p (a b) -> p a b", a=shape[0])
            return a

        m_xg, m_S, m_SG, m_gt = view(KD, P), view(NT, P), view(NT, P), view(T)
        m_tanh, m_silu, m_h, m_ht, m_y = view(FF), view(FF), view(FF), view(FF), view(2, BLK)
        r_lg, r_eg, r_n, r_gs, r_es, r_ex = (view(NT, NG + NE), view(NT, NG), view(NT, 2), view(NT, 1), view(NT, EPG),
                                             view(NT, EPG))
        r_c1, r_c2, r_gsel, r_sel, r_sum = view(NE, 2), view(NE, 2), view(NT, NG), view(NT, EPG), view(NT, 4)
        r_mask, r_gate, r_pm, r_pass = view(NT, NE), view(NT, NE + QUAD), view(NT, NE + QUAD), view(2, 16)
        r_prod = view(NG, EPG)
        N_SMALL = 12 + NG + 2

        f_l = [cmf[:, 24 * T + i * 384:24 * T + (i + 1) * 384] for i in (0, 1)]
        f_p = [cmf[:, 27 * T + i * 384:27 * T + (i + 1) * 384] for i in (0, 1)]
        f_pt = [cmf[:, 30 * T + i * 384:30 * T + (i + 1) * 384] for i in (0, 1)]
        f_n = tiles(33, 1, 2)[:, 0:2, :]
        f_s = tiles(33, 1, 2)[:, 2:4, :]
        f_r = tiles(33, 1, 2)[:, 4:6, :]

        g_Q, g_QT, g_R, g_dt = (hnTf[:, i * 512:(i + 1) * 512] for i in range(4))
        g_d = tf(40, 2)
        g_km, g_qm = tiles(42, 1, P), tiles(43, 1, P)
        g_w = [hn[:, 0, i * 512:(i + 1) * 512] for i in (0, 1)]
        g_qd = [hn[:, 1, i * 512:(i + 1) * 512] for i in (0, 1)]
        g_u = [tf(8 + 2 * i, 2) for i in range(4)]
        g_qkk = [tf(24 + 2 * i, 2) for i in range(4)]
        g_kbg, g_kdec = tf(32, 4), tf(36, 4)

        def slot_value(n):
            return 32 * (n // SLOTS + 1)

        def released(n):
            for li, l in enumerate(LAYERS):
                b = RING_BASE[l]
                if b <= n < b + PROJ_BLOCKS[l]:
                    return s["proj_done"], PROJ_BASE[l] + 2 * (n - b) + 2
                b = RING_BASE[l + "_out"]
                if l == "ssd" and b <= n < b + 4:
                    return s["outp_done"], 4 * li + 2 * ((n - b) // 2) + 1 + (n - b) % 2
                if l != "ssd" and b <= n < b + 2:
                    return s["outp_done"], 4 * li + 2 * (n - b) + 2
            return s["ring_used"], n - RING_BASE["moe"] + 1

        def block_halves(w, col):
            v = w[:, col:col + BLK].rearrange("(c p) n -> p c n", p=P)
            return [v[:, 0:4, :], v[:, 4:8, :]]

        up_v = [w.rearrange("(q j) (c p) f -> q c p j f", j=QUAD, p=P) for w in (w_gate, w_up)]
        down_v = w_down.rearrange("(q j) (c p) n -> q c p j n", j=QUAD, p=P)

        def slot_half(i, h):
            return ring[:, i, h * (SLOT // 2):(h + 1) * (SLOT // 2)]

        def moe_halves(i, q, j):
            if j < STEPS_UP:
                return [(slot_half(i, h).rearrange("p (e f) -> p e f", e=QUAD), up_v[h][q, j]) for h in (0, 1)]
            return [(slot_half(i, h).rearrange("p (e f) -> p e f", e=QUAD // 2),
                     down_v[q, j - STEPS_UP][:, 2 * h:2 * h + 2, :]) for h in (0, 1)]

        col_of = {
            "ssd": [SSD_W + BLK * i for i in range(3)] +
                   [SSD_W + SSD_XBC + SSD_H + D + BLK * i for i in range(4)] +
                   [SSD_W + SSD_XBC + SSD_H + BLK * i for i in range(2)] +
                   [BLK * i for i in range(2)],
            "fox0": [BLK * i for i in range(8)], "fox1": [BLK * i for i in range(8)],
            "gla": [BLK * i for i in range(6)],
            "gdn": [BLK * i for i in range(6)],
        }
        w_of = {"ssd": w_in[0], "fox0": fox_w_in[0], "gla": gla_w_in[0], "gdn": gdn_w_in[0], "fox1": fox_w_in[1]}
        wo_of = {"ssd": w_out[0], "fox0": fox_w_out[0], "gla": gla_w_out[0], "gdn": gdn_w_out[0], "fox1": fox_w_out[1]}

        stop = ["ssd", "moe", "fox0", "gla", "gdn", "all"].index(upto)
        layers = LAYERS[:[1, 1, 2, 3, 4, 5][stop]]

        block = ctx.enter_context(nc.Block())

        @block.sync
        def _(sp):
            for t in range(NT):
                sp.dma_start(x_res[:, t, :], x_in[0, t * P:(t + 1) * P, :]).then_inc(s["x_loaded"], 16)

            def put(n, halves):
                i = n % SLOTS
                if n >= SLOTS:
                    sp.wait_ge(*released(n - SLOTS))
                for dst, src in halves:
                    sp.dma_start(dst, src).then_inc(ready[i], 16)

            def put_block(n, w, col):
                halves = block_halves(w, col)
                put(n, [(slot_half(n % SLOTS, h).rearrange("p (c n) -> p c n", c=4), halves[h]) for h in (0, 1)])

            for l in layers:
                for i, col in enumerate(col_of[l]):
                    put_block(RING_BASE[l] + i, w_of[l], col)
                groups = wo_of[l].shape[0] // D
                for i in range(2 * groups):
                    rows_of = wo_of[l][(i % groups) * D:(i % groups + 1) * D, :]
                    put_block(RING_BASE[l + "_out"] + i, rows_of, BLK * (i // groups))
                if l == "ssd" and stop >= 1:
                    base = RING_BASE["moe"]
                    for j in range(SLOTS):
                        put(base + j, moe_halves((base + j) % SLOTS, 0, j))
                    for j in range(SLOTS, MOE_STEPS):
                        put(base + j, moe_halves((base + j) % SLOTS, 0, j))
                    with sp.Fori(1, NQ) as q:
                        for j in range(MOE_STEPS):
                            i = (base + j) % SLOTS
                            sp.wait_ge(s["ring_used"], q * MOE_STEPS + (j - SLOTS + 1))
                            sp.sem_inc(s["sp_turn"], 1)
                            for dst, src in moe_halves(i, q, j):
                                sp.dma_start(dst, src).then_inc(ready[i], 16)
                    sp.wait_ge(s["rt_passes"], 1)
                    passes = sp.value_load(count_i[0:1, 0:1], min_val=1, max_val=T // CAP)
                    with sp.If(passes > 1):
                        sp.wait_ge(s["ring_used"], NQ * MOE_STEPS)
                        with sp.Fori(1, passes) as p:
                            with sp.Fori(0, NQ) as q:
                                for j in range(MOE_STEPS):
                                    for dst, src in moe_halves(0, q, j):
                                        sp.dma_start(dst, src).then_inc(ov_ready, 16)
                                    sp.wait_ge(ov_used, (p - 1) * (NQ * MOE_STEPS) + q * MOE_STEPS + (j + 1))
                                    sp.sem_inc(s["sp_turn"], 1)
            last = {0: 4, 1: 6, 2: 10, 3: 14, 4: 18, 5: 22}[stop]
            sp.wait_ge(s["x_ready"], last)
            for t in range(NT):
                sp.dma_start(out[0, t * P:(t + 1) * P, :], x_res[:, t, :]).then_inc(s["out_stored"], 16)
            sp.wait_ge(s["out_stored"], 16 * NT)

        @block.gpsimd
        def _(pool):
            n = [0]

            def link(ins):
                n[0] += 1
                ins.then_inc(s["pool_chain"], 1)
                pool.wait_ge(s["pool_chain"], n[0])

            for t in (ident, onehot, colsel64, rowsel, lastrow, negmask):
                link(nc.gpsimd.memset(t[:], 0.0))
            for t in (ones, upper, supper, slower, upper64, earlier):
                link(nc.gpsimd.memset(t[:], 1.0))
            link(nc.gpsimd.iota(iota_i[:], pattern=[[1, CAP]], base=0, channel_multiplier=0))
            link(nc.gpsimd.tensor_copy(iota[:], iota_i[:]))

            def select(a, op, fill, base, pattern, cmul):
                link(nc.gpsimd.affine_select(out=a, in_=a, compare_op=op, fill=fill, base=base,
                                             pattern=pattern, channel_multiplier=cmul))

            select(lastrow[:], ALU.not_equal, 1.0, -(P - 1), [[0, P]], 1)
            select(rowsel[:], ALU.not_equal, 1.0, 0, [[-1, 16], [0, P]], 1)
            select(onehot[:], ALU.not_equal, 1.0, -15, [[1, 32]], 0)
            for half in (0, 1):
                select(colsel64[64 * half:64 * half + 64], ALU.not_equal, 1.0, half, [[2, 8], [-1, 16]], 0)
            select(upper[:], ALU.is_ge, 0.0, 0, [[1, P]], -1)
            select(supper[:], ALU.is_ge, 0.0, -1, [[1, P]], -1)
            select(slower[:], ALU.is_ge, 0.0, -1, [[-1, P]], 1)
            select(earlier[:], ALU.is_ge, 0.0, -1, [[1, 8], [-1, 8]], 0)
            select(negmask[:, 1, :], ALU.is_ge, -1e30, 0, [[-1, P]], 1)
            select(upper64[:], ALU.is_ge, 0.0, 0, [[1, P]], -1)
            select(upper64[:, 64:P], ALU.is_ge, 0.0, -64, [[0, 64]], 1)
            select(ident[:], ALU.not_equal, 1.0, 0, [[-1, P]], 1)
            pool.sem_inc(s["consts_ready"], 1)
            for b in range(4):
                pool.wait_ge(s["proj_copied"], 6 + 4 + b + 1)
                nc.gpsimd.tensor_tensor(tiles(28 + 2 * b, 2), tiles(28 + 2 * b, 2), tiles(36 + 2 * b, 2),
                                        ALU.mult).then_inc(s["cv_ready"], 1)

        @block.scalar
        def _(act):
            n_link = [0]

            def link(ins):
                n_link[0] += 1
                ins.then_inc(s["act_chain"], 1)
                act.wait_ge(s["act_chain"], n_link[0])

            af = nc.scalar.activation

            staged = [tiles(0, 1)[0:NA, 0, 0:P], tiles(1, 1)[0:NB, 0, 0:P]]
            srcs = {"ssd_conv_w": ssd_conv_w, "ssd_conv_b": ssd_conv_b, "ssd_norm": ssd_norm, "sc_conv_w": sc_conv_w,
                    "sc_norm": sc_norm, "norm_mix": norm_mix, "norm_ffn": norm_ffn, "fox_q_gain": fox_q_gain,
                    "fox_k_gain": fox_k_gain, "gla_o_gain": gla_o_gain, "gla_b_gate": gla_b_gate,
                    "gdn_o_gain": gdn_o_gain, "norm_w": norm_w, "gdn_conv_w": gdn_conv_w}
            for tab, dst in zip((VEC_A, VEC_B), staged):
                at = 0
                for name, k in tab:
                    src = srcs[name]
                    flat = src.rearrange("a b c -> (a b c)") if len(src.shape) == 3 else src.rearrange("a b -> (a b)")
                    act.dma_start(dst[at:at + k, :], flat.rearrange("(r p) -> r p", p=P)).then_inc(s["vec_loaded"], 16)
                    at += k

            small = []
            for dst, src in (
                (w_dt[:], w_in[0][:, SSD_W + SSD_XBC:SSD_W + SSD_XBC + SSD_H].rearrange("(c p) n -> p c n", p=P)),
                (w_f[:, 0], fox_w_in[0][:, 4 * D:4 * D + FOX_H].rearrange("(c p) n -> p c n", p=P)),
                (w_f[:, 1], fox_w_in[1][:, 4 * D:4 * D + FOX_H].rearrange("(c p) n -> p c n", p=P)),
                (w_low[:], gla_w_in[0][:, 3 * D:3 * D + 16].rearrange("(c p) n -> p c n", p=P)),
                (w_ab[:], gdn_w_in[0][:, 3 * D:3 * D + 16].rearrange("(c p) n -> p c n", p=P)),
                (w_rt[:, :, 0:NG], w_router_group[0].rearrange("(c p) n -> p c n", p=P)),
                (w_gup[:], gla_w_gate_up[0]),
                (cols[0:16, 0:1], a_log.rearrange("a h -> h a")), (cols[0:16, 1:2], dt_bias.rearrange("a h -> h a")),
                (cols[0:8, 2:4], fox_b_f.rearrange("a h -> h a")),
                (cols[0:8, 4:5], gdn_a_log.rearrange("a h -> h a")), (cols[0:8, 5:6], gdn_dt_bias.rearrange("a h -> h a")),
            ) + tuple((w_rt[:, :, NG + EPG * g:NG + EPG * (g + 1)],
                       w_router_expert[0, g].rearrange("(c p) n -> p c n", p=P)) for g in range(NG)) \
              + tuple((dsk[64 * h:64 * h + 64, :],
                       d_skip[0].rearrange("(i two) -> two i", two=2)[h:h + 1, :].to_broadcast([64, 8])) for h in (0, 1)):
                small.append(act.dma_start(dst, src, allow_slow_non_contiguous=True).then_inc(s["small_loaded"], 16))
            assert len(small) == N_SMALL

            def square_sum(which, value):
                if which == 0:
                    act.wait_ge(s["x_loaded"], 16 * NT)
                else:
                    act.wait_ge(s["x_ready"], value)
                for t in range(NT):
                    af(hn[:, t, :], x_res[:, t, :], ACT.Square, accum_out=ss[:, t:t + 1]).then_inc(s["ss_ready"], 1)

            def norm_copies(u, col):
                for b in (0, 2):
                    act.wait_ge(s["turned"], 4 * u + b + 1)
                    for j in (0, 1):
                        i = af(hnT[:, 2 * b + j, :], b2(6)[:, j, :], ACT.Copy,
                               scale=vec[:, col + 2 * b + j:col + 2 * b + j + 1])
                    i.then_inc(s["hnT_act"], 1)

            def copy_bank(layer, b, dst, scale=1.0):
                g = PROJ_BASE[layer] + b
                act.wait_ge(s["proj_done"], g + 1)
                af(dst, bank[g % 4][:], ACT.Copy, scale=scale).then_inc(s["proj_copied"], 1)

            def own_copies(layer, banks):
                act.wait_ge(s["proj_copied"], PROJ_BASE[layer] + banks)

            def squares(name, k, src):
                _, before, _ = ROWN[name]
                g = before // 4 + k
                if g >= 2:
                    act.wait_ge(s["sq_summed"], g - 1)
                af(sq[:, g % 2].rearrange("p a b -> p (a b)"), src, ACT.Square).then_inc(s["sq_ready"], 1)

            def silu_z(li, z0, summed):
                act.wait_ge(s["sq_summed"], summed)
                for b in (0, 1):
                    af(sq[:, b].rearrange("p a b -> p (a b)"), cmf[:, (z0 + 4 * b) * T:(z0 + 4 * b + 4) * T],
                       ACT.Tanh).then_inc(s["z_tanh"], 1)

            def softplus_row(k, src, dst, parts):
                act.wait_ge(s["row_arg"], k)
                link(af(dst[0:parts], src[0:parts], ACT.Exp, scale=-1.0))
                af(dst[0:parts], dst[0:parts], ACT.Ln, bias=1.0).then_inc(s["row_ln"], 1)

            act.wait_ge(s["small_loaded"], 16 * N_SMALL)
            af(ncols[0:16, 0:1], cols[0:16, 0:1], ACT.Exp)
            af(ncols[0:8, 1:2], cols[0:8, 4:5], ACT.Exp).then_inc(s["cols_ready"], 1)

            square_sum(0, 0)
            act.wait_ge(s["vec_ready"], 1)
            norm_copies(0, VCOL["norm_mix"])
            softplus_row(1, rows[:, 1, :], rows[:, 2, :], 16)
            for b in range(6):
                copy_bank("ssd", b, cmf[:, (8 + 2 * b) * T:(10 + 2 * b) * T])
            dst = [28 + 2 * i for i in range(4)] + [36 + 2 * i for i in range(4)] + [20 + 2 * i for i in range(4)] + \
                  [2 * i for i in range(4)]
            for b in range(16):
                copy_bank("ssd", 6 + b, cmf[:, dst[b] * T:(dst[b] + 2) * T], 0.5 if b >= 12 else 1.0)
                if b in (0, 3, 6):
                    k = b // 3
                    act.wait_ge(s["lin_ready"], k + 1)
                    af(vtm[:, 1, :], vtm[:, 0, :], ACT.Tanh).then_inc(s["tanh_ready"], 1)
            for k in range(2):
                act.wait_ge(s["ssd_conv_done"], 3 + k + 1)
                squares("sc", k, cmf[:, (36 + 4 * k) * T:(40 + 4 * k) * T])
            own_copies("ssd", 22)
            silu_z(0, 0, 2)
            act.wait_ge(s["ssd_dte_arg"], 1)
            af(tok[:, 4, :], tok[:, 4, :], ACT.Exp).then_inc(s["ssd_dte"], 1)
            for i in range(8):
                c, hq = i // 4, i % 4
                act.wait_ge(s["ssd_seg"], i + 1)
                m = hnTf[:, (i % 2) * 512:(i % 2) * 512 + 512]
                if c == 1:
                    ce = hnTf[:, 1024 + (i % 2) * 512:1536 + (i % 2) * 512]
                    if i >= 6:
                        act.wait_ge(s["ssd_y"], i - 1)
                    af(ce, bank[i % 2][:], ACT.Exp)
                af(m, m, ACT.Exp).then_inc(s["ssd_exp"], 1)
            for k in range(2):
                act.wait_ge(s["ssd_yready"], k + 1)
                act.wait_ge(s["z_ready"], 2)
                squares("ssd", k, cmf[:, (8 + 4 * k) * T:(12 + 4 * k) * T])

            if stop >= 1:
                square_sum(1, X_BEFORE["moe"])
                norm_copies(1, VCOL["norm_ffn"])
                for t in range(NT):
                    act.wait_ge(s["rt_arg"], t + 1)
                    link(af(r_eg[:, t, :], r_lg[:, t, 0:NG], ACT.Exp, bias=r_n[:, t, 0:1], accum_out=r_gs[:, t, :]))
                    af(r_ex[:, t, :], r_es[:, t, :], ACT.Exp, bias=r_n[:, t, 1:2]).then_inc(s["rt_exp"], 1)

                def act_quad(it, used, base):
                    act.wait_ge(used, base + STEPS_UP)
                    af(m_tanh, bank[0][:], ACT.Tanh, scale=0.5).then_inc(s["moe_tanh"], 1)
                    act.wait_ge(s["moe_gt"], it + 1)
                    af(m_gt, bank[7][:, 0:T], ACT.Copy).then_inc(s["moe_gtc"], 1)
                    act.wait_ge(s["moe_ht"], it + 1)
                    af(m_ht, bank[2][:], ACT.Copy, scale=0.5).then_inc(s["moe_htc"], 1)
                    act.wait_ge(used, base + MOE_STEPS)
                    af(m_y[:, 0, :], bank[3][:], ACT.Copy).then_inc(s["moe_ya"], 1)

                for name in ("moe_gtc", "moe_htc"):
                    act.sem_inc(s[name], 1)
                with act.Fori(0, NQ) as q:
                    act_quad(q, s["ring_used"], q * MOE_STEPS)
                act.wait_ge(s["rt_passes"], 1)
                passes = act.value_load(count_i[0:1, 0:1], min_val=1, max_val=T // CAP)
                with act.If(passes > 1):
                    with act.Fori(1, passes) as p:
                        with act.Fori(0, NQ) as q:
                            act_quad(p * NQ + q, ov_used, (p - 1) * (NQ * MOE_STEPS) + q * MOE_STEPS)
                act.wait_ge(s["moe_acc"], 1 + NQ)
                act.dma_start(cmf[:, 40 * T:44 * T], final_norm.rearrange("(a d) -> a d", a=1).to_broadcast([P, D]))\
                   .then_inc(s["fnorm_loaded"], 16)
                act.wait_ge(s["moe_done"], 1)
                for t in range(NT):
                    af(hn[:, t, :], x_res[:, t, :], ACT.Square, accum_out=ss[:, t:t + 1]).then_inc(s["ss_ready"], 1)

            def fox(occ, li, name):
                u = NORMS.index(name)
                square_sum(SQS.index(name), X_BEFORE[name])
                norm_copies(u, VCOL["norm_w"] + 8 * (0 if occ == 0 else 3))
                softplus_row(SOFT_USE[name], rows[:, 1, :], rows[:, 2, :], 8)
                for b in range(8):
                    copy_bank(name, b, cmf[:, 2 * b * T:(2 * b + 2) * T])
                    if b % 2:
                        own_copies(name, b + 1)
                        squares(name, b // 2, cmf[:, (2 * b - 2) * T:(2 * b + 2) * T])
                for b in range(4):
                    copy_bank(name, 8 + b, vtm[:, b % 2, (b // 2) * BLK:(b // 2 + 1) * BLK])
                for b in range(4):
                    copy_bank(name, 12 + b, cmf[:, (16 + 2 * b) * T:(18 + 2 * b) * T], 0.5)
                own_copies(name, 16)
                silu_z(li, 16, ROWN[name][1] // 4 + 4)
                for h in range(FOX_H):
                    k = occ * FOX_H + h
                    act.wait_ge(s["fox_l"], k + 1)
                    for t, (a, b) in enumerate(((0, P), (P, 3 * P))):
                        i = af(f_p[h % 2][:, a:b], f_l[h % 2][:, a:b], ACT.Exp, bias=f_n[:, h % 2, t:t + 1],
                               accum_out=f_s[:, h % 2, t:t + 1])
                    i.then_inc(s["fox_e"], 1)
                    act.wait_ge(s["fox_t"], k + 1)
                    af(f_pt[h % 2], bank[2 + h % 2][:, 0:3 * P], ACT.Copy).then_inc(s["fox_tc"], 1)

            def gla():
                square_sum(SQS.index("gla"), X_BEFORE["gla"])
                norm_copies(NORMS.index("gla"), VCOL["norm_w"] + 8)
                for b in range(4):
                    copy_bank("gla", b, cmf[:, 2 * b * T:(2 * b + 2) * T])
                for b in range(4):
                    copy_bank("gla", 4 + b, vtm[:, b % 2, (b // 2) * BLK:(b // 2 + 1) * BLK])
                for b in range(4):
                    copy_bank("gla", 8 + b, cmf[:, (8 + 2 * b) * T:(10 + 2 * b) * T], 0.5)
                own_copies("gla", 12)
                silu_z(2, 8, ROWN["fox0"][1] // 4 + 4)
                act.wait_ge(s["gla_arg"], 1)
                link(af(tf(20, 4), tf(20, 4), ACT.Exp, scale=-1.0))
                af(tf(20, 4), tf(20, 4), ACT.Ln, bias=1.0).then_inc(s["gla_ln"], 1)
                act.wait_ge(s["gla_dec"], 1)
                af(tf(20, 4), tf(16, 4), ACT.Exp, scale=1.0 / 16)
                af(tf(24, 4), tf(16, 4), ACT.Exp, scale=-1.0 / 16)
                af(tf(28, 4), tf(28, 4), ACT.Exp, scale=1.0 / 16).then_inc(s["gla_exp"], 1)
                act.wait_ge(s["gla_kt"], 1)
                for k in (0, 1):
                    i = af(tf(40 + 2 * k, 2), bank[2 + k][:], ACT.Copy)
                i.then_inc(s["gla_ktc"], 1)
                act.wait_ge(s["z_ready"], 6)
                for k in range(2):
                    act.wait_ge(s["gla_oc"], 2 * k + 2)
                    squares("gla", k, tf(32 + 4 * k, 4))

            def gdn():
                square_sum(SQS.index("gdn"), X_BEFORE["gdn"])
                norm_copies(NORMS.index("gdn"), VCOL["norm_w"] + 16)
                softplus_row(SOFT_USE["gdn"], rows[:, 1, :], rows[:, 2, :], 8)
                act.wait_ge(s["gdn_row_free"], 1)
                af(rows[0:8, 0], bank[5][0:8, T:2 * T], ACT.Exp, scale=-1.0).then_inc(s["gdn_beta_exp"], 1)
                for b in range(12):
                    copy_bank("gdn", b, tf(2 * b, 2), 0.5 if b >= 8 else 1.0)
                    if b in (4, 6, 8, 10):
                        k = (b - 4) // 2
                        act.wait_ge(s["lin_ready"], 3 + k + 1)
                        af(vtm[:, 1, :], vtm[:, 0, :], ACT.Tanh).then_inc(s["tanh_ready"], 1)
                        if 1 <= k <= 2:
                            act.wait_ge(s["gdn_conv_done"], k)
                            squares("gdn_qk", k - 1, tf(4 * (k - 1), 4))
                own_copies("gdn", 12)
                silu_z(3, 16, ROWN["gdn_qk"][1] // 4 + 2)
                act.wait_ge(s["gdn_col_arg"], 1)
                af(tok[:, 4:6, 0:8], tok[:, 4:6, 0:8], ACT.Exp).then_inc(s["gdn_col_exp"], 1)
                for i in range(4):
                    act.wait_ge(s["gdn_arg"], i + 1)
                    if i >= 2:
                        af(g_qd[i - 2], bank[0][:], ACT.Exp)
                    af(g_dt, g_dt, ACT.Exp)
                    af(g_d, g_d, ACT.Exp, scale=-1.0).then_inc(s["gdn_exp"], 1)
                    act.wait_ge(s["gdn_turned"], i + 1)
                    af(g_Q, bank[5][:], ACT.Copy).then_inc(s["gdn_q_ready"], 1)
                    for j in range(6):
                        act.wait_ge(s["gdn_power"], 6 * i + j + 1)
                        if j == 0:
                            act.wait_ge(s["gdn_r_ready"], 7 * i + 1)
                        af(g_Q, bank[6][:], ACT.Copy).then_inc(s["gdn_q_ready"], 1)
                    act.wait_ge(s["gdn_uw"], i + 1)
                    af(g_u[i], bank[2][:], ACT.Copy).then_inc(s["gdn_u_ready"], 1)
                act.wait_ge(s["z_ready"], 8)
                for k in range(2):
                    act.wait_ge(s["gdn_oc"], 2 * k + 2)
                    squares("gdn_o", k, tf(4 * k, 4))

            if stop >= 2:
                fox(0, 1, "fox0")
            if stop >= 3:
                gla()
            if stop >= 4:
                gdn()
            if stop >= 5:
                fox(1, 4, "fox1")

        @block.vector
        def _(dve):
            v = nc.vector
            n_link = [0]

            def link(ins):
                n_link[0] += 1
                ins.then_inc(s["dve_chain"], 1)
                dve.wait_ge(s["dve_chain"], n_link[0])

            def inverse_root(dst, x, t, done=None):
                link(v.tensor_scalar(dst.bitcast(I32), x.bitcast(I32), -0.5, RSQRT_SEED, ALU.mult, ALU.add))
                for k in range(3):
                    link(v.tensor_tensor(t, dst, dst, ALU.mult))
                    link(v.scalar_tensor_tensor(out=t, in0=t, scalar=-0.5, in1=x, op0=ALU.mult, op1=ALU.mult))
                    i = v.scalar_tensor_tensor(out=dst, in0=t, scalar=1.5, in1=dst, op0=ALU.add, op1=ALU.mult)
                    if k == 2 and done is not None:
                        i.then_inc(done[0], 1)
                        dve.wait_ge(done[0], done[1])
                    else:
                        link(i)

            def token_scale(which):
                dve.wait_ge(s["ss_ready"], NT * (which + 1))
                link(v.tensor_scalar(ss[:, 2:4], ss[:, 0:2], 1.0 / D, EPS, ALU.mult, ALU.add))
                inverse_root(ss[:, 4:6], ss[:, 2:4], ss[:, 6:8])

            def norm(name, col):
                u = NORMS.index(name)
                token_scale(SQS.index(name))
                for t in range(NT):
                    v.tensor_scalar(hn[:, t, :], x_res[:, t, :], ss[:, 4 + t:5 + t], None,
                                    ALU.mult).then_inc(s["xn_ready"], 1)
                for b in (1, 3):
                    dve.wait_ge(s["turned"], 4 * u + b + 1)
                    for j in (0, 1):
                        i = v.tensor_scalar(hnT[:, 2 * b + j, :], b2(7)[:, j, :],
                                            vec[:, col + 2 * b + j:col + 2 * b + j + 1], None, ALU.mult)
                    i.then_inc(s["hnT_dve"], 1)

            def rownorm(name, R, scale, use):
                r, before, n = ROWN[name]
                dve.wait_ge(s["sq_summed"], (before + n) // 4)
                link(v.tensor_scalar(rrow[0:R, 0], bank[SUM_BANK[name]][0:R, 0:T], scale, EPS, ALU.mult, ALU.add))
                inverse_root(rrow[0:R, 1], rrow[0:R, 0], rrow[0:R, 2], (s["rownorm_ready"], r + 1))
                for b in range(n // 2):
                    g = before // 2 + b
                    dve.wait_ge(s["spread_done"], g + 1)
                    use(2 * b, b2(6 + g % 2)[:, 0, :])
                    use(2 * b + 1, b2(6 + g % 2)[:, 1, :]).then_inc(s["spread_used"], 1)
                dve.wait_ge(s["spread_used"], (before + n) // 2)

            def add_projection(li):
                dve.sem_inc(s["outT_ready"], 1)
                for k in range(4):
                    n, t = k // 2, k % 2
                    dve.wait_ge(s["outp_done"], 4 * li + k + 1)
                    dst = x_res[:, t, n * BLK:(n + 1) * BLK]
                    v.tensor_tensor(dst, bank[t + 2 * n][:], dst, ALU.add).then_inc(s["x_ready"], 1)

            def silu_z(li, z0):
                for b in (0, 1):
                    dve.wait_ge(s["z_tanh"], 2 * li + b + 1)
                    z = tf(z0 + 4 * b, 4)
                    v.scalar_tensor_tensor(out=z, in0=sq[:, b].rearrange("p a b -> p (a b)"), scalar=1.0, in1=z,
                                           op0=ALU.add, op1=ALU.mult).then_inc(s["z_ready"], 1)
                dve.wait_ge(s["z_ready"], 2 * li + 2)

            def conv(src, dst, weights, stride, taps, bias=None):
                n = len(src)
                for d in range(taps):
                    tap = taps - 1 - d
                    for i in range(n):
                        w = vec[:, weights + stride * tap + i:weights + stride * tap + i + 1]
                        if d == 0 and bias is None:
                            x = v.tensor_scalar(dst[i], src[i], w, None, ALU.mult)
                        elif d == 0:
                            x = v.tensor_scalar(dst[i], src[i], w, vec[:, bias + i:bias + i + 1], ALU.mult, ALU.add)
                        else:
                            x = v.scalar_tensor_tensor(out=dst[i][:, d:T], in0=src[i][:, 0:T - d], scalar=w,
                                                       in1=dst[i][:, d:T], op0=ALU.mult, op1=ALU.add)
                    if d < taps - 1:
                        link(x)
                return x

            def conv_silu(k, t0, weights, stride, bias, done):
                lin = [vtm[:, 0, i * T:(i + 1) * T] for i in range(4)]
                conv([cm[:, t0 + i, :] for i in range(4)], lin, weights, stride, 4, bias).then_inc(s["lin_ready"], 1)
                dve.wait_ge(s["lin_ready"], k + 1)
                dve.wait_ge(s["tanh_ready"], k + 1)
                v.scalar_tensor_tensor(out=tf(t0, 4), in0=vtm[:, 1, :], scalar=1.0, in1=vtm[:, 0, :],
                                       op0=ALU.add, op1=ALU.mult).then_inc(done[0], 1)
                dve.wait_ge(*done)

            dve.wait_ge(s["vec_turned"], 2)
            v.tensor_copy(vec[:, 0:NA], bank[5][:, 0:NA])
            link(v.tensor_copy(vec[:, P:P + NB], bank[5][:, P:P + NB]))
            v.tensor_scalar(vec[:, 0:60], vec[:, 0:60], 0.5, None, ALU.mult)
            v.tensor_scalar(vec[:, P + 32:P + 96], vec[:, P + 32:P + 96], 0.5, None, ALU.mult).then_inc(s["vec_ready"], 1)
            dve.wait_ge(s["vec_ready"], 1)
            norm("ssd", VCOL["norm_mix"])
            dve.wait_ge(s["cols_ready"], 1)
            v.tensor_scalar(ncols[0:16, 0:1], ncols[0:16, 0:1], -1.0, None, ALU.mult)
            link(v.tensor_scalar(ncols[0:8, 1:2], ncols[0:8, 1:2], -1.0, None, ALU.mult))

            def softplus_args(k, R, src, bias, sign):
                link(v.tensor_scalar(rows[0:R, 0], src, bias, sign, ALU.add, ALU.mult))
                v.scalar_tensor_tensor(out=rows[0:R, 1], in0=rows[0:R, 0], scalar=-1.0, in1=rows[0:R, 0],
                                       op0=ALU.mult, op1=ALU.max).then_inc(s["row_arg"], 1)
                dve.wait_ge(s["row_ln"], k)

            def softplus_tail(R, dst):
                link(v.scalar_tensor_tensor(out=dst, in0=rows[0:R, 0], scalar=0.0, in1=rows[0:R, 2],
                                            op0=ALU.max, op1=ALU.add))

            dve.wait_ge(s["small_done"], 1)
            softplus_args(1, 16, bank[5][0:16, 0:T], cols[0:16, 1:2], 1.0)
            softplus_tail(16, rows[0:16, 3])
            link(v.tensor_scalar(rows[0:16, 1], rows[0:16, 3], ncols[0:16, 0:1], None, ALU.mult))
            for c in range(NT):
                x = v.tensor_tensor_scan(rows[0:16, 2, c * P:(c + 1) * P], ones[0:16, :], rows[0:16, 1, c * P:(c + 1) * P],
                                         0.0, ALU.mult, ALU.add)
            x.then_inc(s["row_ready"], 1)
            dve.wait_ge(s["row_turned"], 1)
            v.tensor_copy(tok[:, 0:4, :], bank[5][:, T:T + 64].rearrange("p (a b) -> p a b", a=4)).then_inc(s["col_ready"], 1)
            dve.wait_ge(s["col_ready"], 1)

            for k in range(3):
                dve.wait_ge(s["proj_copied"], 2 * k + 2)
                conv_silu(k, 8 + 4 * k, VCOL["ssd_conv_w"] + 4 * k, 12, VCOL["ssd_conv_b"] + 4 * k,
                          (s["ssd_conv_done"], k + 1))
            for k in range(2):
                dve.wait_ge(s["cv_ready"], 2 * k + 2)
                dve.wait_ge(s["proj_copied"], 14 + 2 * k + 2)
                link(conv([cm[:, 28 + 4 * k + i, :] for i in range(4)], [cm[:, 36 + 4 * k + i, :] for i in range(4)],
                          VCOL["sc_conv_w"] + 4 * k, 8, 3))
                v.tensor_tensor(tf(36 + 4 * k, 4), tf(36 + 4 * k, 4), tf(20 + 4 * k, 4),
                                ALU.mult).then_inc(s["ssd_conv_done"], 1)
                dve.wait_ge(s["ssd_conv_done"], 3 + k + 1)

            def sc_out(i, spread):
                return v.scalar_tensor_tensor(out=cm[:, 36 + i, :], in0=spread, scalar=vec[:, VCOL["sc_norm"] + i:VCOL["sc_norm"] + i + 1],
                                              in1=cm[:, 36 + i, :], op0=ALU.mult, op1=ALU.mult)

            rownorm("sc", 16, 1.0 / 64, sc_out)
            silu_z(0, 0)
            xdt = vtm
            for k in range(4):
                c, hf = k // 2, k % 2
                dve.wait_ge(s["ssd_xt_done"], k + 1)
                dst = xdt[:, c, hf * BLK:(hf + 1) * BLK].rearrange("p (h d) -> p h d", d=64)
                dtc = tok[:, 2 + c, 8 * hf:8 * hf + 8].unsqueeze(2).to_broadcast([P, 8, 64])
                v.tensor_tensor(dst, bank[k % 2][:].rearrange("p (h d) -> p h d", d=64), dtc,
                                ALU.mult).then_inc(s["ssd_xt_used"], 1)
            dve.wait_ge(s["ssd_xt_used"], 4)
            dve.wait_ge(s["ssd_g_done"], 1)
            v.tensor_tensor(tok[:, 4, :], bank[3][:, 2 * P:2 * P + 16], tok[:, 0, :], ALU.subtract).then_inc(s["ssd_dte_arg"], 1)
            v.tensor_copy(tiles(30, 1, P)[:, :, :], b4(3)[:, 0:2, :])
            for j in range(4):
                x = v.tensor_tensor(tf(28, 2)[:, j * P:(j + 1) * P], b4(2)[:, j, :], upper[:], ALU.mult)
            link(x)
            dve.wait_ge(s["ssd_dte"], 1)
            v.tensor_tensor(hn[:, 0, :].rearrange("p (h d) -> p h d", d=64), xdt[:, 0, :].rearrange("p (h d) -> p h d", d=64),
                            tok[:, 4, :].unsqueeze(2).to_broadcast([P, 16, 64]), ALU.mult).then_inc(s["ssd_xdte"], 1)
            dve.wait_ge(s["ssd_state"], 1)
            for g in range(2):
                x = v.tensor_copy(hn[:, 1, g * BLK:(g + 1) * BLK], bank[g + 6][:])
            x.then_inc(s["ssd_state_used"], 1)
            for i in range(8):
                c, hq = i // 4, i % 4
                g = hq // 2
                m = hnTf[:, (i % 2) * 512:(i % 2) * 512 + 512]
                dve.wait_ge(s["ssd_bc"], i + 1)
                if i >= 2:
                    dve.wait_ge(s["ssd_y"], i - 1)
                for j in range(4):
                    h = 4 * hq + j
                    x = v.tensor_scalar(m[:, j * P:(j + 1) * P], b4(i % 2)[:, j, :], tok[:, c, h:h + 1], 0.0,
                                        ALU.subtract, ALU.min)
                x.then_inc(s["ssd_seg"], 1)
                dve.wait_ge(s["ssd_exp"], i + 1)
                m4 = m.rearrange("p (a b) -> p a b", b=P)
                gm = tf(28, 2)[:, (2 * c + g) * P:(2 * c + g + 1) * P].unsqueeze(1).to_broadcast([P, 4, P])
                if c == 1:
                    ce = hnTf[:, 1024 + (i % 2) * 512:1536 + (i % 2) * 512].rearrange("p (a b) -> p a b", b=P)
                    v.tensor_tensor(ce, ce, cm[:, 18 + g, P:T].unsqueeze(1).to_broadcast([P, 4, P]), ALU.mult)
                v.tensor_tensor(m4, m4, gm, ALU.mult).then_inc(s["ssd_m"], 1)
            for k in range(2):
                dve.wait_ge(s["ssd_y"], 4 + 2 * k + 2)
                for i in range(4 * k, 4 * k + 4):
                    x = v.scalar_tensor_tensor(out=cm[:, 8 + i, :], in0=cm[:, 8 + i, :], scalar=dsk[:, i:i + 1],
                                               in1=b2(2 + i // 2)[:, i % 2, :], op0=ALU.mult, op1=ALU.add)
                link(x)
                v.tensor_tensor(tf(8 + 4 * k, 4), tf(8 + 4 * k, 4), tf(4 * k, 4), ALU.mult).then_inc(s["ssd_yready"], 1)
                dve.wait_ge(s["ssd_yready"], k + 1)

            def ssd_out(i, spread):
                return v.scalar_tensor_tensor(out=cm[:, 8 + i, :], in0=spread, scalar=vec[:, VCOL["ssd_norm"] + i:VCOL["ssd_norm"] + i + 1],
                                              in1=cm[:, 8 + i, :], op0=ALU.mult, op1=ALU.mult)

            rownorm("ssd", 2, 1.0 / BLK, ssd_out)
            add_projection(0)

            if stop >= 1:
                norm("moe", VCOL["norm_ffn"])
                dve.wait_ge(s["rt_done"], 1)
                link(v.tensor_copy(r_lg, bank[5][:, 0:NT * (NG + NE)].rearrange("p (a b) -> p a b", a=NT)))

                def rank(x, n, limit, dst):
                    c1 = r_c1[:, 0:n * n // 2, :].rearrange("p a b -> p (a b)").rearrange("p (i j) -> p i j", i=n)
                    c2 = r_c2[:, 0:n * n // 2, :].rearrange("p a b -> p (a b)").rearrange("p (i j) -> p i j", i=n)
                    other = x.unsqueeze(1).to_broadcast([P, n, n])
                    own = x.unsqueeze(2).to_broadcast([P, n, n])
                    v.tensor_tensor(c1, other, own, ALU.is_gt)
                    link(v.tensor_tensor(c2, other, own, ALU.is_equal))
                    link(v.tensor_tensor(c2, c2, earlier[:, 0:n, 0:n], ALU.mult))
                    link(v.tensor_tensor(c1, c1, c2, ALU.add))
                    link(v.tensor_reduce(dst, c1, AX.X, ALU.add))
                    link(v.tensor_scalar(dst, dst, limit - 0.5, None, ALU.is_lt))

                for t in range(NT):
                    gl, el = r_lg[:, t, 0:NG], r_lg[:, t, NG:NG + NE].rearrange("p (g e) -> p g e", g=NG)
                    rank(gl, NG, 1, r_gsel[:, t, :])
                    v.tensor_reduce(r_n[:, t, 0:1], gl, AX.X, ALU.max, negate=True)
                    link(v.tensor_tensor(r_prod, el, r_gsel[:, t, :].unsqueeze(2).to_broadcast([P, NG, EPG]), ALU.mult))
                    link(v.tensor_reduce(r_es[:, t, :], r_prod.rearrange("p g e -> p e g"), AX.X, ALU.add))
                    v.tensor_reduce(r_n[:, t, 1:2], r_es[:, t, :], AX.X, ALU.max, negate=True).then_inc(s["rt_arg"], 1)
                    rank(r_es[:, t, :], EPG, 2, r_sel[:, t, :])
                v.memset(r_gate, 0.0)
                link(v.memset(r_pm, -1.0))
                for t in range(NT):
                    dve.wait_ge(s["rt_exp"], t + 1)
                    link(v.tensor_tensor(r_ex[:, t, :], r_ex[:, t, :], r_sel[:, t, :], ALU.mult))
                    link(v.tensor_reduce(r_sum[:, t, 0:1], r_ex[:, t, :], AX.X, ALU.add))
                    link(v.tensor_tensor(r_sum[:, t, 1:2], r_sum[:, t, 0:1], r_gs[:, t, :], ALU.mult))
                    link(v.reciprocal(r_sum[:, t, 2:3], r_sum[:, t, 1:2]))
                    link(v.tensor_scalar(r_ex[:, t, :], r_ex[:, t, :], r_sum[:, t, 2:3], None, ALU.mult))
                    gs = r_gsel[:, t, :].unsqueeze(2).to_broadcast([P, NG, EPG])
                    v.tensor_tensor(r_gate[:, t, 0:NE].rearrange("p (g e) -> p g e", g=NG),
                                    r_ex[:, t, :].unsqueeze(1).to_broadcast([P, NG, EPG]), gs, ALU.mult)
                    v.tensor_tensor(r_mask[:, t, :].rearrange("p (g e) -> p g e", g=NG),
                                    r_sel[:, t, :].unsqueeze(1).to_broadcast([P, NG, EPG]), gs,
                                    ALU.mult).then_inc(s["rt_mask"], 1)
                dve.wait_ge(s["rt_mask"], 2)
                dve.wait_ge(s["rt_rank"], 1)
                for t in range(NT):
                    pm = r_pm[:, t, 0:NE]
                    link(v.scalar_tensor_tensor(out=pm, in0=bank[5][:, P + t * NE:P + (t + 1) * NE], scalar=1.0,
                                                in1=r_mask[:, t, :], op0=ALU.add, op1=ALU.mult))
                    link(v.tensor_scalar(pm, pm, -1.0, None, ALU.add))
                link(v.tensor_reduce(r_pass[0:1, 0, 0:1], bank[5][0:1, T:T + NE], AX.X, ALU.max))
                link(v.tensor_scalar(r_pass[0:1, 1, 0:8], iota[0:1, 0:8], float(CAP), r_pass[0:1, 0, 0:1], ALU.mult, ALU.is_lt))
                link(v.tensor_reduce(r_pass[0:1, 0, 1:2], r_pass[0:1, 1, 0:8], AX.X, ALU.add))
                v.tensor_copy(count_i[0:1, 0:1], r_pass[0:1, 0, 1:2]).then_inc(s["rt_passes"], 1)

                iota4 = iota[:].unsqueeze(1).to_broadcast([P, QUAD, CAP])

                def select_tokens(q):
                    for t in range(NT):
                        place = r_pm[:, t, bass.ds(q * QUAD, QUAD)].unsqueeze(2).to_broadcast([P, QUAD, CAP])
                        x = v.tensor_tensor(m_S[:, t, :].rearrange("p (e c) -> p e c", e=QUAD), iota4, place, ALU.is_equal)
                    x.then_inc(s["moe_sel"], 1)

                def gathered(g):
                    dve.wait_ge(s["moe_gath"], g + 1)
                    for half in (0, 1):
                        gain = vec[:, VCOL["norm_ffn"] + 4 * half:VCOL["norm_ffn"] + 4 * half + 4]
                        x = v.tensor_tensor(m_xg[:, 4 * half:4 * half + 4, :], b4(5 + half)[:],
                                            gain.unsqueeze(2).to_broadcast([P, 4, P]), ALU.mult)
                    x.then_inc(s["moe_xg"], 1)

                def dve_quad(q, it, g):
                    dve.wait_ge(s["moe_sel"], g + 1)
                    for t in range(NT):
                        gate = r_gate[:, t, bass.ds(q * QUAD, QUAD)].unsqueeze(2).to_broadcast([P, QUAD, CAP])
                        x = v.tensor_tensor(m_SG[:, t, :].rearrange("p (e c) -> p e c", e=QUAD),
                                            m_S[:, t, :].rearrange("p (e c) -> p e c", e=QUAD), gate, ALU.mult)
                    x.then_inc(s["moe_sg"], 1)
                    dve.wait_ge(s["moe_sg"], it + 1)
                    select_tokens(q + 1)
                    dve.wait_ge(s["moe_tanh"], it + 1)
                    v.scalar_tensor_tensor(out=m_silu, in0=m_tanh, scalar=1.0, in1=bank[0][:], op0=ALU.add,
                                           op1=ALU.mult).then_inc(s["moe_chain"], 1)
                    dve.wait_ge(s["moe_chain"], it + 1)
                    v.tensor_tensor(m_h, m_silu, bank[1][:], ALU.mult).then_inc(s["moe_h"], 1)
                    gathered(g + 1)
                    return

                def dve_quad_end(it, used, base):
                    dve.wait_ge(used, base + MOE_STEPS)
                    v.tensor_copy(m_y[:, 1, :], bank[4][:]).then_inc(s["moe_yd"], 1)
                    dve.wait_ge(s["moe_scat"], it + 1)
                    for k in range(4):
                        t, n = k // 2, k % 2
                        dst = x_res[:, t, n * BLK:(n + 1) * BLK]
                        x = v.tensor_tensor(dst, bank[[5, 6, 3, 4][k]][:], dst, ALU.add)
                    x.then_inc(s["moe_acc"], 1)

                dve.sem_inc(s["moe_h"], 1)
                dve.sem_inc(s["moe_acc"], 1)
                dve.wait_ge(s["rt_passes"], 1)
                select_tokens(0)
                gathered(0)
                with dve.Fori(0, NQ) as q:
                    dve_quad(q, q, q)
                    dve_quad_end(q, s["ring_used"], q * MOE_STEPS)
                passes = dve.value_load(count_i[0:1, 0:1], min_val=1, max_val=T // CAP)
                with dve.If(passes > 1):
                    with dve.Fori(1, passes) as p:
                        for t in range(NT):
                            x = v.tensor_scalar(r_pm[:, t, :], r_pm[:, t, :], -float(CAP), None, ALU.add)
                        x.then_inc(s["pass_chain"], 1)
                        dve.wait_ge(s["pass_chain"], p)
                        select_tokens(0)
                        gathered(p * (NQ + 1))
                        with dve.Fori(0, NQ) as q:
                            dve_quad(q, p * NQ + q, p * (NQ + 1) + q)
                            dve_quad_end(p * NQ + q, ov_used, (p - 1) * (NQ * MOE_STEPS) + q * MOE_STEPS)
                v.drain().then_inc(s["moe_done"], 1)
                token_scale(2)
                dve.wait_ge(s["fnorm_loaded"], 16)
                for t in range(NT):
                    v.scalar_tensor_tensor(out=x_res[:, t, :], in0=x_res[:, t, :], scalar=ss[:, 4 + t:5 + t],
                                           in1=tf(40, 4), op0=ALU.mult, op1=ALU.mult).then_inc(s["x_ready"], 1)
                dve.wait_ge(s["x_ready"], X_BEFORE["fox0"])

            def fox(occ, li, name):
                norm(name, VCOL["norm_w"] + 8 * (0 if occ == 0 else 3))
                dve.wait_ge(s["small_done"], li + 1)
                softplus_args(SOFT_USE[name], FOX_H, bank[5][0:FOX_H, 0:T], cols[0:FOX_H, 2 + occ:3 + occ], -1.0)
                softplus_tail(FOX_H, rows[0:FOX_H, 1])
                link(v.tensor_tensor_scan(rows[0:FOX_H, 3], ones[0:FOX_H, 0:1].to_broadcast([FOX_H, T]), rows[0:FOX_H, 1], 0.0, ALU.mult, ALU.subtract))
                v.tensor_scalar(rows[0:FOX_H, 2], rows[0:FOX_H, 3], -1.0, None, ALU.mult).then_inc(s["row_ready"], 1)
                dve.wait_ge(s["row_turned"], ROW_USE[name])
                link(v.tensor_copy(tok[:, 5:7, 0:FOX_H], bank[5][:, T:T + 16].rearrange("p (a b) -> p a b", a=2)))

                def qk_out(i, spread):
                    gain = VCOL["fox_q_gain"] + occ if i < 8 else VCOL["fox_k_gain"] + occ
                    if i < 8:
                        return v.scalar_tensor_tensor(out=cm[:, i, :], in0=spread, scalar=qgain[:, 0:1], in1=cm[:, i, :],
                                                      op0=ALU.mult, op1=ALU.mult)
                    return v.scalar_tensor_tensor(out=cm[:, i, :], in0=spread, scalar=vec[:, gain:gain + 1], in1=cm[:, i, :],
                                                  op0=ALU.mult, op1=ALU.mult)

                qcol = VCOL["fox_q_gain"] + occ
                link(v.tensor_scalar(qgain[:, 0:1], vec[:, qcol:qcol + 1], float(P) ** -0.5, None, ALU.mult))
                rownorm(name, 16, 1.0 / P, qk_out)
                dve.sem_inc(s["qk_ready"], 1)
                silu_z(li, 16)
                for h in range(FOX_H + 1):
                    k = occ * FOX_H + h
                    if h < FOX_H:
                        dve.wait_ge(s["fox_s"], k + 1)
                        v.scalar_tensor_tensor(out=f_l[h % 2][:, 0:P], in0=bank[h % 2][:, 0:P], scalar=tok[:, 5, h:h + 1],
                                               in1=negmask[:, 1, :], op0=ALU.add, op1=ALU.add)
                        link(v.scalar_tensor_tensor(out=f_l[h % 2][:, P:3 * P], in0=bank[h % 2][:, P:3 * P],
                                                    scalar=tok[:, 6, h:h + 1], in1=negmask[:].rearrange("p a b -> p (a b)"),
                                                    op0=ALU.add, op1=ALU.add))
                        v.tensor_reduce(f_n[:, h % 2, 0:1], f_l[h % 2][:, 0:P], AX.X, ALU.max, negate=True)
                        v.tensor_reduce(f_n[:, h % 2, 1:2], f_l[h % 2][:, P:3 * P], AX.X, ALU.max,
                                        negate=True).then_inc(s["fox_l"], 1)
                        dve.wait_ge(s["fox_e"], k + 1)
                        link(v.reciprocal(f_r[:, h % 2, :], f_s[:, h % 2, :]))
                        v.tensor_scalar(f_p[h % 2][:, 0:P], f_p[h % 2][:, 0:P], f_r[:, h % 2, 0:1], None, ALU.mult)
                        v.tensor_scalar(f_p[h % 2][:, P:3 * P], f_p[h % 2][:, P:3 * P], f_r[:, h % 2, 1:2], None,
                                        ALU.mult).then_inc(s["fox_p"], 1)
                    if h >= 1:
                        dve.wait_ge(s["fox_o"], k)
                        z = cm[:, 16 + h - 1, :]
                        v.tensor_tensor(z, bank[6 + (h - 1) % 2][:, 0:T], z, ALU.mult).then_inc(s["fox_oc"], 1)
                dve.wait_ge(s["fox_oc"], (occ + 1) * FOX_H)
                add_projection(li)

            def ones_free(R, n):
                return ones[0:R, 0:1].to_broadcast([R, n])

            def gla():
                norm("gla", VCOL["norm_w"] + 8)
                dve.wait_ge(s["small_done"], 3)
                v.tensor_copy(rows[0:16, 0], bank[5][0:16, 0:T]).then_inc(s["gla_low"], 1)
                dve.wait_ge(s["gla_gate"], 1)
                for h in range(GLA_H):
                    x = v.tensor_scalar(cm[:, 16 + h, :], b2(4 + h // 2)[:, h % 2, :],
                                        vec[:, VCOL["gla_b_gate"] + h:VCOL["gla_b_gate"] + h + 1], -1.0, ALU.add, ALU.mult)
                link(x)
                v.scalar_tensor_tensor(out=tf(20, 4), in0=tf(16, 4), scalar=-1.0, in1=tf(16, 4), op0=ALU.mult,
                                       op1=ALU.max).then_inc(s["gla_arg"], 1)
                dve.wait_ge(s["gla_ln"], 1)
                link(v.scalar_tensor_tensor(out=tf(20, 4), in0=tf(16, 4), scalar=0.0, in1=tf(20, 4), op0=ALU.max,
                                            op1=ALU.add))
                for k in range(GLA_H * T // GLA_CH):
                    x = v.tensor_tensor_scan(tf(16, 4)[:, k * 64:(k + 1) * 64], ones[:, 0:64], tf(20, 4)[:, k * 64:(k + 1) * 64],
                                             0.0, ALU.mult, ALU.subtract)
                link(x)
                cum = tiles(16, 4, 64)
                v.tensor_tensor(tiles(28, 4, 64), cum[:, :, 63:64].to_broadcast([P, 16, 64]), cum,
                                ALU.subtract).then_inc(s["gla_dec"], 1)
                silu_z(2, 8)
                dve.wait_ge(s["gla_exp"], 1)
                dve.wait_ge(s["proj_copied"], PROJ_BASE["gla"] + 4)
                v.scalar_tensor_tensor(out=tf(0, 4), in0=tf(0, 4), scalar=float(GLA_DK) ** -0.5, in1=tf(20, 4),
                                       op0=ALU.mult, op1=ALU.mult)
                link(v.tensor_tensor(tf(28, 4), tf(4, 4), tf(28, 4), ALU.mult))
                v.tensor_tensor(tf(4, 4), tf(4, 4), tf(24, 4), ALU.mult).then_inc(s["gla_qk"], 1)
                dve.wait_ge(s["gla_qk"], 1)
                dve.wait_ge(s["gla_at"], 1)
                for k in (0, 1):
                    x = v.tensor_tensor(tiles(24 + 2 * k, 2, P), b4(k), upper64[:].unsqueeze(1).to_broadcast([P, 4, P]),
                                        ALU.mult)
                x.then_inc(s["gla_atc"], 1)
                state = tiles(16, 4, GLA_DV)
                for c in range(3):
                    dve.wait_ge(s["gla_st"], c + 1)
                    if c:
                        dve.wait_ge(s["gla_stc"], c)
                    for h in range(GLA_H):
                        new = b2(2 * (c % 2) + h // 2)[:, h % 2, :]
                        if c == 0:
                            x = v.tensor_copy(state[:, h, :], new)
                        else:
                            a = h * T + c * 64 + 63
                            x = v.scalar_tensor_tensor(out=state[:, h, :], in0=state[:, h, :], scalar=tf(20, 4)[:, a:a + 1],
                                                       in1=new, op0=ALU.mult, op1=ALU.add)
                    x.then_inc(s["gla_stc"], 1)
                dve.wait_ge(s["gla_o"], 1)
                for h in range(GLA_H):
                    v.tensor_copy(tf(32 + 2 * h, 2), bank[4 + h][:]).then_inc(s["gla_oc"], 1)
                dve.wait_ge(s["gla_oc"], 4)
                link(v.tensor_tensor(tf(8, 8), tf(8, 8), tf(32, 8), ALU.mult))

                def out(i, spread):
                    gain = VCOL["gla_o_gain"] + i % 2
                    return v.scalar_tensor_tensor(out=cm[:, 8 + i, :], in0=spread, scalar=vec[:, gain:gain + 1],
                                                  in1=cm[:, 8 + i, :], op0=ALU.mult, op1=ALU.mult)

                rownorm("gla", GLA_H, 1.0 / GLA_DV, out)
                add_projection(2)

            def gdn():
                norm("gdn", VCOL["norm_w"] + 16)
                dve.wait_ge(s["small_done"], 4)
                softplus_args(SOFT_USE["gdn"], 8, bank[5][0:8, 0:T], cols[0:8, 5:6], 1.0)
                softplus_tail(8, rows[0:8, 3])
                v.tensor_scalar(rows[0:8, 1], rows[0:8, 3], ncols[0:8, 1:2], None, ALU.mult).then_inc(s["gdn_row_free"], 1)
                dve.wait_ge(s["gdn_row_free"], 1)
                for c in range(NT):
                    x = v.tensor_tensor_scan(rows[0:8, 2, c * P:(c + 1) * P], ones[0:8, :], rows[0:8, 1, c * P:(c + 1) * P],
                                             0.0, ALU.mult, ALU.add)
                dve.wait_ge(s["gdn_beta_exp"], 1)
                link(v.tensor_scalar(rows[0:8, 0], rows[0:8, 0], 1.0, None, ALU.add))
                v.reciprocal(rows[0:8, 0], rows[0:8, 0]).then_inc(s["row_ready"], 1)
                dve.wait_ge(s["row_turned"], ROW_USE["gdn"])
                v.tensor_copy(tok[:, 0:4, 0:8], bank[5][:, T:T + 32].rearrange("p (a b) -> p a b", a=4)).then_inc(s["col_ready"], 1)
                dve.wait_ge(s["col_ready"], 2)
                v.tensor_scalar(tok[:, 6:8, 0:8], tok[:, 2:4, 0:8], -1.0, None, ALU.mult)
                v.tensor_copy(tok[:, 5, 0:8], tok[:, 1, 0:8])
                dve.wait_ge(s["gdn_last"], 1)
                v.tensor_tensor(tok[:, 4, 0:8], bank[5][:, T + 32:T + 40], tok[:, 0, 0:8],
                                ALU.subtract).then_inc(s["gdn_col_arg"], 1)
                for k in range(4):
                    dve.wait_ge(s["proj_copied"], PROJ_BASE["gdn"] + 2 * k + 2)
                    conv_silu(3 + k, 4 * k, VCOL["gdn_conv_w"] + 4 * k, 16, None, (s["gdn_conv_done"], k + 1))

                def qk_out(i, spread):
                    return v.scalar_tensor_tensor(out=cm[:, i, :], in0=spread, scalar=float(P) ** -0.5 if i < 4 else 1.0,
                                                  in1=cm[:, i, :], op0=ALU.mult, op1=ALU.mult)

                rownorm("gdn_qk", 8, 1.0, qk_out)
                dve.sem_inc(s["gdn_qk_ready"], 1)
                silu_z(3, 16)
                for k in range(4):
                    c, hf = k // 2, k % 2
                    dve.wait_ge(s["gdn_xt"], k + 1)
                    v.tensor_tensor(vtm[:, c, hf * BLK:(hf + 1) * BLK].rearrange("p (h d) -> p h d", h=4), b4(k % 2),
                                    tok[:, 2 + c, 4 * hf:4 * hf + 4].unsqueeze(2).to_broadcast([P, 4, P]),
                                    ALU.mult).then_inc(s["gdn_xtc"], 1)
                dve.wait_ge(s["gdn_xtc"], 4)
                dve.wait_ge(s["gdn_col_exp"], 1)
                link(v.tensor_tensor(tok[:, 5, 0:8], tok[:, 5, 0:8], tok[:, 3, 0:8], ALU.mult))
                dve.wait_ge(s["gdn_kt"], 1)
                for dst, b, col in ((g_kdec, 2, 4), (g_kbg, 3, 5)):
                    x = v.tensor_tensor(dst.rearrange("p (h r d) -> p h r d", h=4, r=2), b4(b).unsqueeze(2).to_broadcast([P, 4, 2, P]),
                                        tok[:, col, 0:8].rearrange("p (h r) -> p h r", r=2).unsqueeze(3).to_broadcast([P, 4, 2, P]),
                                        ALU.mult)
                x.then_inc(s["gdn_ktc"], 1)
                dve.wait_ge(s["gdn_ktc"], 1)
                for i in range(4):
                    c, hf = i // 2, i % 2
                    dve.wait_ge(s["gdn_bc"], i + 1)
                    for j in range(4):
                        h = 4 * hf + j
                        col = tok[:, c, h:h + 1]
                        v.tensor_scalar(g_dt[:, j * P:(j + 1) * P], b4(0)[:, j, :], col, 0.0, ALU.subtract, ALU.min)
                        x = v.tensor_scalar(g_d[:, j * P:(j + 1) * P], b4(0)[:, j, :], col, 0.0, ALU.subtract, ALU.max)
                    x.then_inc(s["gdn_arg"], 1)
                    v.tensor_tensor(g_km, b4(1)[:, 0:2, :], slower[:].unsqueeze(1).to_broadcast([P, 2, P]), ALU.mult)
                    link(v.tensor_tensor(g_qm, b4(1)[:, 2:4, :], upper[:].unsqueeze(1).to_broadcast([P, 2, P]), ALU.mult))
                    dve.wait_ge(s["gdn_exp"], i + 1)
                    for j in range(4):
                        h = 4 * hf + j
                        x = v.scalar_tensor_tensor(out=g_QT[:, j * P:(j + 1) * P], in0=g_km[:, j // 2, :],
                                                   scalar=tok[:, 6 + c, h:h + 1], in1=g_d[:, j * P:(j + 1) * P],
                                                   op0=ALU.mult, op1=ALU.mult)
                    x.then_inc(s["gdn_x"], 1)
                    v.tensor_tensor(g_qkk[i].rearrange("p (h r d) -> p h r d", h=2, r=2),
                                    g_dt.rearrange("p (h r d) -> p h r d", h=2, r=2),
                                    g_qm.unsqueeze(2).to_broadcast([P, 2, 2, P]), ALU.mult)
                    if c == 1:
                        v.tensor_tensor(g_qd[hf].rearrange("p (h r d) -> p h r d", h=2, r=2),
                                        g_qd[hf].rearrange("p (h r d) -> p h r d", h=2, r=2),
                                        cm[:, 2 * hf:2 * hf + 2, P:T].unsqueeze(2).to_broadcast([P, 2, 2, P]), ALU.mult)
                    dve.wait_ge(s["gdn_q_ready"], 7 * i + 1)
                    v.tensor_tensor(g_R.rearrange("p (h d) -> p h d", h=4), g_Q.rearrange("p (h d) -> p h d", h=4), ident[:].unsqueeze(1).to_broadcast([P, 4, P]),
                                    ALU.add).then_inc(s["gdn_r_ready"], 1)
                    for j in range(6):
                        dve.wait_ge(s["gdn_power"], 6 * i + j + 1)
                        v.tensor_copy(g_QT, bank[7][:]).then_inc(s["gdn_qt_ready"], 1)
                        dve.wait_ge(s["gdn_r"], 6 * i + j + 1)
                        dve.wait_ge(s["gdn_r_ready"], 7 * i + j + 1)
                        v.tensor_tensor(g_R, g_R, bank[4][:], ALU.add).then_inc(s["gdn_r_ready"], 1)
                    if c == 1:
                        dve.wait_ge(s["gdn_uw"], i + 1)
                        v.tensor_copy(g_w[hf], bank[3][:]).then_inc(s["gdn_w_ready"], 1)
                dve.wait_ge(s["gdn_s"], 1)
                for k in (0, 1):
                    x = v.tensor_copy(tf(40 + 2 * k, 2), bank[k][:])
                x.then_inc(s["gdn_s_ready"], 1)
                dve.wait_ge(s["gdn_ws"], 1)
                for k in (0, 1):
                    x = v.tensor_tensor(g_u[2 + k], g_u[2 + k], bank[2 + k][:], ALU.subtract)
                x.then_inc(s["gdn_new"], 1)
                dve.wait_ge(s["gdn_o"], 1)
                for k in range(4):
                    v.tensor_copy(tf(2 * k, 2), bank[4 + k][:]).then_inc(s["gdn_oc"], 1)
                dve.wait_ge(s["gdn_oc"], 4)
                link(v.tensor_tensor(tf(16, 8), tf(16, 8), tf(0, 8), ALU.mult))

                def out(i, spread):
                    gain = VCOL["gdn_o_gain"]
                    return v.scalar_tensor_tensor(out=cm[:, 16 + i, :], in0=spread, scalar=vec[:, gain:gain + 1],
                                                  in1=cm[:, 16 + i, :], op0=ALU.mult, op1=ALU.mult)

                rownorm("gdn_o", 8, 1.0 / P, out)
                add_projection(3)

            if stop >= 2:
                fox(0, 1, "fox0")
            if stop >= 3:
                gla()
            if stop >= 4:
                gdn()
            if stop >= 5:
                fox(1, 4, "fox1")

        @block.tensor
        def _(pe):
            mm, tr = nc.tensor.matmul, nc.tensor.transpose

            def in_slot(n):
                pe.wait_ge(ready[n % SLOTS], slot_value(n))

            def slot(i, width):
                return ring[:, i, :].rearrange("p (c n) -> p c n", n=width)

            def norm(name):
                u = NORMS.index(name)
                pe.wait_ge(s["xn_ready"], NT * u + NT)
                for b in range(4):
                    if b == 2:
                        pe.wait_ge(s["hnT_act"], 2 * u + 1)
                    if b == 3:
                        pe.wait_ge(s["hnT_dve"], 2 * u + 1)
                    for j in (0, 1):
                        for t in range(NT):
                            k = 2 * b + j
                            x = tr(b2(6 + b % 2)[:, j, t * P:(t + 1) * P], hn[:, t, k * P:(k + 1) * P], ident[:])
                    x.then_inc(s["turned"], 1)

            def normed(name):
                u = NORMS.index(name)
                pe.wait_ge(s["hnT_act"], 2 * u + 2)
                pe.wait_ge(s["hnT_dve"], 2 * u + 2)

            def small(dst, w, last=True):
                for k in range(KD):
                    x = mm(dst, w[:, k, :], hnT[:, k, :], start=(k == 0), stop=(k == KD - 1))
                if last:
                    x.then_inc(s["small_done"], 1)

            def project(name, kinds, first=0):
                for i, kind in enumerate(kinds):
                    i += first
                    n = RING_BASE[name] + i
                    in_slot(n)
                    w = slot(n % SLOTS, BLK)
                    for half in (0, 1):
                        g = PROJ_BASE[name] + 2 * i + half
                        if g >= 4:
                            pe.wait_ge(s["proj_copied"], g - 3)
                        for j in ((0, 1) if kind == "channels" else (0,)):
                            for k in range(KD):
                                if kind == "channels":
                                    c = half * T + j * P
                                    x = mm(b2(g % 4)[:, j, :], w[:, k, c:c + P], hnT[:, k, :],
                                           start=(k == 0), stop=(k == KD - 1))
                                else:
                                    x = mm(bank[g % 4][:], hnT[:, k, half * P:(half + 1) * P], w[:, k, :],
                                           start=(k == 0), stop=(k == KD - 1))
                        x.then_inc(s["proj_done"], 1)

            def sum_squares(name, R, pick, batches=None):
                _, before, n = ROWN[name]
                for i in range(n):
                    if batches is not None and i // 4 not in batches:
                        continue
                    g = (before + i) // 4
                    if i % 4 == 0:
                        pe.wait_ge(s["sq_ready"], g + 1)
                    x = mm(bank[SUM_BANK[name]][0:R, 0:T], pick(i), sq[:, g % 2, i % 4, :], start=(i == 0), stop=(i == n - 1))
                    if i % 4 == 3:
                        x.then_inc(s["sq_summed"], 1)

            def spread(name, R, pick):
                r, before, n = ROWN[name]
                pe.wait_ge(s["rownorm_ready"], r + 1)
                for b in range(n // 2):
                    g = before // 2 + b
                    if g >= 2:
                        pe.wait_ge(s["spread_used"], g - 1)
                    for j in (0, 1):
                        picked = pick(2 * b + j)
                        m = P // len(picked)
                        for i, sel in enumerate(picked):
                            x = mm(b2(6 + g % 2)[m * i:m * i + m, j, :], sel, rrow[0:R, 1], start=True, stop=True)
                    x.then_inc(s["spread_done"], 1)

            def out_projection(name, lhs):
                li, groups = LAYERS.index(name), wo_of[name].shape[0] // D
                pe.wait_ge(s["outT_ready"], li + 1)
                for i in range(2 * groups):
                    n, kg = i // groups, i % groups
                    step = RING_BASE[name + "_out"] + i
                    in_slot(step)
                    w = slot(step % SLOTS, BLK)
                    for t in range(NT):
                        for k in range(KD):
                            x = mm(bank[t + 2 * n][:], lhs(kg * KD + k)[:, t * P:(t + 1) * P], w[:, k, :],
                                   start=(kg == 0 and k == 0), stop=(kg == groups - 1 and k == KD - 1))
                        if kg == groups - 1:
                            x.then_inc(s["outp_done"], 1)

            pe.wait_ge(s["consts_ready"], 1)
            pe.wait_ge(s["vec_loaded"], 16 * (len(VEC_A) + len(VEC_B)))
            tr(bank[5][:, 0:NA], cm[0:NA, 0, 0:P], ident[0:NA, 0:NA]).then_inc(s["vec_turned"], 1)
            tr(bank[5][:, P:P + NB], cm[0:NB, 1, 0:P], ident[0:NB, 0:NB]).then_inc(s["vec_turned"], 1)
            norm("ssd")
            pe.wait_ge(s["small_loaded"], 16 * N_SMALL)
            normed("ssd")
            pe.wait_ge(s["vec_ready"], 1)
            small(bank[5][0:16, 0:T], w_dt)
            project("ssd", ["channels"] * 3)
            pe.wait_ge(s["row_ready"], 1)
            for k in range(4):
                c = k % 2
                x = tr(bank[5][:, T + 16 * k:T + 16 * k + 16], rows[0:16, 2 + k // 2, c * P:(c + 1) * P], ident[0:16, 0:16])
            x.then_inc(s["row_turned"], 1)
            project("ssd", ["channels"] * 8, first=3)
            sum_squares("sc", 16, lambda i: colsel64[:, i, :])
            spread("sc", 16, lambda i: [rowsel[:, 2 * i, 0:64], rowsel[:, 2 * i + 1, 0:64]])
            pe.wait_ge(s["ssd_conv_done"], 3)
            pe.wait_ge(s["proj_copied"], 22)
            for k in range(4):
                c, hf = k // 2, k % 2
                if k >= 2:
                    pe.wait_ge(s["ssd_xt_used"], k - 1)
                for j in range(4):
                    x = tr(b4(k % 2)[:, j, :], cm[:, 8 + 4 * hf + j, c * P:(c + 1) * P], ident[:])
                x.then_inc(s["ssd_xt_done"], 1)
            pe.wait_ge(s["col_ready"], 1)
            for g in range(2):
                tr(b4(3)[:, g, :], cm[:, 16 + g, 0:P], ident[:])
            mm(bank[3][:, 2 * P:2 * P + 16], lastrow[:], tok[:, 0, :], start=True, stop=True)
            for j in range(4):
                c, g = j // 2, j % 2
                x = mm(b4(2)[:, j, :], cm[:, 16 + g, c * P:(c + 1) * P], cm[:, 18 + g, c * P:(c + 1) * P], start=True, stop=True)
            x.then_inc(s["ssd_g_done"], 1)
            pe.wait_ge(s["ssd_xdte"], 1)
            pe.wait_ge(s["spread_used"], 4)
            for g in range(2):
                x = mm(bank[6 + g][:], tiles(30, 1, P)[:, g, :], hn[:, 0, g * BLK:(g + 1) * BLK], start=True, stop=True)
            x.then_inc(s["ssd_state"], 1)

            def ssd_spread(i):
                c, hq = i // 4, i % 4
                if i >= 2:
                    pe.wait_ge(s["ssd_exp"], i - 1)
                for j in range(4):
                    x = mm(b4(i % 2)[:, j, :], rowsel[:, 4 * hq + j, :], rows[0:16, 2, c * P:(c + 1) * P], start=True, stop=True)
                x.then_inc(s["ssd_bc"], 1)

            pe.wait_ge(s["ssd_xt_used"], 4)
            ssd_spread(0)
            for i in range(8):
                c, hq = i // 4, i % 4
                if i < 7:
                    ssd_spread(i + 1)
                pe.wait_ge(s["ssd_m"], i + 1)
                if c == 1:
                    pe.wait_ge(s["ssd_state_used"], 1)
                for j in range(4):
                    h = 4 * hq + j
                    dst = b2(2 + hq)[64 * (h % 2):64 * (h % 2) + 64, j // 2, c * P:(c + 1) * P]
                    m = hnTf[:, (i % 2) * 512 + j * P:(i % 2) * 512 + (j + 1) * P]
                    x = mm(dst, vtm[:, c, 64 * h:64 * h + 64], m, start=True, stop=(c == 0))
                    if c == 1:
                        ce = hnTf[:, 1024 + (i % 2) * 512 + j * P:1024 + (i % 2) * 512 + (j + 1) * P]
                        x = mm(dst, hn[:, 1, 64 * h:64 * h + 64], ce, start=False, stop=True)
                x.then_inc(s["ssd_y"], 1)
            sum_squares("ssd", 2, lambda i: column(i // 4, 2))
            spread("ssd", 2, lambda i: [rowsel[0:2, i // 4, :]])
            out_projection("ssd", lambda k: cm[:, (8 + k) if k < 8 else (28 + k), :])

            if stop >= 1:
                norm("moe")
                normed("moe")
                pe.wait_ge(s["x_ready"], X_BEFORE["moe"])
                for t in range(NT):
                    for k in range(KD):
                        x = mm(bank[5][:, t * (NG + NE):(t + 1) * (NG + NE)], hnT[:, k, t * P:(t + 1) * P], w_rt[:, k, :],
                               start=(k == 0), stop=(k == KD - 1))
                x.then_inc(s["rt_done"], 1)
                pe.wait_ge(s["rt_mask"], 2)
                mm(bank[5][:, P:P + NE], supper[:], r_mask[:, 0, :], start=True, stop=True)
                mm(bank[5][:, P + NE:P + 2 * NE], ones[:], r_mask[:, 0, :], start=True, stop=False)
                mm(bank[5][:, P + NE:P + 2 * NE], supper[:], r_mask[:, 1, :], start=False, stop=True)
                for t in range(NT):
                    x = mm(bank[5][:, T:T + NE], ones[:], r_mask[:, t, :], start=(t == 0), stop=(t == 1))
                x.then_inc(s["rt_rank"], 1)

                def gather(g, acc):
                    pe.wait_ge(s["moe_sel"], g + 1)
                    pe.wait_ge(s["moe_acc"], acc)
                    for k in range(KD):
                        for t in range(NT):
                            x = mm(b4(5 + k // 4)[:, k % 4, :], hn[:, t, k * P:(k + 1) * P], m_S[:, t, :],
                                   start=(t == 0), stop=(t == NT - 1))
                    x.then_inc(s["moe_gath"], 1)

                def pe_quad(q, it, g, wait_slot, release):
                    pe.wait_ge(s["moe_xg"], g + 1)
                    pe.wait_ge(s["moe_h"], it + 1)
                    for j in range(STEPS_UP):
                        w = wait_slot(q, j).rearrange("p (a e f) -> p a e f", a=2, e=QUAD)
                        for a in (0, 1):
                            for e in range(QUAD):
                                x = mm(bank[a][CAP * e:CAP * (e + 1), :], m_xg[:, j, CAP * e:CAP * (e + 1)], w[:, a, e, :],
                                       start=(j == 0), stop=(j == STEPS_UP - 1), tile_position=(0, CAP * e))
                        x.then_inc(release, 1)
                    gather(g + 1, it + 1)
                    pe.wait_ge(s["moe_sg"], it + 1)
                    pe.wait_ge(s["moe_gtc"], it + 1)
                    for t in range(NT):
                        x = tr(bank[7][:, t * P:(t + 1) * P], m_SG[:, t, :], ident[:])
                    x.then_inc(s["moe_gt"], 1)
                    pe.wait_ge(s["moe_h"], it + 2)
                    pe.wait_ge(s["moe_htc"], it + 1)
                    for c in range(STEPS_DOWN):
                        x = tr(b4(2)[:, c, :], m_h[:, c * P:(c + 1) * P], ident[:])
                    x.then_inc(s["moe_ht"], 1)
                    pe.wait_ge(s["moe_htc"], it + 2)
                    pe.wait_ge(s["moe_acc"], it + 1)
                    for c in range(STEPS_DOWN):
                        w = wait_slot(q, STEPS_UP + c).rearrange("p (e n) -> p e n", e=QUAD)
                        for n in (0, 1):
                            for e in range(QUAD):
                                x = mm(bank[3 + n][CAP * e:CAP * (e + 1), :], m_ht[:, c * P + CAP * e:c * P + CAP * (e + 1)],
                                       w[:, e, n * BLK:(n + 1) * BLK], start=(c == 0), stop=(c == STEPS_DOWN - 1),
                                       tile_position=(0, CAP * e))
                        x.then_inc(release, 1)
                    pe.wait_ge(s["moe_gtc"], it + 2)
                    pe.wait_ge(s["moe_ya"], it + 1)
                    pe.wait_ge(s["moe_yd"], it + 1)
                    pe.wait_ge(s["moe_xg"], g + 2)
                    for k in range(4):
                        t, n = k // 2, k % 2
                        x = mm(bank[[5, 6, 3, 4][k]][:], m_gt[:, t * P:(t + 1) * P], m_y[:, n, :], start=True, stop=True)
                    x.then_inc(s["moe_scat"], 1)

                base = RING_BASE["moe"]

                def ring_slot(q, j):
                    i = (base + j) % SLOTS
                    pe.wait_ge(ready[i], q * (32 * MOE_STEPS // SLOTS) + slot_value(base + j))
                    return ring[:, i, :]

                gather(0, 1)
                with pe.Fori(0, NQ) as q:
                    pe_quad(q, q, q, ring_slot, s["ring_used"])
                passes = pe.value_load(count_i[0:1, 0:1], min_val=1, max_val=T // CAP)
                with pe.If(passes > 1):
                    with pe.Fori(1, passes) as p:
                        gather(p * (NQ + 1), p * NQ + 1)

                        def ov_slot(q, j):
                            pe.wait_ge(ov_ready, (p - 1) * (32 * NQ * MOE_STEPS) + q * (32 * MOE_STEPS) + 32 * (j + 1))
                            return ring[:, 0, :]

                        with pe.Fori(0, NQ) as q:
                            pe_quad(q, p * NQ + q, p * (NQ + 1) + q, ov_slot, ov_used)

            def turn_rows(use, name, pairs):
                pe.wait_ge(s["row_ready"], use)
                for k, (src, R) in enumerate(pairs):
                    x = tr(bank[5][:, T + R * k:T + R * k + R], src, ident[0:R, 0:R])
                x.then_inc(s["row_turned"], 1)

            def fox(occ, li, name):
                norm(name)
                normed(name)
                small(bank[5][0:FOX_H, 0:T], w_f[:, occ])
                project(name, ["channels"] * 2)
                turn_rows(ROW_USE[name], name, [(rows[0:FOX_H, 3, t * P:(t + 1) * P], FOX_H) for t in range(NT)])
                for k, kind in enumerate(("channels", "channels", "tokens", "tokens")):
                    project(name, [kind], first=2 + k)
                    sum_squares(name, 16, lambda i: column(i, 16), [k])
                project(name, ["channels"], first=6)
                spread(name, 16, lambda i: [rowsel[:, i, :]])
                project(name, ["channels"], first=7)
                pe.wait_ge(s["proj_copied"], PROJ_BASE[name] + 16)
                pe.wait_ge(s["qk_ready"], occ + 1)

                def scores(h):
                    k = occ * FOX_H + h
                    if h >= 2:
                        pe.wait_ge(s["fox_l"], k - 1)
                    q, kk = cm[:, h, :], cm[:, 8 + h, :]
                    for t, (a, b) in enumerate(((0, P), (P, 3 * P))):
                        mm(bank[h % 2][:, a:b], q[:, t * P:(t + 1) * P], kk[:, 0:b - a], start=True, stop=False)
                        x = mm(bank[h % 2][:, a:b], rowsel[0:FOX_H, h, :], rows[0:FOX_H, 2, 0:b - a], start=False, stop=True)
                    x.then_inc(s["fox_s"], 1)

                scores(0)
                for h in range(FOX_H):
                    k = occ * FOX_H + h
                    if h < FOX_H - 1:
                        scores(h + 1)
                    pe.wait_ge(s["fox_p"], k + 1)
                    if h >= 2:
                        pe.wait_ge(s["fox_tc"], k - 1)
                    for j in range(3):
                        x = tr(bank[2 + h % 2][:, j * P:(j + 1) * P], f_p[h % 2][:, j * P:(j + 1) * P], ident[:])
                    x.then_inc(s["fox_t"], 1)
                    pe.wait_ge(s["fox_tc"], k + 1)
                    if h >= 2:
                        pe.wait_ge(s["fox_oc"], k - 1)
                    o, pt = bank[6 + h % 2], f_pt[h % 2]
                    mm(o[:, 0:P], vtm[:, 0, h * P:(h + 1) * P], pt[:, 0:P], start=True, stop=True)
                    mm(o[:, P:T], vtm[:, 0, h * P:(h + 1) * P], pt[:, P:2 * P], start=True, stop=False)
                    mm(o[:, P:T], vtm[:, 1, h * P:(h + 1) * P], pt[:, 2 * P:3 * P], start=False, stop=True)\
                        .then_inc(s["fox_o"], 1)
                out_projection(name, lambda k: cm[:, 16 + k, :])

            def gla():
                norm("gla")
                normed("gla")
                small(bank[5][0:16, 0:T], w_low)
                project("gla", ["channels"])
                pe.wait_ge(s["gla_low"], 1)
                for h in range(GLA_H):
                    x = mm(b2(4 + h // 2)[:, h % 2, :], w_gup[:, h * P:(h + 1) * P], rows[0:16, 0], start=True, stop=True)
                x.then_inc(s["gla_gate"], 1)
                project("gla", ["channels"] + ["tokens"] * 2 + ["channels"] * 2, first=1)
                pe.wait_ge(s["proj_copied"], PROJ_BASE["gla"] + 12)
                pe.wait_ge(s["gla_qk"], 1)
                for h in range(GLA_H):
                    for t in range(NT):
                        i, tt = 2 * h + t, slice(t * P, (t + 1) * P)
                        x = mm(b4(i // 4)[:, i % 4, :], cm[:, 4 + h, tt], cm[:, h, tt], start=True, stop=True)
                x.then_inc(s["gla_at"], 1)
                for t in range(NT):
                    for h in range(GLA_H):
                        x = tr(b4(2 + t)[:, h, :], cm[:, 28 + h, t * P:(t + 1) * P], ident[:])
                x.then_inc(s["gla_kt"], 1)

                kdec = [tf(40 + 2 * t, 2) for t in range(NT)]

                def update(c):
                    t, lo = c // 2, 64 * (c % 2)
                    for h in range(GLA_H):
                        x = mm(b2(2 * (c % 2) + h // 2)[:, h % 2, :], kdec[t][lo:lo + 64, h * P:(h + 1) * P],
                               vtm[lo:lo + 64, t, h * GLA_DV:(h + 1) * GLA_DV], start=True, stop=True)
                    x.then_inc(s["gla_st"], 1)

                pe.wait_ge(s["gla_atc"], 1)
                for h in range(GLA_H):
                    for j in (0, 1):
                        for t in range(NT):
                            i = 2 * h + t
                            mm(b2(4 + h)[:, j, t * P:(t + 1) * P], vtm[:, t, h * GLA_DV + j * P:h * GLA_DV + (j + 1) * P],
                               tiles(24, 4, P)[:, i, :], start=(j == 0 and t == 0), stop=False, skip_group_check=True)
                pe.wait_ge(s["gla_ktc"], 1)
                update(0)
                for c in range(1, 4):
                    pe.wait_ge(s["gla_stc"], c)
                    for h in range(GLA_H):
                        for j in (0, 1):
                            x = mm(b2(4 + h)[:, j, c * 64:(c + 1) * 64], tiles(16, 4, GLA_DV)[:, h, j * P:(j + 1) * P],
                                   cm[:, h, c * 64:(c + 1) * 64], start=False, stop=(c == 3 and j == 1), skip_group_check=True)
                    if c < 3:
                        update(c)
                x.then_inc(s["gla_o"], 1)
                sum_squares("gla", GLA_H, lambda i: column(i // 2, GLA_H))
                spread("gla", GLA_H, lambda i: [rowsel[0:GLA_H, i // 2, :]])
                out_projection("gla", lambda k: cm[:, 8 + k, :])

            def gdn():
                norm("gdn")
                normed("gdn")
                small(bank[5][0:8, 0:T], w_ab[:, :, 0:8], last=False)
                small(bank[5][0:8, T:2 * T], w_ab[:, :, 8:16])
                project("gdn", ["channels"] * 2)
                turn_rows(ROW_USE["gdn"], "gdn", [(rows[0:8, r, t * P:(t + 1) * P], 8) for r in (2, 0) for t in range(NT)])
                project("gdn", ["channels"], first=2)
                pe.wait_ge(s["col_ready"], 2)
                mm(bank[5][:, T + 32:T + 40], lastrow[:], tok[:, 0, 0:8], start=True, stop=True).then_inc(s["gdn_last"], 1)
                project("gdn", ["channels"], first=3)
                project("gdn", ["channels"], first=4)
                sum_squares("gdn_qk", 8, lambda i: column(i, 8), [0])
                project("gdn", ["channels"], first=5)
                sum_squares("gdn_qk", 8, lambda i: column(i, 8), [1])
                spread("gdn_qk", 8, lambda i: [rowsel[0:8, i, :]])
                pe.wait_ge(s["gdn_conv_done"], 4)
                pe.wait_ge(s["proj_copied"], PROJ_BASE["gdn"] + 12)
                for k in range(4):
                    c, hf = k // 2, k % 2
                    if k >= 2:
                        pe.wait_ge(s["gdn_xtc"], k - 1)
                    for j in range(4):
                        x = tr(b4(k % 2)[:, j, :], cm[:, 8 + 4 * hf + j, c * P:(c + 1) * P], ident[:])
                    x.then_inc(s["gdn_xt"], 1)
                pe.wait_ge(s["gdn_qk_ready"], 1)
                for c in range(NT):
                    for h in range(GDN_QH):
                        x = tr(b4(2 + c)[:, h, :], cm[:, 4 + h, c * P:(c + 1) * P], ident[:])
                x.then_inc(s["gdn_kt"], 1)
                pe.wait_ge(s["gdn_xtc"], 4)

                def blocks(a):
                    return a.rearrange("p (h d) -> p h d", d=P)

                for i in range(4):
                    c, hf = i // 2, i % 2
                    cc = slice(c * P, (c + 1) * P)
                    if i:
                        pe.wait_ge(s["gdn_exp"], i)
                        pe.wait_ge(s["gdn_x"], i)
                    for j in range(4):
                        mm(b4(0)[:, j, :], rowsel[0:8, 4 * hf + j, :], rows[0:8, 2, cc], start=True, stop=True)
                    for j in range(2):
                        k = cm[:, 4 + 2 * hf + j, cc]
                        mm(b4(1)[:, j, :], k, k, start=True, stop=True)
                        x = mm(b4(1)[:, 2 + j, :], k, cm[:, 2 * hf + j, cc], start=True, stop=True)
                    x.then_inc(s["gdn_bc"], 1)
                    pe.wait_ge(s["gdn_x"], i + 1)
                    if i:
                        pe.wait_ge(s["gdn_r_ready"], 7 * i)
                    for j in range(4):
                        x = tr(b4(5)[:, j, :], blocks(g_QT)[:, j, :], ident[:])
                    x.then_inc(s["gdn_turned"], 1)
                    for j in range(6):
                        pe.wait_ge(s["gdn_q_ready"], 7 * i + j + 1)
                        if i or j:
                            pe.wait_ge(s["gdn_qt_ready"], 6 * i + j)
                        Q, QT, R = blocks(g_Q), blocks(g_QT), blocks(g_R)
                        for h in range(4):
                            mm(b4(6)[:, h, :], QT[:, h, :], Q[:, h, :], start=True, stop=True)
                            x = mm(b4(7)[:, h, :], Q[:, h, :], QT[:, h, :], start=True, stop=True)
                        x.then_inc(s["gdn_power"], 1)
                        pe.wait_ge(s["gdn_qt_ready"], 6 * i + j + 1)
                        pe.wait_ge(s["gdn_r_ready"], 7 * i + j + 1)
                        for h in range(4):
                            x = mm(b4(4)[:, h, :], QT[:, h, :], R[:, h, :], start=True, stop=True)
                        x.then_inc(s["gdn_r"], 1)
                    pe.wait_ge(s["gdn_r_ready"], 7 * i + 7)
                    if i:
                        pe.wait_ge(s["gdn_u_ready"], i)
                    if i == 3:
                        pe.wait_ge(s["gdn_w_ready"], 1)
                    if i == 0:
                        pe.wait_ge(s["gdn_ktc"], 1)
                    for h in range(4):
                        if c == 1:
                            mm(b4(3)[:, h, :], blocks(g_kbg)[:, 4 * hf + h, :], R[:, h, :], start=True, stop=True)
                        x = mm(b4(2)[:, h, :], R[:, h, :], vtm[:, c, (4 * hf + h) * P:(4 * hf + h + 1) * P], start=True, stop=True)
                    x.then_inc(s["gdn_uw"], 1)
                pe.wait_ge(s["gdn_u_ready"], 4)
                pe.wait_ge(s["gdn_w_ready"], 2)
                u = [blocks(g_u[i]) for i in range(4)]
                qkk = [blocks(g_qkk[i]) for i in range(4)]
                state = tiles(40, 4, P)
                for h in range(8):
                    x = mm(b4(h // 4)[:, h % 4, :], blocks(g_kdec)[:, h, :], u[h // 4][:, h % 4, :], start=True, stop=True)
                x.then_inc(s["gdn_s"], 1)
                for h in range(8):
                    mm(b2(4 + h // 2)[:, h % 2, 0:P], u[h // 4][:, h % 4, :], qkk[h // 4][:, h % 4, :], start=True, stop=True)
                pe.wait_ge(s["gdn_s_ready"], 1)
                for h in range(8):
                    x = mm(b4(2 + h // 4)[:, h % 4, :], blocks(g_w[h // 4])[:, h % 4, :], state[:, h, :], start=True, stop=True)
                x.then_inc(s["gdn_ws"], 1)
                pe.wait_ge(s["gdn_new"], 1)
                for h in range(8):
                    dst = b2(4 + h // 2)[:, h % 2, P:T]
                    mm(dst, state[:, h, :], blocks(g_qd[h // 4])[:, h % 4, :], start=True, stop=False)
                    x = mm(dst, u[2 + h // 4][:, h % 4, :], qkk[2 + h // 4][:, h % 4, :], start=False, stop=True)
                x.then_inc(s["gdn_o"], 1)
                sum_squares("gdn_o", 8, lambda i: column(i, 8))
                spread("gdn_o", 8, lambda i: [rowsel[0:8, i, :]])
                out_projection("gdn", lambda k: cm[:, 16 + k, :])

            if stop >= 2:
                fox(0, 1, "fox0")
            if stop >= 3:
                gla()
            if stop >= 4:
                gdn()
            if stop >= 5:
                fox(1, 4, "fox1")


_INS = ["x", "norm_mix", "w_in", "ssd_conv_w", "ssd_conv_b", "dt_bias", "a_log", "d_skip", "ssd_norm", "sc_conv_w",
        "sc_norm", "w_out", "norm_ffn", "w_router_group", "w_router_expert", "w_gate", "w_up", "w_down", "final_norm",
        "norm_w_2", "fox_w_in_2", "fox_b_f_2", "fox_q_gain_2", "fox_k_gain_2", "fox_w_out_2", "gla_w_in_2",
        "gla_w_gate_up_2", "gla_b_gate_2", "gla_o_gain_2", "gla_w_out_2", "gdn_w_in_2", "gdn_conv_w_2",
        "gdn_a_log_2", "gdn_dt_bias_2", "gdn_o_gain_2", "gdn_w_out_2"]
UPTO = "all"


def kernel(**inputs):
    import numpy as _np
    import concourse.bacc as _bacc
    from concourse.bass_utils import run_bass_kernel_spmd as _run

    nc = _bacc.Bacc("TRN2", target_bir_lowering=False, num_devices=1)
    arrays, args = {}, []
    for name in _INS:
        a = _np.ascontiguousarray(inputs[name])
        if name in ("w_gate", "w_up", "w_down"):
            a = a[0]
        arrays[f"in_{name}"] = a
        args.append(nc.dram_tensor(f"in_{name}", a.shape, F32, kind="ExternalInput").ap())
    out = nc.dram_tensor("out", (1, T, D), F32, kind="ExternalOutput").ap()
    build(nc, *args, out, upto=UPTO)
    r = _run(nc, [arrays], core_ids=[0])
    return r.results[0]["out"]
```

```python
from contextlib import ExitStack

import concourse.bass as bass
from concourse import mybir

F32 = mybir.dt.float32
F32R = mybir.dt.float32r
I32 = mybir.dt.int32
ALU = mybir.AluOpType
ACT = mybir.ActivationFunctionType
AX = mybir.AxisListType

P = 128
T = 256
NT = T // P
D = 1024
KD = D // P
BLK = 512
EPS = 1e-6
RSQRT_SEED = 1597463007.0

SLOTS = 4
SLOT = KD * BLK
UNITS = 4
UNIT = SLOT // UNITS
PARTS = 3

SSD_H, SSD_N = 16, 128
SSD_W, SSD_XBC = 1024, 1536
FOX_H = 8
GLA_H, GLA_DK, GLA_DV, GLA_CH = 4, 128, 256, 64
GDN_QH, GDN_VH = 4, 8
NG, EPG = 4, 8
NE = NG * EPG
QUAD = 4
CAP = P // QUAD
NQ = NE // QUAD
FF = 512
STEPS_UP, STEPS_DOWN = KD, FF // P
MOE_STEPS = STEPS_UP + STEPS_DOWN

VEC_A = [("ssd_conv_w", 48), ("ssd_conv_b", 12), ("ssd_norm", 8), ("sc_conv_w", 24), ("sc_norm", 8),
         ("norm_mix", 8), ("norm_ffn", 8), ("fox_q_gain", 2), ("fox_k_gain", 2), ("gla_o_gain", 2),
         ("gla_b_gate", 4), ("gdn_o_gain", 1)]
VEC_B = [("norm_w", 32), ("gdn_conv_w", 64)]
NA = sum(n for _, n in VEC_A)
NB = sum(n for _, n in VEC_B)
VCOL = {}
for _tab, _start in ((VEC_A, 0), (VEC_B, P)):
    for _name, _n in _tab:
        VCOL[_name] = _start
        _start += _n

LAYERS = ["ssd", "fox0", "gla", "gdn", "fox1"]
KINDS = {"ssd": ["channels"] * 11,
         "fox0": ["channels"] * 4 + ["tokens"] * 2 + ["channels"] * 2,
         "gla": ["channels"] * 2 + ["tokens"] * 2 + ["channels"] * 2,
         "gdn": ["channels"] * 6}
KINDS["fox1"] = KINDS["fox0"]
PROJ_BLOCKS = {_l: len(KINDS[_l]) for _l in LAYERS}
PROJ_BASE, _n = {}, 0
for _l in LAYERS:
    PROJ_BASE[_l] = _n
    _n += 2 * PROJ_BLOCKS[_l]

OUT_GROUPS = {_l: 2 if _l == "ssd" else 1 for _l in LAYERS}
UNIT_BASE, PAIR_BASE, _n, _m = {}, {}, 0, 0
for _l in LAYERS:
    UNIT_BASE[_l] = _n
    UNIT_BASE[_l + "_out"] = _n + UNITS * PROJ_BLOCKS[_l]
    _n += UNITS * (PROJ_BLOCKS[_l] + 2 * OUT_GROUPS[_l])
    PAIR_BASE[_l] = _m
    _m += 4 * OUT_GROUPS[_l]

RING_BASE, _n = {}, 0
for _l in LAYERS:
    RING_BASE[_l] = _n
    _n += PROJ_BLOCKS[_l]
    RING_BASE[_l + "_out"] = _n
    _n += 2 * OUT_GROUPS[_l]
    if _l == "ssd":
        RING_BASE["moe"] = _n
        _n += NQ * MOE_STEPS

ROWN = {}
_n = 0
for _name, _tiles in (("sc", 8), ("ssd", 8), ("fox0", 16), ("gla", 8), ("gdn_qk", 8), ("gdn_o", 8), ("fox1", 16)):
    ROWN[_name] = (len(ROWN), _n, _tiles)
    _n += _tiles

SOFT_USE = {"ssd": 1, "fox0": 2, "gdn": 3, "fox1": 4}
ROW_USE = {"ssd": 1, "fox0": 2, "gdn": 3, "fox1": 4}
SUM_BANK = 4

X_BEFORE = {"moe": 4, "fox0": 6, "gla": 10, "gdn": 14, "fox1": 18, "end": 22}
NORMS = ["ssd", "moe", "fox0", "gla", "gdn", "fox1"]
SPLIT_NORMS = [_n for _n in NORMS if _n != "moe"]
SQS = ["ssd", "moe", "final", "fox0", "gla", "gdn", "fox1"]


def build(nc, x_in, norm_mix, w_in, ssd_conv_w, ssd_conv_b, dt_bias, a_log, d_skip, ssd_norm, sc_conv_w,
          sc_norm, w_out, norm_ffn, w_router_group, w_router_expert, w_gate, w_up, w_down, final_norm,
          norm_w, fox_w_in, fox_b_f, fox_q_gain, fox_k_gain, fox_w_out, gla_w_in, gla_w_gate_up, gla_b_gate,
          gla_o_gain, gla_w_out, gdn_w_in, gdn_conv_w, gdn_a_log, gdn_dt_bias, gdn_o_gain, gdn_w_out, out,
          upto="all"):
    ctx = ExitStack()
    with ctx:
        def sb(name, shape, dt=F32):
            return ctx.enter_context(nc.sbuf_tensor(name, shape, dt))

        def sem(name):
            return ctx.enter_context(nc.semaphore(name))

        ring = sb("ring", [P, SLOTS, SLOT])
        x_res = sb("x_res", [P, NT, D])
        hn = sb("hn", [P, NT, D])
        hnT = sb("hnT", [P, KD, T])
        hnT_h, hnT_l = sb("hnT_h", [P, KD, T], F32R), sb("hnT_l", [P, KD, T], F32R)
        w_h, w_l = sb("w_h", [P, PARTS, UNIT], F32R), sb("w_l", [P, PARTS, UNIT], F32R)
        cm = sb("cm", [P, 44, T])
        vtm = sb("vtm", [P, NT, D])
        sq = sb("sq", [P, 2, 4, T])
        onehot = sb("onehot", [P, 32])
        colsel64 = sb("colsel64", [P, 8, 16])
        ident = sb("ident", [P, P])
        ones = sb("ones", [P, P])
        qgain = sb("qgain", [P, 1])
        upper = sb("upper", [P, P])
        supper = sb("supper", [P, P])
        slower = sb("slower", [P, P])
        upper64 = sb("upper64", [P, P])
        lastrow = sb("lastrow", [P, P])
        negmask = sb("negmask", [P, 2, P])
        iota_i = sb("iota_i", [P, CAP], I32)
        iota = sb("iota", [P, CAP])
        vec = sb("vec", [P, 2 * P])
        ss = sb("ss", [P, 8])
        w_dt = sb("w_dt", [P, KD, SSD_H])
        w_f = sb("w_f", [P, 2, KD, FOX_H])
        w_low = sb("w_low", [P, KD, 16])
        w_ab = sb("w_ab", [P, KD, 16])
        w_rt = sb("w_rt", [P, KD, NG + NE])
        w_gup = sb("w_gup", [16, BLK])
        cols = sb("cols", [16, 8])
        ncols = sb("ncols", [16, 2])
        dsk = sb("dsk", [P, 8])
        rrow = sb("rrow", [16, 3, T])
        rows = sb("rows", [16, 4, T])
        tok = sb("tok", [P, 8, 16])
        count_i = sb("count_i", [1, 1], I32)

        bank = [ctx.enter_context(nc.psum_tensor(f"bank{i}", [P, 512], F32)) for i in range(8)]

        cmf = cm[:].rearrange("p a b -> p (a b)")
        hnTf = hnT[:].rearrange("p a b -> p (a b)")

        def tiles(a, n, inner=T):
            return cmf[:, a * T:(a + n) * T].rearrange("p (n i) -> p n i", i=inner)

        def b2(i):
            return bank[i][:].rearrange("p (a b) -> p a b", b=T)

        def b4(i):
            return bank[i][:].rearrange("p (a b) -> p a b", b=P)

        s = {n: sem(n) for n in (
            "x_loaded", "vec_loaded", "small_loaded", "fnorm_loaded", "out_stored", "ring_used",
            "pool_chain", "ident_ready", "consts_ready",
            "dve_chain", "act_chain", "moe_chain", "pass_chain", "sp_turn",
            "vec_turned", "vec_ready", "cols_ready",
            "ss_ready", "xn_ready", "turned", "hnT_act", "hnT_dve", "x_ready",
            "hnT_high", "hnT_own", "hnT_split", "high_ready", "low_ready", "unit_done", "proj_copied", "small_done",
            "sq_ready", "sq_summed", "rownorm_ready", "spread_done", "spread_used",
            "out_high", "out_low",
            "lin_ready", "tanh_ready", "z_tanh", "z_ready",
            "row_arg", "qk_ready", "row_ln", "row_ready", "row_turned", "col_ready",
            "ssd_conv_done", "ssd_xt_done", "ssd_xt_used", "ssd_g_done", "ssd_bc", "ssd_seg", "ssd_exp",
            "ssd_m", "ssd_y", "ssd_dte_arg", "ssd_dte", "ssd_xdte", "ssd_state", "ssd_state_used", "ssd_yready",
            "rt_done", "rt_arg", "rt_exp", "rt_mask", "rt_rank", "rt_passes", "moe_sel", "moe_sg", "moe_gath", "moe_xg", "moe_tanh",
            "moe_h", "moe_gt", "moe_gtc", "moe_ht", "moe_htc", "moe_ya", "moe_yd", "moe_scat", "moe_acc", "moe_done",
            
            "fox_s", "fox_l", "fox_e", "fox_p", "fox_t", "fox_tc", "fox_o", "fox_oc",
            "gla_low", "gla_gate", "gla_arg", "gla_ln", "gla_dec", "gla_exp", "gla_qk", "gla_at", "gla_atc", "gla_kt",
            "gla_ktc", "gla_st", "gla_stc", "gla_o", "gla_oc",
            "gdn_row_free", "gdn_beta_exp", "gdn_last", "gdn_col_arg", "gdn_col_exp", "gdn_conv_done", "gdn_qk_ready",
            "gdn_xt", "gdn_xtc", "gdn_kt", "gdn_ktc", "gdn_bc", "gdn_arg", "gdn_exp", "gdn_x", "gdn_turned", "gdn_q_ready",
            "gdn_qt_ready", "gdn_power", "gdn_r", "gdn_r_ready", "gdn_uw", "gdn_u_ready", "gdn_w_ready", "gdn_s",
            "gdn_s_ready", "gdn_ws", "gdn_new", "gdn_o", "gdn_oc",
        )}
        ready = [sem(f"slot_ready{i}") for i in range(SLOTS)]
        ov_ready, ov_used = sem("ov_ready"), sem("ov_used")

        earlier = sb("earlier", [P, 8, 8])

        def column(r, R):
            return onehot[:, 15 - r:15 - r + R]

        def row_of(r, R, n=P):
            return ident[0:R, r:r + 1].to_broadcast([R, n])

        def tf(a, n):
            return cmf[:, a * T:(a + n) * T]

        used_floats = [0]

        def view(*shape):
            size = 1
            for k in shape:
                size *= k
            a = cmf[:, used_floats[0]:used_floats[0] + size]
            used_floats[0] += size
            if len(shape) == 2:
                return a.rearrange("p (a b) -> p a b", a=shape[0])
            return a

        m_xg, m_S, m_SG, m_gt = view(KD, P), view(NT, P), view(NT, P), view(T)
        m_tanh, m_silu, m_h, m_ht, m_y = view(FF), view(FF), view(FF), view(FF), view(2, BLK)
        r_lg, r_eg, r_n, r_gs, r_es, r_ex = (view(NT, NG + NE), view(NT, NG), view(NT, 2), view(NT, 1), view(NT, EPG),
                                             view(NT, EPG))
        r_c1, r_c2, r_gsel, r_sel, r_sum = view(NE, 2), view(NE, 2), view(NT, NG), view(NT, EPG), view(NT, 4)
        r_mask, r_gate, r_pm, r_pass = view(NT, NE), view(NT, NE + QUAD), view(NT, NE + QUAD), view(2, 16)
        r_prod = view(NG, EPG)
        N_SMALL = 12 + NG + 2

        f_l = [cmf[:, 24 * T + i * 384:24 * T + (i + 1) * 384] for i in (0, 1)]
        f_p = [cmf[:, 27 * T + i * 384:27 * T + (i + 1) * 384] for i in (0, 1)]
        f_pt = [cmf[:, 30 * T + i * 384:30 * T + (i + 1) * 384] for i in (0, 1)]
        f_n = tiles(33, 1, 2)[:, 0:2, :]
        f_s = tiles(33, 1, 2)[:, 2:4, :]
        f_r = tiles(33, 1, 2)[:, 4:6, :]

        g_Q, g_QT, g_R, g_dt = (hnTf[:, i * 512:(i + 1) * 512] for i in range(4))
        g_d = tf(40, 2)
        g_km, g_qm = tiles(42, 1, P), tiles(43, 1, P)
        g_w = [hn[:, 0, i * 512:(i + 1) * 512] for i in (0, 1)]
        g_qd = [hn[:, 1, i * 512:(i + 1) * 512] for i in (0, 1)]
        g_u = [tf(8 + 2 * i, 2) for i in range(4)]
        g_qkk = [tf(24 + 2 * i, 2) for i in range(4)]
        g_kbg, g_kdec = tf(32, 4), tf(36, 4)

        def slot_value(n):
            return 32 * (n // SLOTS + 1)

        def released(n):
            for l in LAYERS:
                b = RING_BASE[l]
                if b <= n < b + PROJ_BLOCKS[l] + 2 * OUT_GROUPS[l]:
                    return s["low_ready"], UNIT_BASE[l] + UNITS * (n - b + 1)
            return s["ring_used"], n - RING_BASE["moe"] + 1

        def unit_of(u):
            for l in LAYERS:
                i, m = (u - UNIT_BASE[l]) // UNITS, (u - UNIT_BASE[l]) % UNITS
                if 0 <= i < PROJ_BLOCKS[l] + 2 * OUT_GROUPS[l]:
                    n = RING_BASE[l] + i
                    w = ring[:, n % SLOTS, :].rearrange("p (c n) -> p c n", n=BLK)
                    if i < PROJ_BLOCKS[l] and KINDS[l][i] == "channels":
                        return n, w[:, :, m * P:(m + 1) * P], P
                    return n, w[:, 2 * m:2 * m + 2, :], BLK

        def part(x, u, width):
            return x[:, u % PARTS, :].rearrange("p (c n) -> p c n", n=width)

        def bank_units(layer, b):
            if KINDS[layer][b // 2] == "channels":
                return UNIT_BASE[layer] + 2 * b + 2
            return UNIT_BASE[layer] + UNITS * (b // 2 + 1)

        def block_halves(w, col):
            v = w[:, col:col + BLK].rearrange("(c p) n -> p c n", p=P)
            return [v[:, 0:4, :], v[:, 4:8, :]]

        up_v = [w.rearrange("(q j) (c p) f -> q c p j f", j=QUAD, p=P) for w in (w_gate, w_up)]
        down_v = w_down.rearrange("(q j) (c p) n -> q c p j n", j=QUAD, p=P)

        def slot_half(i, h):
            return ring[:, i, h * (SLOT // 2):(h + 1) * (SLOT // 2)]

        def moe_halves(i, q, j):
            if j < STEPS_UP:
                return [(slot_half(i, h).rearrange("p (e f) -> p e f", e=QUAD), up_v[h][q, j]) for h in (0, 1)]
            return [(slot_half(i, h).rearrange("p (e f) -> p e f", e=QUAD // 2),
                     down_v[q, j - STEPS_UP][:, 2 * h:2 * h + 2, :]) for h in (0, 1)]

        col_of = {
            "ssd": [SSD_W + BLK * i for i in range(3)] +
                   [SSD_W + SSD_XBC + SSD_H + D + BLK * i for i in range(4)] +
                   [SSD_W + SSD_XBC + SSD_H + BLK * i for i in range(2)] +
                   [BLK * i for i in range(2)],
            "fox0": [BLK * i for i in range(8)], "fox1": [BLK * i for i in range(8)],
            "gla": [BLK * i for i in range(6)],
            "gdn": [BLK * i for i in range(6)],
        }
        w_of = {"ssd": w_in[0], "fox0": fox_w_in[0], "gla": gla_w_in[0], "gdn": gdn_w_in[0], "fox1": fox_w_in[1]}
        wo_of = {"ssd": w_out[0], "fox0": fox_w_out[0], "gla": gla_w_out[0], "gdn": gdn_w_out[0], "fox1": fox_w_out[1]}

        stop = ["ssd", "moe", "fox0", "gla", "gdn", "all"].index(upto)
        layers = LAYERS[:[1, 1, 2, 3, 4, 5][stop]]

        block = ctx.enter_context(nc.Block())

        @block.sync
        def _(sp):
            for t in range(NT):
                sp.dma_start(x_res[:, t, :], x_in[0, t * P:(t + 1) * P, :]).then_inc(s["x_loaded"], 16)

            def put(n, halves):
                i = n % SLOTS
                if n >= SLOTS:
                    sp.wait_ge(*released(n - SLOTS))
                for dst, src in halves:
                    sp.dma_start(dst, src).then_inc(ready[i], 16)

            def put_block(n, w, col):
                halves = block_halves(w, col)
                put(n, [(slot_half(n % SLOTS, h).rearrange("p (c n) -> p c n", c=4), halves[h]) for h in (0, 1)])

            sp.wait_ge(s["vec_loaded"], 16 * (len(VEC_A) + len(VEC_B)))
            sp.wait_ge(s["small_loaded"], 16 * N_SMALL)
            for l in layers:
                for i, col in enumerate(col_of[l]):
                    put_block(RING_BASE[l] + i, w_of[l], col)
                groups = wo_of[l].shape[0] // D
                for i in range(2 * groups):
                    g = groups - 1 - i // 2
                    put_block(RING_BASE[l + "_out"] + i, wo_of[l][g * D:(g + 1) * D, :], BLK * (i % 2))
                if l == "ssd" and stop >= 1:
                    base = RING_BASE["moe"]
                    for j in range(SLOTS):
                        put(base + j, moe_halves((base + j) % SLOTS, 0, j))
                    for j in range(SLOTS, MOE_STEPS):
                        put(base + j, moe_halves((base + j) % SLOTS, 0, j))
                    with sp.Fori(1, NQ) as q:
                        for j in range(MOE_STEPS):
                            i = (base + j) % SLOTS
                            sp.wait_ge(s["ring_used"], q * MOE_STEPS + (j - SLOTS + 1))
                            sp.sem_inc(s["sp_turn"], 1)
                            for dst, src in moe_halves(i, q, j):
                                sp.dma_start(dst, src).then_inc(ready[i], 16)
                    sp.wait_ge(s["rt_passes"], 1)
                    passes = sp.value_load(count_i[0:1, 0:1], min_val=1, max_val=T // CAP)
                    with sp.If(passes > 1):
                        sp.wait_ge(s["ring_used"], NQ * MOE_STEPS)
                        with sp.Fori(1, passes) as p:
                            with sp.Fori(0, NQ) as q:
                                for j in range(MOE_STEPS):
                                    for dst, src in moe_halves(0, q, j):
                                        sp.dma_start(dst, src).then_inc(ov_ready, 16)
                                    sp.wait_ge(ov_used, (p - 1) * (NQ * MOE_STEPS) + q * MOE_STEPS + (j + 1))
                                    sp.sem_inc(s["sp_turn"], 1)
            last = {0: 4, 1: 6, 2: 10, 3: 14, 4: 18, 5: 22}[stop]
            sp.wait_ge(s["x_ready"], last)
            for t in range(NT):
                sp.dma_start(out[0, t * P:(t + 1) * P, :], x_res[:, t, :]).then_inc(s["out_stored"], 16)
            sp.wait_ge(s["out_stored"], 16 * NT)

        @block.gpsimd
        def _(pool):
            n = [0]

            def link(ins):
                n[0] += 1
                ins.then_inc(s["pool_chain"], 1)
                pool.wait_ge(s["pool_chain"], n[0])

            link(nc.gpsimd.memset(ident[:], 0.0))
            link(nc.gpsimd.affine_select(out=ident[:], in_=ident[:], compare_op=ALU.not_equal, fill=1.0, base=0,
                                         pattern=[[-1, P]], channel_multiplier=1))
            pool.sem_inc(s["ident_ready"], 1)
            for t in (onehot, colsel64, lastrow, negmask):
                link(nc.gpsimd.memset(t[:], 0.0))
            for t in (ones, upper, supper, slower, upper64, earlier):
                link(nc.gpsimd.memset(t[:], 1.0))
            link(nc.gpsimd.iota(iota_i[:], pattern=[[1, CAP]], base=0, channel_multiplier=0))
            link(nc.gpsimd.tensor_copy(iota[:], iota_i[:]))

            def select(a, op, fill, base, pattern, cmul):
                link(nc.gpsimd.affine_select(out=a, in_=a, compare_op=op, fill=fill, base=base,
                                             pattern=pattern, channel_multiplier=cmul))

            select(lastrow[:], ALU.not_equal, 1.0, -(P - 1), [[0, P]], 1)
            select(onehot[:], ALU.not_equal, 1.0, -15, [[1, 32]], 0)
            for half in (0, 1):
                select(colsel64[64 * half:64 * half + 64], ALU.not_equal, 1.0, half, [[2, 8], [-1, 16]], 0)
            select(upper[:], ALU.is_ge, 0.0, 0, [[1, P]], -1)
            select(supper[:], ALU.is_ge, 0.0, -1, [[1, P]], -1)
            select(slower[:], ALU.is_ge, 0.0, -1, [[-1, P]], 1)
            select(earlier[:], ALU.is_ge, 0.0, -1, [[1, 8], [-1, 8]], 0)
            select(negmask[:, 1, :], ALU.is_ge, -1e30, 0, [[-1, P]], 1)
            select(upper64[:], ALU.is_ge, 0.0, 0, [[1, P]], -1)
            select(upper64[:, 64:P], ALU.is_ge, 0.0, -64, [[0, 64]], 1)
            pool.sem_inc(s["consts_ready"], 1)
            for u in range(UNIT_BASE[layers[-1] + "_out"] + 2 * UNITS * OUT_GROUPS[layers[-1]]):
                _, w, width = unit_of(u)
                pool.wait_ge(s["high_ready"], u + 1)
                nc.gpsimd.tensor_tensor(part(w_l, u, width), w, part(w_h, u, width).bitcast(F32),
                                        ALU.subtract).then_inc(s["low_ready"], 1)

        @block.scalar
        def _(act):
            n_link = [0]

            def link(ins):
                n_link[0] += 1
                ins.then_inc(s["act_chain"], 1)
                act.wait_ge(s["act_chain"], n_link[0])

            af = nc.scalar.activation

            staged = [tiles(0, 1)[0:NA, 0, 0:P], tiles(1, 1)[0:NB, 0, 0:P]]
            srcs = {"ssd_conv_w": ssd_conv_w, "ssd_conv_b": ssd_conv_b, "ssd_norm": ssd_norm, "sc_conv_w": sc_conv_w,
                    "sc_norm": sc_norm, "norm_mix": norm_mix, "norm_ffn": norm_ffn, "fox_q_gain": fox_q_gain,
                    "fox_k_gain": fox_k_gain, "gla_o_gain": gla_o_gain, "gla_b_gate": gla_b_gate,
                    "gdn_o_gain": gdn_o_gain, "norm_w": norm_w, "gdn_conv_w": gdn_conv_w}
            for tab, dst in zip((VEC_A, VEC_B), staged):
                at = 0
                for name, k in tab:
                    src = srcs[name]
                    flat = src.rearrange("a b c -> (a b c)") if len(src.shape) == 3 else src.rearrange("a b -> (a b)")
                    act.dma_start(dst[at:at + k, :], flat.rearrange("(r p) -> r p", p=P)).then_inc(s["vec_loaded"], 16)
                    at += k

            small = []
            for dst, src in (
                (w_dt[:], w_in[0][:, SSD_W + SSD_XBC:SSD_W + SSD_XBC + SSD_H].rearrange("(c p) n -> p c n", p=P)),
                (w_f[:, 0], fox_w_in[0][:, 4 * D:4 * D + FOX_H].rearrange("(c p) n -> p c n", p=P)),
                (w_f[:, 1], fox_w_in[1][:, 4 * D:4 * D + FOX_H].rearrange("(c p) n -> p c n", p=P)),
                (w_low[:], gla_w_in[0][:, 3 * D:3 * D + 16].rearrange("(c p) n -> p c n", p=P)),
                (w_ab[:], gdn_w_in[0][:, 3 * D:3 * D + 16].rearrange("(c p) n -> p c n", p=P)),
                (w_rt[:, :, 0:NG], w_router_group[0].rearrange("(c p) n -> p c n", p=P)),
                (w_gup[:], gla_w_gate_up[0]),
                (cols[0:16, 0:1], a_log.rearrange("a h -> h a")), (cols[0:16, 1:2], dt_bias.rearrange("a h -> h a")),
                (cols[0:8, 2:4], fox_b_f.rearrange("a h -> h a")),
                (cols[0:8, 4:5], gdn_a_log.rearrange("a h -> h a")), (cols[0:8, 5:6], gdn_dt_bias.rearrange("a h -> h a")),
            ) + tuple((w_rt[:, :, NG + EPG * g:NG + EPG * (g + 1)],
                       w_router_expert[0, g].rearrange("(c p) n -> p c n", p=P)) for g in range(NG)) \
              + tuple((dsk[64 * h:64 * h + 64, :],
                       d_skip[0].rearrange("(i two) -> two i", two=2)[h:h + 1, :].to_broadcast([64, 8])) for h in (0, 1)):
                small.append(act.dma_start(dst, src, allow_slow_non_contiguous=True).then_inc(s["small_loaded"], 16))
            assert len(small) == N_SMALL

            def square_sum(which, value):
                if which == 0:
                    act.wait_ge(s["x_loaded"], 16 * NT)
                else:
                    act.wait_ge(s["x_ready"], value)
                for t in range(NT):
                    af(hn[:, t, :], x_res[:, t, :], ACT.Square, accum_out=ss[:, t:t + 1]).then_inc(s["ss_ready"], 1)

            n_high = [0]

            def high(end):
                for u in range(n_high[0], end):
                    n, w, width = unit_of(u)
                    act.wait_ge(ready[n % SLOTS], slot_value(n))
                    if u >= PARTS:
                        act.wait_ge(s["unit_done"], u - PARTS + 1)
                    af(part(w_h, u, width), w, ACT.Copy).then_inc(s["high_ready"], 1)
                n_high[0] = max(n_high[0], end)

            def layer_start(name):
                if name != "ssd":
                    high(UNIT_BASE[name] + 2)
                square_sum(SQS.index(name), X_BEFORE.get(name, 0))
                if name != "ssd":
                    high(UNIT_BASE[name] + 3)

            def out_high(name, pair, src, n=1):
                k = 2 * (pair % 4)
                if pair >= 4:
                    act.wait_ge(s["unit_done"], UNIT_BASE[name + "_out"] + UNITS + pair % 4 + 1)
                af(hnT_h[:, k:k + 2 * n, :], src, ACT.Copy).then_inc(s["out_high"], n)

            def norm_copies(u, col, split=True):
                for b in (0, 2):
                    act.wait_ge(s["turned"], 4 * u + b + 1)
                    for j in (0, 1):
                        i = af(hnT[:, 2 * b + j, :], b2(6)[:, j, :], ACT.Copy,
                               scale=vec[:, col + 2 * b + j:col + 2 * b + j + 1])
                    i.then_inc(s["hnT_act"], 1)
                    if split:
                        act.wait_ge(s["hnT_act"], 2 * u + b // 2 + 1)
                        af(hnT_h[:, 2 * b:2 * b + 2, :], hnT[:, 2 * b:2 * b + 2, :], ACT.Copy).then_inc(s["hnT_high"], 1)

            def copy_bank(layer, b, dst, scale=1.0):
                g = PROJ_BASE[layer] + b
                done = bank_units(layer, b)
                high(min(done + PARTS, UNIT_BASE[layer + "_out"] + PARTS))
                act.wait_ge(s["unit_done"], done)
                af(dst, bank[g % 4][:], ACT.Copy, scale=scale).then_inc(s["proj_copied"], 1)

            def own_copies(layer, banks):
                act.wait_ge(s["proj_copied"], PROJ_BASE[layer] + banks)

            def squares(name, k, src):
                _, before, _ = ROWN[name]
                g = before // 4 + k
                if g >= 2:
                    act.wait_ge(s["sq_summed"], g - 1)
                af(sq[:, g % 2].rearrange("p a b -> p (a b)"), src, ACT.Square).then_inc(s["sq_ready"], 1)

            def silu_z(li, z0, summed):
                act.wait_ge(s["sq_summed"], summed)
                for b in (0, 1):
                    af(sq[:, b].rearrange("p a b -> p (a b)"), cmf[:, (z0 + 4 * b) * T:(z0 + 4 * b + 4) * T],
                       ACT.Tanh).then_inc(s["z_tanh"], 1)

            def softplus_row(k, src, dst, parts):
                act.wait_ge(s["row_arg"], k)
                link(af(dst[0:parts], src[0:parts], ACT.Exp, scale=-1.0))
                af(dst[0:parts], dst[0:parts], ACT.Ln, bias=1.0).then_inc(s["row_ln"], 1)

            layer_start("ssd")
            act.wait_ge(s["small_loaded"], 16 * N_SMALL)
            af(ncols[0:16, 0:1], cols[0:16, 0:1], ACT.Exp)
            af(ncols[0:8, 1:2], cols[0:8, 4:5], ACT.Exp).then_inc(s["cols_ready"], 1)
            act.wait_ge(s["vec_ready"], 1)
            norm_copies(0, VCOL["norm_mix"])
            softplus_row(1, rows[:, 1, :], rows[:, 2, :], 16)
            for b in range(6):
                copy_bank("ssd", b, cmf[:, (8 + 2 * b) * T:(10 + 2 * b) * T])
            dst = [28 + 2 * i for i in range(4)] + [36 + 2 * i for i in range(4)] + [20 + 2 * i for i in range(4)] + \
                  [2 * i for i in range(4)]
            for b in range(16):
                copy_bank("ssd", 6 + b, cmf[:, dst[b] * T:(dst[b] + 2) * T], 0.5 if b >= 12 else 1.0)
                if b in (0, 3, 6):
                    k = b // 3
                    act.wait_ge(s["lin_ready"], k + 1)
                    af(vtm[:, 1, :], vtm[:, 0, :], ACT.Tanh).then_inc(s["tanh_ready"], 1)
            for k in range(2):
                act.wait_ge(s["ssd_conv_done"], 3 + k + 1)
                squares("sc", k, cmf[:, (36 + 4 * k) * T:(40 + 4 * k) * T])
            own_copies("ssd", 22)
            silu_z(0, 0, 2)
            act.wait_ge(s["spread_used"], 4)
            out_high("ssd", 0, tiles(36, 8), 4)
            act.wait_ge(s["ssd_dte_arg"], 1)
            af(tok[:, 4, :], tok[:, 4, :], ACT.Exp).then_inc(s["ssd_dte"], 1)
            for i in range(8):
                c, hq = i // 4, i % 4
                act.wait_ge(s["ssd_seg"], i + 1)
                m = hnTf[:, (i % 2) * 512:(i % 2) * 512 + 512]
                if c == 1:
                    ce = hnTf[:, 1024 + (i % 2) * 512:1536 + (i % 2) * 512]
                    if i >= 6:
                        act.wait_ge(s["ssd_y"], i - 1)
                    af(ce, bank[i % 2][:], ACT.Exp)
                af(m, m, ACT.Exp).then_inc(s["ssd_exp"], 1)
            for k in range(2):
                act.wait_ge(s["ssd_yready"], k + 1)
                act.wait_ge(s["z_ready"], 2)
                if k == 0:
                    high(UNIT_BASE["ssd_out"] + UNITS)
                squares("ssd", k, cmf[:, (8 + 4 * k) * T:(12 + 4 * k) * T])
            high(UNIT_BASE["ssd_out"] + 2 * UNITS + PARTS)
            for b in range(4):
                act.wait_ge(s["spread_used"], 4 + b + 1)
                out_high("ssd", 4 + b, tiles(8 + 2 * b, 2))
            high(UNIT_BASE["ssd_out"] + 4 * UNITS)

            if stop >= 1:
                square_sum(1, X_BEFORE["moe"])
                act.dma_start(cmf[:, 40 * T:44 * T], final_norm.rearrange("(a d) -> a d", a=1).to_broadcast([P, D]))\
                   .then_inc(s["fnorm_loaded"], 16)
                norm_copies(1, VCOL["norm_ffn"], False)
                for t in range(NT):
                    act.wait_ge(s["rt_arg"], t + 1)
                    link(af(r_eg[:, t, :], r_lg[:, t, 0:NG], ACT.Exp, bias=r_n[:, t, 0:1], accum_out=r_gs[:, t, :]))
                    af(r_ex[:, t, :], r_es[:, t, :], ACT.Exp, bias=r_n[:, t, 1:2]).then_inc(s["rt_exp"], 1)

                def act_quad(it, used, base):
                    act.wait_ge(used, base + STEPS_UP)
                    af(m_tanh, bank[0][:], ACT.Tanh, scale=0.5).then_inc(s["moe_tanh"], 1)
                    act.wait_ge(s["moe_gt"], it + 1)
                    af(m_gt, bank[7][:, 0:T], ACT.Copy).then_inc(s["moe_gtc"], 1)
                    act.wait_ge(s["moe_ht"], it + 1)
                    af(m_ht, bank[2][:], ACT.Copy, scale=0.5).then_inc(s["moe_htc"], 1)
                    act.wait_ge(used, base + MOE_STEPS)
                    af(m_y[:, 0, :], bank[3][:], ACT.Copy).then_inc(s["moe_ya"], 1)

                for name in ("moe_gtc", "moe_htc"):
                    act.sem_inc(s[name], 1)
                with act.Fori(0, NQ) as q:
                    act_quad(q, s["ring_used"], q * MOE_STEPS)
                act.wait_ge(s["rt_passes"], 1)
                passes = act.value_load(count_i[0:1, 0:1], min_val=1, max_val=T // CAP)
                with act.If(passes > 1):
                    with act.Fori(1, passes) as p:
                        with act.Fori(0, NQ) as q:
                            act_quad(p * NQ + q, ov_used, (p - 1) * (NQ * MOE_STEPS) + q * MOE_STEPS)
                act.wait_ge(s["moe_done"], 1)
                for t in range(NT):
                    af(hn[:, t, :], x_res[:, t, :], ACT.Square, accum_out=ss[:, t:t + 1]).then_inc(s["ss_ready"], 1)

            def fox(occ, li, name):
                u = NORMS.index(name)
                layer_start(name)
                norm_copies(u, VCOL["norm_w"] + 8 * (0 if occ == 0 else 3))
                softplus_row(SOFT_USE[name], rows[:, 1, :], rows[:, 2, :], 8)
                for b in range(8):
                    copy_bank(name, b, cmf[:, 2 * b * T:(2 * b + 2) * T])
                    if b % 2:
                        own_copies(name, b + 1)
                        squares(name, b // 2, cmf[:, (2 * b - 2) * T:(2 * b + 2) * T])
                for b in range(4):
                    copy_bank(name, 8 + b, vtm[:, b % 2, (b // 2) * BLK:(b // 2 + 1) * BLK])
                for b in range(4):
                    copy_bank(name, 12 + b, cmf[:, (16 + 2 * b) * T:(18 + 2 * b) * T], 0.5)
                own_copies(name, 16)
                silu_z(li, 16, ROWN[name][1] // 4 + 4)
                for h in range(FOX_H):
                    k = occ * FOX_H + h
                    act.wait_ge(s["fox_l"], k + 1)
                    for t, (a, b) in enumerate(((0, P), (P, 3 * P))):
                        i = af(f_p[h % 2][:, a:b], f_l[h % 2][:, a:b], ACT.Exp, bias=f_n[:, h % 2, t:t + 1],
                               accum_out=f_s[:, h % 2, t:t + 1])
                    i.then_inc(s["fox_e"], 1)
                    act.wait_ge(s["fox_t"], k + 1)
                    af(f_pt[h % 2], bank[2 + h % 2][:, 0:3 * P], ACT.Copy).then_inc(s["fox_tc"], 1)
                    if h >= 2 and h % 2 == 0:
                        act.wait_ge(s["fox_oc"], k)
                        out_high(name, h // 2 - 1, tiles(14 + h, 2))
                act.wait_ge(s["fox_oc"], (occ + 1) * FOX_H)
                out_high(name, 3, tiles(22, 2))
                high(UNIT_BASE[name + "_out"] + 2 * UNITS)

            def gla():
                layer_start("gla")
                norm_copies(NORMS.index("gla"), VCOL["norm_w"] + 8)
                for b in range(4):
                    copy_bank("gla", b, cmf[:, 2 * b * T:(2 * b + 2) * T])
                for b in range(4):
                    copy_bank("gla", 4 + b, vtm[:, b % 2, (b // 2) * BLK:(b // 2 + 1) * BLK])
                for b in range(4):
                    copy_bank("gla", 8 + b, cmf[:, (8 + 2 * b) * T:(10 + 2 * b) * T], 0.5)
                own_copies("gla", 12)
                silu_z(2, 8, ROWN["fox0"][1] // 4 + 4)
                act.wait_ge(s["gla_arg"], 1)
                link(af(tf(20, 4), tf(20, 4), ACT.Exp, scale=-1.0))
                af(tf(20, 4), tf(20, 4), ACT.Ln, bias=1.0).then_inc(s["gla_ln"], 1)
                act.wait_ge(s["gla_dec"], 1)
                af(tf(20, 4), tf(16, 4), ACT.Exp, scale=1.0 / 16)
                af(tf(24, 4), tf(16, 4), ACT.Exp, scale=-1.0 / 16)
                af(tf(28, 4), tf(28, 4), ACT.Exp, scale=1.0 / 16).then_inc(s["gla_exp"], 1)
                act.wait_ge(s["gla_kt"], 1)
                for k in (0, 1):
                    i = af(tf(40 + 2 * k, 2), bank[2 + k][:], ACT.Copy)
                i.then_inc(s["gla_ktc"], 1)
                act.wait_ge(s["z_ready"], 6)
                for k in range(2):
                    act.wait_ge(s["gla_oc"], 2 * k + 2)
                    squares("gla", k, tf(32 + 4 * k, 4))
                for b in range(4):
                    act.wait_ge(s["spread_used"], ROWN["gla"][1] // 2 + b + 1)
                    out_high("gla", b, tiles(8 + 2 * b, 2))
                high(UNIT_BASE["gla_out"] + 2 * UNITS)

            def gdn():
                layer_start("gdn")
                norm_copies(NORMS.index("gdn"), VCOL["norm_w"] + 16)
                softplus_row(SOFT_USE["gdn"], rows[:, 1, :], rows[:, 2, :], 8)
                act.wait_ge(s["gdn_row_free"], 1)
                af(rows[0:8, 0], bank[5][0:8, T:2 * T], ACT.Exp, scale=-1.0).then_inc(s["gdn_beta_exp"], 1)
                for b in range(12):
                    copy_bank("gdn", b, tf(2 * b, 2), 0.5 if b >= 8 else 1.0)
                    if b in (4, 6, 8, 10):
                        k = (b - 4) // 2
                        act.wait_ge(s["lin_ready"], 3 + k + 1)
                        af(vtm[:, 1, :], vtm[:, 0, :], ACT.Tanh).then_inc(s["tanh_ready"], 1)
                        if 1 <= k <= 2:
                            act.wait_ge(s["gdn_conv_done"], k)
                            squares("gdn_qk", k - 1, tf(4 * (k - 1), 4))
                own_copies("gdn", 12)
                silu_z(3, 16, ROWN["gdn_qk"][1] // 4 + 2)
                act.wait_ge(s["gdn_col_arg"], 1)
                af(tok[:, 4:6, 0:8], tok[:, 4:6, 0:8], ACT.Exp).then_inc(s["gdn_col_exp"], 1)
                for i in range(4):
                    act.wait_ge(s["gdn_arg"], i + 1)
                    if i >= 2:
                        af(g_qd[i - 2], bank[0][:], ACT.Exp)
                    af(g_dt, g_dt, ACT.Exp)
                    af(g_d, g_d, ACT.Exp, scale=-1.0).then_inc(s["gdn_exp"], 1)
                    act.wait_ge(s["gdn_turned"], i + 1)
                    af(g_Q, bank[5][:], ACT.Copy).then_inc(s["gdn_q_ready"], 1)
                    for j in range(6):
                        act.wait_ge(s["gdn_power"], 6 * i + j + 1)
                        if j == 0:
                            act.wait_ge(s["gdn_r_ready"], 7 * i + 1)
                        af(g_Q, bank[6][:], ACT.Copy).then_inc(s["gdn_q_ready"], 1)
                    act.wait_ge(s["gdn_uw"], i + 1)
                    af(g_u[i], bank[2][:], ACT.Copy).then_inc(s["gdn_u_ready"], 1)
                act.wait_ge(s["z_ready"], 8)
                for k in range(2):
                    act.wait_ge(s["gdn_oc"], 2 * k + 2)
                    squares("gdn_o", k, tf(4 * k, 4))
                for b in range(4):
                    act.wait_ge(s["spread_used"], ROWN["gdn_o"][1] // 2 + b + 1)
                    out_high("gdn", b, tiles(16 + 2 * b, 2))
                high(UNIT_BASE["gdn_out"] + 2 * UNITS)

            if stop >= 2:
                fox(0, 1, "fox0")
            if stop >= 3:
                gla()
            if stop >= 4:
                gdn()
            if stop >= 5:
                fox(1, 4, "fox1")

        @block.vector
        def _(dve):
            v = nc.vector
            n_link = [0]

            def link(ins):
                n_link[0] += 1
                ins.then_inc(s["dve_chain"], 1)
                dve.wait_ge(s["dve_chain"], n_link[0])

            def inverse_root(dst, x, t, done=None):
                link(v.tensor_scalar(dst.bitcast(I32), x.bitcast(I32), -0.5, RSQRT_SEED, ALU.mult, ALU.add))
                for k in range(3):
                    link(v.tensor_tensor(t, dst, dst, ALU.mult))
                    link(v.scalar_tensor_tensor(out=t, in0=t, scalar=-0.5, in1=x, op0=ALU.mult, op1=ALU.mult))
                    i = v.scalar_tensor_tensor(out=dst, in0=t, scalar=1.5, in1=dst, op0=ALU.add, op1=ALU.mult)
                    if k == 2 and done is not None:
                        i.then_inc(done[0], 1)
                        dve.wait_ge(done[0], done[1])
                    else:
                        link(i)

            def token_scale(which):
                dve.wait_ge(s["ss_ready"], NT * (which + 1))
                link(v.tensor_scalar(ss[:, 2:4], ss[:, 0:2], 1.0 / D, EPS, ALU.mult, ALU.add))
                inverse_root(ss[:, 4:6], ss[:, 2:4], ss[:, 6:8])

            def out_low(name, pair, src, n=1):
                k = 2 * (pair % 4)
                dve.wait_ge(s["out_high"], PAIR_BASE[name] + pair + n)
                v.tensor_tensor(hnT_l[:, k:k + 2 * n, :], src, hnT_h[:, k:k + 2 * n, :].bitcast(F32),
                                ALU.subtract).then_inc(s["out_low"], n)

            def norm(name, col):
                u = NORMS.index(name)
                token_scale(SQS.index(name))
                for t in range(NT):
                    v.tensor_scalar(hn[:, t, :], x_res[:, t, :], ss[:, 4 + t:5 + t], None,
                                    ALU.mult).then_inc(s["xn_ready"], 1)
                for b in (1, 3):
                    dve.wait_ge(s["turned"], 4 * u + b + 1)
                    for j in (0, 1):
                        i = v.tensor_scalar(hnT[:, 2 * b + j, :], b2(7)[:, j, :],
                                            vec[:, col + 2 * b + j:col + 2 * b + j + 1], None, ALU.mult)
                    i.then_inc(s["hnT_dve"], 1)
                    if name == "moe":
                        continue
                    w = SPLIT_NORMS.index(name)
                    dve.wait_ge(s["hnT_dve"], 2 * u + b // 2 + 1)
                    v.tensor_copy(hnT_h[:, 2 * b:2 * b + 2, :], hnT[:, 2 * b:2 * b + 2, :]).then_inc(s["hnT_own"], 1)
                    dve.wait_ge(s["hnT_own"], 2 * w + b // 2 + 1)
                    dve.wait_ge(s["hnT_high"], 2 * w + b // 2 + 1)
                    c = slice(2 * b - 2, 2 * b + 2)
                    v.tensor_tensor(hnT_l[:, c, :], hnT[:, c, :], hnT_h[:, c, :].bitcast(F32),
                                    ALU.subtract).then_inc(s["hnT_split"], 1)

            def rownorm(name, R, scale, use, split=None):
                r, before, n = ROWN[name]
                dve.wait_ge(s["sq_summed"], (before + n) // 4)
                link(v.tensor_scalar(rrow[0:R, 0], bank[SUM_BANK][0:R, 0:T], scale, EPS, ALU.mult, ALU.add))
                inverse_root(rrow[0:R, 1], rrow[0:R, 0], rrow[0:R, 2], (s["rownorm_ready"], r + 1))
                for b in range(n // 2):
                    g = before // 2 + b
                    dve.wait_ge(s["spread_done"], g + 1)
                    use(2 * b, b2(6 + g % 2)[:, 0, :])
                    use(2 * b + 1, b2(6 + g % 2)[:, 1, :]).then_inc(s["spread_used"], 1)
                    if split and b:
                        out_low(split[0], split[1] + b - 1, tiles(split[2] + 2 * b - 2, 2))
                if split:
                    out_low(split[0], split[1] + n // 2 - 1, tiles(split[2] + n - 2, 2))
                dve.wait_ge(s["spread_used"], (before + n) // 2)

            def add_projection(li):
                done = UNIT_BASE[LAYERS[li] + "_out"] + 2 * UNITS * (OUT_GROUPS[LAYERS[li]] - 1)
                for k in range(4):
                    n, t = k // 2, k % 2
                    dve.wait_ge(s["unit_done"], done + UNITS * (n + 1))
                    dst = x_res[:, t, n * BLK:(n + 1) * BLK]
                    v.tensor_tensor(dst, bank[t + 2 * n][:], dst, ALU.add).then_inc(s["x_ready"], 1)

            def silu_z(li, z0):
                for b in (0, 1):
                    dve.wait_ge(s["z_tanh"], 2 * li + b + 1)
                    z = tf(z0 + 4 * b, 4)
                    v.scalar_tensor_tensor(out=z, in0=sq[:, b].rearrange("p a b -> p (a b)"), scalar=1.0, in1=z,
                                           op0=ALU.add, op1=ALU.mult).then_inc(s["z_ready"], 1)
                dve.wait_ge(s["z_ready"], 2 * li + 2)

            def conv(src, dst, weights, stride, taps, bias=None):
                n = len(src)
                for d in range(taps):
                    tap = taps - 1 - d
                    for i in range(n):
                        w = vec[:, weights + stride * tap + i:weights + stride * tap + i + 1]
                        if d == 0 and bias is None:
                            x = v.tensor_scalar(dst[i], src[i], w, None, ALU.mult)
                        elif d == 0:
                            x = v.tensor_scalar(dst[i], src[i], w, vec[:, bias + i:bias + i + 1], ALU.mult, ALU.add)
                        else:
                            x = v.scalar_tensor_tensor(out=dst[i][:, d:T], in0=src[i][:, 0:T - d], scalar=w,
                                                       in1=dst[i][:, d:T], op0=ALU.mult, op1=ALU.add)
                    if d < taps - 1:
                        link(x)
                return x

            def conv_silu(k, t0, weights, stride, bias, done):
                lin = [vtm[:, 0, i * T:(i + 1) * T] for i in range(4)]
                conv([cm[:, t0 + i, :] for i in range(4)], lin, weights, stride, 4, bias).then_inc(s["lin_ready"], 1)
                dve.wait_ge(s["lin_ready"], k + 1)
                dve.wait_ge(s["tanh_ready"], k + 1)
                v.scalar_tensor_tensor(out=tf(t0, 4), in0=vtm[:, 1, :], scalar=1.0, in1=vtm[:, 0, :],
                                       op0=ALU.add, op1=ALU.mult).then_inc(done[0], 1)
                dve.wait_ge(*done)

            dve.wait_ge(s["vec_turned"], 2)
            v.tensor_copy(vec[:, 0:NA], bank[5][:, 0:NA])
            link(v.tensor_copy(vec[:, P:P + NB], bank[5][:, P:P + NB]))
            v.tensor_scalar(vec[:, 0:60], vec[:, 0:60], 0.5, None, ALU.mult)
            v.tensor_scalar(vec[:, P + 32:P + 96], vec[:, P + 32:P + 96], 0.5, None, ALU.mult).then_inc(s["vec_ready"], 1)
            dve.wait_ge(s["vec_ready"], 1)
            norm("ssd", VCOL["norm_mix"])
            dve.wait_ge(s["cols_ready"], 1)
            v.tensor_scalar(ncols[0:16, 0:1], ncols[0:16, 0:1], -1.0, None, ALU.mult)
            link(v.tensor_scalar(ncols[0:8, 1:2], ncols[0:8, 1:2], -1.0, None, ALU.mult))

            def softplus_args(k, R, src, bias, sign):
                link(v.tensor_scalar(rows[0:R, 0], src, bias, sign, ALU.add, ALU.mult))
                v.scalar_tensor_tensor(out=rows[0:R, 1], in0=rows[0:R, 0], scalar=-1.0, in1=rows[0:R, 0],
                                       op0=ALU.mult, op1=ALU.max).then_inc(s["row_arg"], 1)
                dve.wait_ge(s["row_ln"], k)

            def softplus_tail(R, dst):
                link(v.scalar_tensor_tensor(out=dst, in0=rows[0:R, 0], scalar=0.0, in1=rows[0:R, 2],
                                            op0=ALU.max, op1=ALU.add))

            dve.wait_ge(s["small_done"], 1)
            dve.wait_ge(s["consts_ready"], 1)
            softplus_args(1, 16, bank[5][0:16, 0:T], cols[0:16, 1:2], 1.0)
            softplus_tail(16, rows[0:16, 3])
            link(v.tensor_scalar(rows[0:16, 1], rows[0:16, 3], ncols[0:16, 0:1], None, ALU.mult))
            for c in range(NT):
                x = v.tensor_tensor_scan(rows[0:16, 2, c * P:(c + 1) * P], ones[0:16, :], rows[0:16, 1, c * P:(c + 1) * P],
                                         0.0, ALU.mult, ALU.add)
            x.then_inc(s["row_ready"], 1)
            dve.wait_ge(s["row_turned"], 1)
            v.tensor_copy(tok[:, 0:4, :], bank[5][:, T:T + 64].rearrange("p (a b) -> p a b", a=4)).then_inc(s["col_ready"], 1)
            dve.wait_ge(s["col_ready"], 1)

            for k in range(3):
                dve.wait_ge(s["proj_copied"], 2 * k + 2)
                conv_silu(k, 8 + 4 * k, VCOL["ssd_conv_w"] + 4 * k, 12, VCOL["ssd_conv_b"] + 4 * k,
                          (s["ssd_conv_done"], k + 1))
            for k in range(2):
                dve.wait_ge(s["proj_copied"], 10 + 2 * k + 2)
                link(v.tensor_tensor(tf(28 + 4 * k, 4), tf(28 + 4 * k, 4), tf(36 + 4 * k, 4), ALU.mult))
                dve.wait_ge(s["proj_copied"], 14 + 2 * k + 2)
                link(conv([cm[:, 28 + 4 * k + i, :] for i in range(4)], [cm[:, 36 + 4 * k + i, :] for i in range(4)],
                          VCOL["sc_conv_w"] + 4 * k, 8, 3))
                v.tensor_tensor(tf(36 + 4 * k, 4), tf(36 + 4 * k, 4), tf(20 + 4 * k, 4),
                                ALU.mult).then_inc(s["ssd_conv_done"], 1)
                dve.wait_ge(s["ssd_conv_done"], 3 + k + 1)

            def sc_out(i, spread):
                return v.scalar_tensor_tensor(out=cm[:, 36 + i, :], in0=spread, scalar=vec[:, VCOL["sc_norm"] + i:VCOL["sc_norm"] + i + 1],
                                              in1=cm[:, 36 + i, :], op0=ALU.mult, op1=ALU.mult)

            rownorm("sc", 16, 1.0 / 64, sc_out)
            silu_z(0, 0)
            out_low("ssd", 0, tiles(36, 8), 4)
            xdt = vtm
            for k in range(4):
                c, hf = k // 2, k % 2
                dve.wait_ge(s["ssd_xt_done"], k + 1)
                dst = xdt[:, c, hf * BLK:(hf + 1) * BLK].rearrange("p (h d) -> p h d", d=64)
                dtc = tok[:, 2 + c, 8 * hf:8 * hf + 8].unsqueeze(2).to_broadcast([P, 8, 64])
                v.tensor_tensor(dst, bank[k % 2][:].rearrange("p (h d) -> p h d", d=64), dtc,
                                ALU.mult).then_inc(s["ssd_xt_used"], 1)
            dve.wait_ge(s["ssd_xt_used"], 4)
            dve.wait_ge(s["ssd_g_done"], 1)
            v.tensor_tensor(tok[:, 4, :], bank[3][:, 2 * P:2 * P + 16], tok[:, 0, :], ALU.subtract).then_inc(s["ssd_dte_arg"], 1)
            v.tensor_copy(tiles(30, 1, P)[:, :, :], b4(3)[:, 0:2, :])
            for j in range(4):
                x = v.tensor_tensor(tf(28, 2)[:, j * P:(j + 1) * P], b4(2)[:, j, :], upper[:], ALU.mult)
            link(x)
            dve.wait_ge(s["ssd_dte"], 1)
            v.tensor_tensor(hn[:, 0, :].rearrange("p (h d) -> p h d", d=64), xdt[:, 0, :].rearrange("p (h d) -> p h d", d=64),
                            tok[:, 4, :].unsqueeze(2).to_broadcast([P, 16, 64]), ALU.mult).then_inc(s["ssd_xdte"], 1)
            dve.wait_ge(s["ssd_state"], 1)
            for g in range(2):
                x = v.tensor_copy(hn[:, 1, g * BLK:(g + 1) * BLK], bank[g + 6][:])
            x.then_inc(s["ssd_state_used"], 1)
            for i in range(8):
                c, hq = i // 4, i % 4
                g = hq // 2
                m = hnTf[:, (i % 2) * 512:(i % 2) * 512 + 512]
                dve.wait_ge(s["ssd_bc"], i + 1)
                if i >= 2:
                    dve.wait_ge(s["ssd_y"], i - 1)
                for j in range(4):
                    h = 4 * hq + j
                    x = v.tensor_scalar(m[:, j * P:(j + 1) * P], b4(i % 2)[:, j, :], tok[:, c, h:h + 1], 0.0,
                                        ALU.subtract, ALU.min)
                x.then_inc(s["ssd_seg"], 1)
                dve.wait_ge(s["ssd_exp"], i + 1)
                m4 = m.rearrange("p (a b) -> p a b", b=P)
                gm = tf(28, 2)[:, (2 * c + g) * P:(2 * c + g + 1) * P].unsqueeze(1).to_broadcast([P, 4, P])
                if c == 1:
                    ce = hnTf[:, 1024 + (i % 2) * 512:1536 + (i % 2) * 512].rearrange("p (a b) -> p a b", b=P)
                    v.tensor_tensor(ce, ce, cm[:, 18 + g, P:T].unsqueeze(1).to_broadcast([P, 4, P]), ALU.mult)
                v.tensor_tensor(m4, m4, gm, ALU.mult).then_inc(s["ssd_m"], 1)
            for k in range(2):
                dve.wait_ge(s["ssd_y"], 4 + 2 * k + 2)
                for i in range(4 * k, 4 * k + 4):
                    x = v.scalar_tensor_tensor(out=cm[:, 8 + i, :], in0=cm[:, 8 + i, :], scalar=dsk[:, i:i + 1],
                                               in1=b2(2 + i // 2)[:, i % 2, :], op0=ALU.mult, op1=ALU.add)
                link(x)
                v.tensor_tensor(tf(8 + 4 * k, 4), tf(8 + 4 * k, 4), tf(4 * k, 4), ALU.mult).then_inc(s["ssd_yready"], 1)
                dve.wait_ge(s["ssd_yready"], k + 1)

            def ssd_out(i, spread):
                return v.scalar_tensor_tensor(out=cm[:, 8 + i, :], in0=spread, scalar=vec[:, VCOL["ssd_norm"] + i:VCOL["ssd_norm"] + i + 1],
                                              in1=cm[:, 8 + i, :], op0=ALU.mult, op1=ALU.mult)

            rownorm("ssd", 2, 1.0 / BLK, ssd_out, ("ssd", 4, 8))
            add_projection(0)

            if stop >= 1:
                norm("moe", VCOL["norm_ffn"])
                dve.wait_ge(s["rt_done"], 1)
                link(v.tensor_copy(r_lg, bank[5][:, 0:NT * (NG + NE)].rearrange("p (a b) -> p a b", a=NT)))

                def rank(x, n, limit, dst):
                    c1 = r_c1[:, 0:n * n // 2, :].rearrange("p a b -> p (a b)").rearrange("p (i j) -> p i j", i=n)
                    c2 = r_c2[:, 0:n * n // 2, :].rearrange("p a b -> p (a b)").rearrange("p (i j) -> p i j", i=n)
                    other = x.unsqueeze(1).to_broadcast([P, n, n])
                    own = x.unsqueeze(2).to_broadcast([P, n, n])
                    v.tensor_tensor(c1, other, own, ALU.is_gt)
                    link(v.tensor_tensor(c2, other, own, ALU.is_equal))
                    link(v.tensor_tensor(c2, c2, earlier[:, 0:n, 0:n], ALU.mult))
                    link(v.tensor_tensor(c1, c1, c2, ALU.add))
                    link(v.tensor_reduce(dst, c1, AX.X, ALU.add))
                    link(v.tensor_scalar(dst, dst, limit - 0.5, None, ALU.is_lt))

                for t in range(NT):
                    gl, el = r_lg[:, t, 0:NG], r_lg[:, t, NG:NG + NE].rearrange("p (g e) -> p g e", g=NG)
                    rank(gl, NG, 1, r_gsel[:, t, :])
                    v.tensor_reduce(r_n[:, t, 0:1], gl, AX.X, ALU.max, negate=True)
                    link(v.tensor_tensor(r_prod, el, r_gsel[:, t, :].unsqueeze(2).to_broadcast([P, NG, EPG]), ALU.mult))
                    link(v.tensor_reduce(r_es[:, t, :], r_prod.rearrange("p g e -> p e g"), AX.X, ALU.add))
                    v.tensor_reduce(r_n[:, t, 1:2], r_es[:, t, :], AX.X, ALU.max, negate=True).then_inc(s["rt_arg"], 1)
                    rank(r_es[:, t, :], EPG, 2, r_sel[:, t, :])
                v.memset(r_gate, 0.0)
                link(v.memset(r_pm, -1.0))
                for t in range(NT):
                    dve.wait_ge(s["rt_exp"], t + 1)
                    link(v.tensor_tensor(r_ex[:, t, :], r_ex[:, t, :], r_sel[:, t, :], ALU.mult))
                    link(v.tensor_reduce(r_sum[:, t, 0:1], r_ex[:, t, :], AX.X, ALU.add))
                    link(v.tensor_tensor(r_sum[:, t, 1:2], r_sum[:, t, 0:1], r_gs[:, t, :], ALU.mult))
                    link(v.reciprocal(r_sum[:, t, 2:3], r_sum[:, t, 1:2]))
                    link(v.tensor_scalar(r_ex[:, t, :], r_ex[:, t, :], r_sum[:, t, 2:3], None, ALU.mult))
                    gs = r_gsel[:, t, :].unsqueeze(2).to_broadcast([P, NG, EPG])
                    v.tensor_tensor(r_gate[:, t, 0:NE].rearrange("p (g e) -> p g e", g=NG),
                                    r_ex[:, t, :].unsqueeze(1).to_broadcast([P, NG, EPG]), gs, ALU.mult)
                    v.tensor_tensor(r_mask[:, t, :].rearrange("p (g e) -> p g e", g=NG),
                                    r_sel[:, t, :].unsqueeze(1).to_broadcast([P, NG, EPG]), gs,
                                    ALU.mult).then_inc(s["rt_mask"], 1)
                dve.wait_ge(s["rt_mask"], 2)
                dve.wait_ge(s["rt_rank"], 1)
                for t in range(NT):
                    pm = r_pm[:, t, 0:NE]
                    link(v.scalar_tensor_tensor(out=pm, in0=bank[5][:, P + t * NE:P + (t + 1) * NE], scalar=1.0,
                                                in1=r_mask[:, t, :], op0=ALU.add, op1=ALU.mult))
                    link(v.tensor_scalar(pm, pm, -1.0, None, ALU.add))
                link(v.tensor_reduce(r_pass[0:1, 0, 0:1], bank[5][0:1, T:T + NE], AX.X, ALU.max))
                link(v.tensor_scalar(r_pass[0:1, 1, 0:8], iota[0:1, 0:8], float(CAP), r_pass[0:1, 0, 0:1], ALU.mult, ALU.is_lt))
                link(v.tensor_reduce(r_pass[0:1, 0, 1:2], r_pass[0:1, 1, 0:8], AX.X, ALU.add))
                v.tensor_copy(count_i[0:1, 0:1], r_pass[0:1, 0, 1:2]).then_inc(s["rt_passes"], 1)

                iota4 = iota[:].unsqueeze(1).to_broadcast([P, QUAD, CAP])

                def select_tokens(q):
                    for t in range(NT):
                        place = r_pm[:, t, bass.ds(q * QUAD, QUAD)].unsqueeze(2).to_broadcast([P, QUAD, CAP])
                        x = v.tensor_tensor(m_S[:, t, :].rearrange("p (e c) -> p e c", e=QUAD), iota4, place, ALU.is_equal)
                    x.then_inc(s["moe_sel"], 1)

                def gathered(g):
                    dve.wait_ge(s["moe_gath"], g + 1)
                    for half in (0, 1):
                        gain = vec[:, VCOL["norm_ffn"] + 4 * half:VCOL["norm_ffn"] + 4 * half + 4]
                        x = v.tensor_tensor(m_xg[:, 4 * half:4 * half + 4, :], b4(5 + half)[:],
                                            gain.unsqueeze(2).to_broadcast([P, 4, P]), ALU.mult)
                    x.then_inc(s["moe_xg"], 1)

                def dve_quad(q, it, g):
                    dve.wait_ge(s["moe_sel"], g + 1)
                    for t in range(NT):
                        gate = r_gate[:, t, bass.ds(q * QUAD, QUAD)].unsqueeze(2).to_broadcast([P, QUAD, CAP])
                        x = v.tensor_tensor(m_SG[:, t, :].rearrange("p (e c) -> p e c", e=QUAD),
                                            m_S[:, t, :].rearrange("p (e c) -> p e c", e=QUAD), gate, ALU.mult)
                    x.then_inc(s["moe_sg"], 1)
                    dve.wait_ge(s["moe_sg"], it + 1)
                    select_tokens(q + 1)
                    dve.wait_ge(s["moe_tanh"], it + 1)
                    v.scalar_tensor_tensor(out=m_silu, in0=m_tanh, scalar=1.0, in1=bank[0][:], op0=ALU.add,
                                           op1=ALU.mult).then_inc(s["moe_chain"], 1)
                    dve.wait_ge(s["moe_chain"], it + 1)
                    v.tensor_tensor(m_h, m_silu, bank[1][:], ALU.mult).then_inc(s["moe_h"], 1)
                    gathered(g + 1)
                    return

                def dve_quad_end(it, used, base):
                    dve.wait_ge(used, base + MOE_STEPS)
                    v.tensor_copy(m_y[:, 1, :], bank[4][:]).then_inc(s["moe_yd"], 1)
                    dve.wait_ge(s["moe_scat"], it + 1)
                    for k in range(4):
                        t, n = k // 2, k % 2
                        dst = x_res[:, t, n * BLK:(n + 1) * BLK]
                        x = v.tensor_tensor(dst, bank[[5, 6, 3, 4][k]][:], dst, ALU.add)
                    x.then_inc(s["moe_acc"], 1)

                dve.sem_inc(s["moe_h"], 1)
                dve.sem_inc(s["moe_acc"], 1)
                dve.wait_ge(s["rt_passes"], 1)
                select_tokens(0)
                gathered(0)
                with dve.Fori(0, NQ) as q:
                    dve_quad(q, q, q)
                    dve_quad_end(q, s["ring_used"], q * MOE_STEPS)
                passes = dve.value_load(count_i[0:1, 0:1], min_val=1, max_val=T // CAP)
                with dve.If(passes > 1):
                    with dve.Fori(1, passes) as p:
                        for t in range(NT):
                            x = v.tensor_scalar(r_pm[:, t, :], r_pm[:, t, :], -float(CAP), None, ALU.add)
                        x.then_inc(s["pass_chain"], 1)
                        dve.wait_ge(s["pass_chain"], p)
                        select_tokens(0)
                        gathered(p * (NQ + 1))
                        with dve.Fori(0, NQ) as q:
                            dve_quad(q, p * NQ + q, p * (NQ + 1) + q)
                            dve_quad_end(p * NQ + q, ov_used, (p - 1) * (NQ * MOE_STEPS) + q * MOE_STEPS)
                v.drain().then_inc(s["moe_done"], 1)
                token_scale(2)
                dve.wait_ge(s["fnorm_loaded"], 16)
                for t in range(NT):
                    v.scalar_tensor_tensor(out=x_res[:, t, :], in0=x_res[:, t, :], scalar=ss[:, 4 + t:5 + t],
                                           in1=tf(40, 4), op0=ALU.mult, op1=ALU.mult).then_inc(s["x_ready"], 1)
                dve.wait_ge(s["x_ready"], X_BEFORE["fox0"])

            def fox(occ, li, name):
                norm(name, VCOL["norm_w"] + 8 * (0 if occ == 0 else 3))
                dve.wait_ge(s["small_done"], li + 1)
                softplus_args(SOFT_USE[name], FOX_H, bank[5][0:FOX_H, 0:T], cols[0:FOX_H, 2 + occ:3 + occ], -1.0)
                softplus_tail(FOX_H, rows[0:FOX_H, 1])
                link(v.tensor_tensor_scan(rows[0:FOX_H, 3], ones[0:FOX_H, 0:1].to_broadcast([FOX_H, T]), rows[0:FOX_H, 1], 0.0, ALU.mult, ALU.subtract))
                v.tensor_scalar(rows[0:FOX_H, 2], rows[0:FOX_H, 3], -1.0, None, ALU.mult).then_inc(s["row_ready"], 1)
                dve.wait_ge(s["row_turned"], ROW_USE[name])
                link(v.tensor_copy(tok[:, 5:7, 0:FOX_H], bank[5][:, T:T + 16].rearrange("p (a b) -> p a b", a=2)))

                def qk_out(i, spread):
                    gain = VCOL["fox_q_gain"] + occ if i < 8 else VCOL["fox_k_gain"] + occ
                    if i < 8:
                        return v.scalar_tensor_tensor(out=cm[:, i, :], in0=spread, scalar=qgain[:, 0:1], in1=cm[:, i, :],
                                                      op0=ALU.mult, op1=ALU.mult)
                    return v.scalar_tensor_tensor(out=cm[:, i, :], in0=spread, scalar=vec[:, gain:gain + 1], in1=cm[:, i, :],
                                                  op0=ALU.mult, op1=ALU.mult)

                qcol = VCOL["fox_q_gain"] + occ
                link(v.tensor_scalar(qgain[:, 0:1], vec[:, qcol:qcol + 1], float(P) ** -0.5, None, ALU.mult))
                rownorm(name, 16, 1.0 / P, qk_out)
                dve.sem_inc(s["qk_ready"], 1)
                silu_z(li, 16)
                for h in range(FOX_H + 1):
                    k = occ * FOX_H + h
                    if h < FOX_H:
                        dve.wait_ge(s["fox_s"], k + 1)
                        v.scalar_tensor_tensor(out=f_l[h % 2][:, 0:P], in0=bank[h % 2][:, 0:P], scalar=tok[:, 5, h:h + 1],
                                               in1=negmask[:, 1, :], op0=ALU.add, op1=ALU.add)
                        link(v.scalar_tensor_tensor(out=f_l[h % 2][:, P:3 * P], in0=bank[h % 2][:, P:3 * P],
                                                    scalar=tok[:, 6, h:h + 1], in1=negmask[:].rearrange("p a b -> p (a b)"),
                                                    op0=ALU.add, op1=ALU.add))
                        v.tensor_reduce(f_n[:, h % 2, 0:1], f_l[h % 2][:, 0:P], AX.X, ALU.max, negate=True)
                        v.tensor_reduce(f_n[:, h % 2, 1:2], f_l[h % 2][:, P:3 * P], AX.X, ALU.max,
                                        negate=True).then_inc(s["fox_l"], 1)
                        dve.wait_ge(s["fox_e"], k + 1)
                        link(v.reciprocal(f_r[:, h % 2, :], f_s[:, h % 2, :]))
                        v.tensor_scalar(f_p[h % 2][:, 0:P], f_p[h % 2][:, 0:P], f_r[:, h % 2, 0:1], None, ALU.mult)
                        v.tensor_scalar(f_p[h % 2][:, P:3 * P], f_p[h % 2][:, P:3 * P], f_r[:, h % 2, 1:2], None,
                                        ALU.mult).then_inc(s["fox_p"], 1)
                    if h >= 1:
                        dve.wait_ge(s["fox_o"], k)
                        z = cm[:, 16 + h - 1, :]
                        v.tensor_tensor(z, bank[6 + (h - 1) % 2][:, 0:T], z, ALU.mult).then_inc(s["fox_oc"], 1)
                    if h >= 3 and h % 2:
                        out_low(name, (h - 3) // 2, tiles(13 + h, 2))
                out_low(name, 3, tiles(22, 2))
                add_projection(li)

            def ones_free(R, n):
                return ones[0:R, 0:1].to_broadcast([R, n])

            def gla():
                norm("gla", VCOL["norm_w"] + 8)
                dve.wait_ge(s["small_done"], 3)
                v.tensor_copy(rows[0:16, 0], bank[5][0:16, 0:T]).then_inc(s["gla_low"], 1)
                dve.wait_ge(s["gla_gate"], 1)
                for h in range(GLA_H):
                    x = v.tensor_scalar(cm[:, 16 + h, :], b2(4 + h // 2)[:, h % 2, :],
                                        vec[:, VCOL["gla_b_gate"] + h:VCOL["gla_b_gate"] + h + 1], -1.0, ALU.add, ALU.mult)
                link(x)
                v.scalar_tensor_tensor(out=tf(20, 4), in0=tf(16, 4), scalar=-1.0, in1=tf(16, 4), op0=ALU.mult,
                                       op1=ALU.max).then_inc(s["gla_arg"], 1)
                dve.wait_ge(s["gla_ln"], 1)
                link(v.scalar_tensor_tensor(out=tf(20, 4), in0=tf(16, 4), scalar=0.0, in1=tf(20, 4), op0=ALU.max,
                                            op1=ALU.add))
                for k in range(GLA_H * T // GLA_CH):
                    x = v.tensor_tensor_scan(tf(16, 4)[:, k * 64:(k + 1) * 64], ones[:, 0:64], tf(20, 4)[:, k * 64:(k + 1) * 64],
                                             0.0, ALU.mult, ALU.subtract)
                link(x)
                cum = tiles(16, 4, 64)
                v.tensor_tensor(tiles(28, 4, 64), cum[:, :, 63:64].to_broadcast([P, 16, 64]), cum,
                                ALU.subtract).then_inc(s["gla_dec"], 1)
                silu_z(2, 8)
                dve.wait_ge(s["gla_exp"], 1)
                dve.wait_ge(s["proj_copied"], PROJ_BASE["gla"] + 4)
                v.scalar_tensor_tensor(out=tf(0, 4), in0=tf(0, 4), scalar=float(GLA_DK) ** -0.5, in1=tf(20, 4),
                                       op0=ALU.mult, op1=ALU.mult)
                link(v.tensor_tensor(tf(28, 4), tf(4, 4), tf(28, 4), ALU.mult))
                v.tensor_tensor(tf(4, 4), tf(4, 4), tf(24, 4), ALU.mult).then_inc(s["gla_qk"], 1)
                dve.wait_ge(s["gla_qk"], 1)
                dve.wait_ge(s["gla_at"], 1)
                for k in (0, 1):
                    x = v.tensor_tensor(tiles(24 + 2 * k, 2, P), b4(k), upper64[:].unsqueeze(1).to_broadcast([P, 4, P]),
                                        ALU.mult)
                x.then_inc(s["gla_atc"], 1)
                state = tiles(16, 4, GLA_DV)
                for c in range(3):
                    dve.wait_ge(s["gla_st"], c + 1)
                    if c:
                        dve.wait_ge(s["gla_stc"], c)
                    for h in range(GLA_H):
                        new = b2(2 * (c % 2) + h // 2)[:, h % 2, :]
                        if c == 0:
                            x = v.tensor_copy(state[:, h, :], new)
                        else:
                            a = h * T + c * 64 + 63
                            x = v.scalar_tensor_tensor(out=state[:, h, :], in0=state[:, h, :], scalar=tf(20, 4)[:, a:a + 1],
                                                       in1=new, op0=ALU.mult, op1=ALU.add)
                    x.then_inc(s["gla_stc"], 1)
                dve.wait_ge(s["gla_o"], 1)
                for h in range(GLA_H):
                    v.tensor_copy(tf(32 + 2 * h, 2), bank[4 + h][:]).then_inc(s["gla_oc"], 1)
                dve.wait_ge(s["gla_oc"], 4)
                link(v.tensor_tensor(tf(8, 8), tf(8, 8), tf(32, 8), ALU.mult))

                def out(i, spread):
                    gain = VCOL["gla_o_gain"] + i % 2
                    return v.scalar_tensor_tensor(out=cm[:, 8 + i, :], in0=spread, scalar=vec[:, gain:gain + 1],
                                                  in1=cm[:, 8 + i, :], op0=ALU.mult, op1=ALU.mult)

                rownorm("gla", GLA_H, 1.0 / GLA_DV, out, ("gla", 0, 8))
                add_projection(2)

            def gdn():
                norm("gdn", VCOL["norm_w"] + 16)
                dve.wait_ge(s["small_done"], 4)
                softplus_args(SOFT_USE["gdn"], 8, bank[5][0:8, 0:T], cols[0:8, 5:6], 1.0)
                softplus_tail(8, rows[0:8, 3])
                v.tensor_scalar(rows[0:8, 1], rows[0:8, 3], ncols[0:8, 1:2], None, ALU.mult).then_inc(s["gdn_row_free"], 1)
                dve.wait_ge(s["gdn_row_free"], 1)
                for c in range(NT):
                    x = v.tensor_tensor_scan(rows[0:8, 2, c * P:(c + 1) * P], ones[0:8, :], rows[0:8, 1, c * P:(c + 1) * P],
                                             0.0, ALU.mult, ALU.add)
                dve.wait_ge(s["gdn_beta_exp"], 1)
                link(v.tensor_scalar(rows[0:8, 0], rows[0:8, 0], 1.0, None, ALU.add))
                v.reciprocal(rows[0:8, 0], rows[0:8, 0]).then_inc(s["row_ready"], 1)
                dve.wait_ge(s["row_turned"], ROW_USE["gdn"])
                v.tensor_copy(tok[:, 0:4, 0:8], bank[5][:, T:T + 32].rearrange("p (a b) -> p a b", a=4)).then_inc(s["col_ready"], 1)
                dve.wait_ge(s["col_ready"], 2)
                v.tensor_scalar(tok[:, 6:8, 0:8], tok[:, 2:4, 0:8], -1.0, None, ALU.mult)
                v.tensor_copy(tok[:, 5, 0:8], tok[:, 1, 0:8])
                dve.wait_ge(s["gdn_last"], 1)
                v.tensor_tensor(tok[:, 4, 0:8], bank[5][:, T + 32:T + 40], tok[:, 0, 0:8],
                                ALU.subtract).then_inc(s["gdn_col_arg"], 1)
                for k in range(4):
                    dve.wait_ge(s["proj_copied"], PROJ_BASE["gdn"] + 2 * k + 2)
                    conv_silu(3 + k, 4 * k, VCOL["gdn_conv_w"] + 4 * k, 16, None, (s["gdn_conv_done"], k + 1))

                def qk_out(i, spread):
                    return v.scalar_tensor_tensor(out=cm[:, i, :], in0=spread, scalar=float(P) ** -0.5 if i < 4 else 1.0,
                                                  in1=cm[:, i, :], op0=ALU.mult, op1=ALU.mult)

                rownorm("gdn_qk", 8, 1.0, qk_out)
                dve.sem_inc(s["gdn_qk_ready"], 1)
                silu_z(3, 16)
                for k in range(4):
                    c, hf = k // 2, k % 2
                    dve.wait_ge(s["gdn_xt"], k + 1)
                    v.tensor_tensor(vtm[:, c, hf * BLK:(hf + 1) * BLK].rearrange("p (h d) -> p h d", h=4), b4(k % 2),
                                    tok[:, 2 + c, 4 * hf:4 * hf + 4].unsqueeze(2).to_broadcast([P, 4, P]),
                                    ALU.mult).then_inc(s["gdn_xtc"], 1)
                dve.wait_ge(s["gdn_xtc"], 4)
                dve.wait_ge(s["gdn_col_exp"], 1)
                link(v.tensor_tensor(tok[:, 5, 0:8], tok[:, 5, 0:8], tok[:, 3, 0:8], ALU.mult))
                dve.wait_ge(s["gdn_kt"], 1)
                for dst, b, col in ((g_kdec, 2, 4), (g_kbg, 3, 5)):
                    x = v.tensor_tensor(dst.rearrange("p (h r d) -> p h r d", h=4, r=2), b4(b).unsqueeze(2).to_broadcast([P, 4, 2, P]),
                                        tok[:, col, 0:8].rearrange("p (h r) -> p h r", r=2).unsqueeze(3).to_broadcast([P, 4, 2, P]),
                                        ALU.mult)
                x.then_inc(s["gdn_ktc"], 1)
                dve.wait_ge(s["gdn_ktc"], 1)
                for i in range(4):
                    c, hf = i // 2, i % 2
                    dve.wait_ge(s["gdn_bc"], i + 1)
                    for j in range(4):
                        h = 4 * hf + j
                        col = tok[:, c, h:h + 1]
                        v.tensor_scalar(g_dt[:, j * P:(j + 1) * P], b4(0)[:, j, :], col, 0.0, ALU.subtract, ALU.min)
                        x = v.tensor_scalar(g_d[:, j * P:(j + 1) * P], b4(0)[:, j, :], col, 0.0, ALU.subtract, ALU.max)
                    x.then_inc(s["gdn_arg"], 1)
                    v.tensor_tensor(g_km, b4(1)[:, 0:2, :], slower[:].unsqueeze(1).to_broadcast([P, 2, P]), ALU.mult)
                    link(v.tensor_tensor(g_qm, b4(1)[:, 2:4, :], upper[:].unsqueeze(1).to_broadcast([P, 2, P]), ALU.mult))
                    dve.wait_ge(s["gdn_exp"], i + 1)
                    for j in range(4):
                        h = 4 * hf + j
                        x = v.scalar_tensor_tensor(out=g_QT[:, j * P:(j + 1) * P], in0=g_km[:, j // 2, :],
                                                   scalar=tok[:, 6 + c, h:h + 1], in1=g_d[:, j * P:(j + 1) * P],
                                                   op0=ALU.mult, op1=ALU.mult)
                    x.then_inc(s["gdn_x"], 1)
                    v.tensor_tensor(g_qkk[i].rearrange("p (h r d) -> p h r d", h=2, r=2),
                                    g_dt.rearrange("p (h r d) -> p h r d", h=2, r=2),
                                    g_qm.unsqueeze(2).to_broadcast([P, 2, 2, P]), ALU.mult)
                    if c == 1:
                        v.tensor_tensor(g_qd[hf].rearrange("p (h r d) -> p h r d", h=2, r=2),
                                        g_qd[hf].rearrange("p (h r d) -> p h r d", h=2, r=2),
                                        cm[:, 2 * hf:2 * hf + 2, P:T].unsqueeze(2).to_broadcast([P, 2, 2, P]), ALU.mult)
                    dve.wait_ge(s["gdn_q_ready"], 7 * i + 1)
                    v.tensor_tensor(g_R.rearrange("p (h d) -> p h d", h=4), g_Q.rearrange("p (h d) -> p h d", h=4), ident[:].unsqueeze(1).to_broadcast([P, 4, P]),
                                    ALU.add).then_inc(s["gdn_r_ready"], 1)
                    for j in range(6):
                        dve.wait_ge(s["gdn_power"], 6 * i + j + 1)
                        v.tensor_copy(g_QT, bank[7][:]).then_inc(s["gdn_qt_ready"], 1)
                        dve.wait_ge(s["gdn_r"], 6 * i + j + 1)
                        dve.wait_ge(s["gdn_r_ready"], 7 * i + j + 1)
                        v.tensor_tensor(g_R, g_R, bank[4][:], ALU.add).then_inc(s["gdn_r_ready"], 1)
                    if c == 1:
                        dve.wait_ge(s["gdn_uw"], i + 1)
                        v.tensor_copy(g_w[hf], bank[3][:]).then_inc(s["gdn_w_ready"], 1)
                dve.wait_ge(s["gdn_s"], 1)
                for k in (0, 1):
                    x = v.tensor_copy(tf(40 + 2 * k, 2), bank[k][:])
                x.then_inc(s["gdn_s_ready"], 1)
                dve.wait_ge(s["gdn_ws"], 1)
                for k in (0, 1):
                    x = v.tensor_tensor(g_u[2 + k], g_u[2 + k], bank[2 + k][:], ALU.subtract)
                x.then_inc(s["gdn_new"], 1)
                dve.wait_ge(s["gdn_o"], 1)
                for k in range(4):
                    v.tensor_copy(tf(2 * k, 2), bank[4 + k][:]).then_inc(s["gdn_oc"], 1)
                dve.wait_ge(s["gdn_oc"], 4)
                link(v.tensor_tensor(tf(16, 8), tf(16, 8), tf(0, 8), ALU.mult))

                def out(i, spread):
                    gain = VCOL["gdn_o_gain"]
                    return v.scalar_tensor_tensor(out=cm[:, 16 + i, :], in0=spread, scalar=vec[:, gain:gain + 1],
                                                  in1=cm[:, 16 + i, :], op0=ALU.mult, op1=ALU.mult)

                rownorm("gdn_o", 8, 1.0 / P, out, ("gdn", 0, 16))
                add_projection(3)

            if stop >= 2:
                fox(0, 1, "fox0")
            if stop >= 3:
                gla()
            if stop >= 4:
                gdn()
            if stop >= 5:
                fox(1, 4, "fox1")

        @block.tensor
        def _(pe):
            mm, tr = nc.tensor.matmul, nc.tensor.transpose

            def norm(name):
                u = NORMS.index(name)
                pe.wait_ge(s["xn_ready"], NT * u + NT)
                for b in range(4):
                    if b == 2:
                        pe.wait_ge(s["hnT_act"], 2 * u + 1)
                    if b == 3:
                        pe.wait_ge(s["hnT_dve"], 2 * u + 1)
                    for j in (0, 1):
                        for t in range(NT):
                            k = 2 * b + j
                            x = tr(b2(6 + b % 2)[:, j, t * P:(t + 1) * P], hn[:, t, k * P:(k + 1) * P], ident[:])
                    x.then_inc(s["turned"], 1)

            def normed(name):
                u = NORMS.index(name)
                pe.wait_ge(s["hnT_act"], 2 * u + 2)
                pe.wait_ge(s["hnT_dve"], 2 * u + 2)

            def split_ready(name):
                pe.wait_ge(s["hnT_split"], 2 * SPLIT_NORMS.index(name) + 2)

            def small(dst, w, last=True):
                for k in range(KD):
                    x = mm(dst, w[:, k, :], hnT[:, k, :], start=(k == 0), stop=(k == KD - 1))
                if last:
                    x.then_inc(s["small_done"], 1)

            def products(dst, stationary, moving, start, stop):
                (sh, sl), (mh, ml) = stationary, moving
                mm(dst, sh, mh, start=start, stop=False)
                mm(dst, sh, ml, start=False, stop=False)
                return mm(dst, sl, mh, start=False, stop=stop)

            def project(name, first, end):
                for i in range(first, end):
                    kind = KINDS[name][i]
                    for m in range(UNITS):
                        u, g = UNIT_BASE[name] + UNITS * i + m, PROJ_BASE[name] + 2 * i
                        if m == 0 and g >= 4:
                            pe.wait_ge(s["proj_copied"], g - 3)
                        if m == (2 if kind == "channels" else 0) and g >= 4:
                            pe.wait_ge(s["proj_copied"], g - 2)
                        pe.wait_ge(s["low_ready"], u + 1)
                        if kind == "channels":
                            wh, wl = part(w_h, u, P), part(w_l, u, P)
                            for k in range(KD):
                                x = products(b2((g + m // 2) % 4)[:, m % 2, :], (wh[:, k, :], wl[:, k, :]),
                                             (hnT_h[:, k, :], hnT_l[:, k, :]), k == 0, k == KD - 1)
                        else:
                            wh, wl = part(w_h, u, BLK), part(w_l, u, BLK)
                            for t in range(NT):
                                for j in (0, 1):
                                    k, tt = 2 * m + j, slice(t * P, (t + 1) * P)
                                    x = products(bank[(g + t) % 4][:], (hnT_h[:, k, tt], hnT_l[:, k, tt]),
                                                 (wh[:, j, :], wl[:, j, :]), k == 0, k == KD - 1)
                        x.then_inc(s["unit_done"], 1)

            def sum_squares(name, R, pick, batches=None):
                _, before, n = ROWN[name]
                for i in range(n):
                    if batches is not None and i // 4 not in batches:
                        continue
                    g = (before + i) // 4
                    if i % 4 == 0:
                        pe.wait_ge(s["sq_ready"], g + 1)
                    x = mm(bank[SUM_BANK][0:R, 0:T], pick(i), sq[:, g % 2, i % 4, :], start=(i == 0), stop=(i == n - 1))
                    if i % 4 == 3:
                        x.then_inc(s["sq_summed"], 1)

            def spread(name, R, pick):
                r, before, n = ROWN[name]
                pe.wait_ge(s["rownorm_ready"], r + 1)
                for b in range(n // 2):
                    g = before // 2 + b
                    if g >= 2:
                        pe.wait_ge(s["spread_used"], g - 1)
                    for j in (0, 1):
                        picked = pick(2 * b + j)
                        m = P // len(picked)
                        for i, sel in enumerate(picked):
                            x = mm(b2(6 + g % 2)[m * i:m * i + m, j, :], sel, rrow[0:R, 1], start=True, stop=True)
                    x.then_inc(s["spread_done"], 1)

            def out_projection(name, groups=None):
                for g in (range(OUT_GROUPS[name]) if groups is None else groups):
                    for n in (0, 1):
                        if name == "ssd" and g == 0 and n == 1:
                            pe.wait_ge(s["ssd_yready"], 1)
                        for m in range(UNITS):
                            u = UNIT_BASE[name + "_out"] + UNITS * (2 * g + n) + m
                            if n == 0:
                                pe.wait_ge(s["out_low"], PAIR_BASE[name] + 4 * g + m + 1)
                            pe.wait_ge(s["low_ready"], u + 1)
                            wh, wl = part(w_h, u, BLK), part(w_l, u, BLK)
                            for t in range(NT):
                                for j in (0, 1):
                                    k, tt = 2 * m + j, slice(t * P, (t + 1) * P)
                                    x = products(bank[t + 2 * n][:], (hnT_h[:, k, tt], hnT_l[:, k, tt]),
                                                 (wh[:, j, :], wl[:, j, :]), g == 0 and k == 0,
                                                 g == OUT_GROUPS[name] - 1 and k == KD - 1)
                            x.then_inc(s["unit_done"], 1)

            pe.wait_ge(s["ident_ready"], 1)
            pe.wait_ge(s["vec_loaded"], 16 * (len(VEC_A) + len(VEC_B)))
            tr(bank[5][:, 0:NA], cm[0:NA, 0, 0:P], ident[0:NA, 0:NA]).then_inc(s["vec_turned"], 1)
            tr(bank[5][:, P:P + NB], cm[0:NB, 1, 0:P], ident[0:NB, 0:NB]).then_inc(s["vec_turned"], 1)
            norm("ssd")
            pe.wait_ge(s["small_loaded"], 16 * N_SMALL)
            normed("ssd")
            pe.wait_ge(s["vec_ready"], 1)
            small(bank[5][0:16, 0:T], w_dt)
            pe.wait_ge(s["consts_ready"], 1)
            split_ready("ssd")
            project("ssd", 0, 3)
            pe.wait_ge(s["row_ready"], 1)
            for k in range(4):
                c = k % 2
                x = tr(bank[5][:, T + 16 * k:T + 16 * k + 16], rows[0:16, 2 + k // 2, c * P:(c + 1) * P], ident[0:16, 0:16])
            x.then_inc(s["row_turned"], 1)
            project("ssd", 3, 11)
            sum_squares("sc", 16, lambda i: colsel64[:, i, :])
            spread("sc", 16, lambda i: [row_of(2 * i, 16, 64), row_of(2 * i + 1, 16, 64)])
            pe.wait_ge(s["ssd_conv_done"], 3)
            pe.wait_ge(s["proj_copied"], 22)
            for k in range(4):
                c, hf = k // 2, k % 2
                if k >= 2:
                    pe.wait_ge(s["ssd_xt_used"], k - 1)
                for j in range(4):
                    x = tr(b4(k % 2)[:, j, :], cm[:, 8 + 4 * hf + j, c * P:(c + 1) * P], ident[:])
                x.then_inc(s["ssd_xt_done"], 1)
            pe.wait_ge(s["col_ready"], 1)
            for g in range(2):
                tr(b4(3)[:, g, :], cm[:, 16 + g, 0:P], ident[:])
            mm(bank[3][:, 2 * P:2 * P + 16], lastrow[:], tok[:, 0, :], start=True, stop=True)
            for j in range(4):
                c, g = j // 2, j % 2
                x = mm(b4(2)[:, j, :], cm[:, 16 + g, c * P:(c + 1) * P], cm[:, 18 + g, c * P:(c + 1) * P], start=True, stop=True)
            x.then_inc(s["ssd_g_done"], 1)
            pe.wait_ge(s["ssd_xdte"], 1)
            pe.wait_ge(s["spread_used"], 4)
            for g in range(2):
                x = mm(bank[6 + g][:], tiles(30, 1, P)[:, g, :], hn[:, 0, g * BLK:(g + 1) * BLK], start=True, stop=True)
            x.then_inc(s["ssd_state"], 1)

            def ssd_spread(i):
                c, hq = i // 4, i % 4
                if i >= 2:
                    pe.wait_ge(s["ssd_exp"], i - 1)
                for j in range(4):
                    x = mm(b4(i % 2)[:, j, :], row_of(4 * hq + j, 16), rows[0:16, 2, c * P:(c + 1) * P], start=True, stop=True)
                x.then_inc(s["ssd_bc"], 1)

            pe.wait_ge(s["ssd_xt_used"], 4)
            ssd_spread(0)
            for i in range(8):
                c, hq = i // 4, i % 4
                if i < 7:
                    ssd_spread(i + 1)
                pe.wait_ge(s["ssd_m"], i + 1)
                if c == 1:
                    pe.wait_ge(s["ssd_state_used"], 1)
                for j in range(4):
                    h = 4 * hq + j
                    dst = b2(2 + hq)[64 * (h % 2):64 * (h % 2) + 64, j // 2, c * P:(c + 1) * P]
                    m = hnTf[:, (i % 2) * 512 + j * P:(i % 2) * 512 + (j + 1) * P]
                    x = mm(dst, vtm[:, c, 64 * h:64 * h + 64], m, start=True, stop=(c == 0))
                    if c == 1:
                        ce = hnTf[:, 1024 + (i % 2) * 512 + j * P:1024 + (i % 2) * 512 + (j + 1) * P]
                        x = mm(dst, hn[:, 1, 64 * h:64 * h + 64], ce, start=False, stop=True)
                x.then_inc(s["ssd_y"], 1)
            out_projection("ssd", [0])
            pe.wait_ge(s["ssd_yready"], 2)
            sum_squares("ssd", 2, lambda i: column(i // 4, 2))
            spread("ssd", 2, lambda i: [row_of(i // 4, 2)])
            out_projection("ssd", [1])

            if stop >= 1:
                norm("moe")
                normed("moe")
                pe.wait_ge(s["x_ready"], X_BEFORE["moe"])
                for t in range(NT):
                    for k in range(KD):
                        x = mm(bank[5][:, t * (NG + NE):(t + 1) * (NG + NE)], hnT[:, k, t * P:(t + 1) * P], w_rt[:, k, :],
                               start=(k == 0), stop=(k == KD - 1))
                x.then_inc(s["rt_done"], 1)
                pe.wait_ge(s["rt_mask"], 2)
                mm(bank[5][:, P:P + NE], supper[:], r_mask[:, 0, :], start=True, stop=True)
                mm(bank[5][:, P + NE:P + 2 * NE], ones[:], r_mask[:, 0, :], start=True, stop=False)
                mm(bank[5][:, P + NE:P + 2 * NE], supper[:], r_mask[:, 1, :], start=False, stop=True)
                for t in range(NT):
                    x = mm(bank[5][:, T:T + NE], ones[:], r_mask[:, t, :], start=(t == 0), stop=(t == 1))
                x.then_inc(s["rt_rank"], 1)

                def gather(g, acc):
                    pe.wait_ge(s["moe_sel"], g + 1)
                    pe.wait_ge(s["moe_acc"], acc)
                    for k in range(KD):
                        for t in range(NT):
                            x = mm(b4(5 + k // 4)[:, k % 4, :], hn[:, t, k * P:(k + 1) * P], m_S[:, t, :],
                                   start=(t == 0), stop=(t == NT - 1))
                    x.then_inc(s["moe_gath"], 1)

                def pe_quad(q, it, g, wait_slot, release):
                    pe.wait_ge(s["moe_xg"], g + 1)
                    pe.wait_ge(s["moe_h"], it + 1)
                    for j in range(STEPS_UP):
                        w = wait_slot(q, j).rearrange("p (a e f) -> p a e f", a=2, e=QUAD)
                        for a in (0, 1):
                            for e in range(QUAD):
                                x = mm(bank[a][CAP * e:CAP * (e + 1), :], m_xg[:, j, CAP * e:CAP * (e + 1)], w[:, a, e, :],
                                       start=(j == 0), stop=(j == STEPS_UP - 1), tile_position=(0, CAP * e))
                        x.then_inc(release, 1)
                    gather(g + 1, it + 1)
                    pe.wait_ge(s["moe_sg"], it + 1)
                    pe.wait_ge(s["moe_gtc"], it + 1)
                    for t in range(NT):
                        x = tr(bank[7][:, t * P:(t + 1) * P], m_SG[:, t, :], ident[:])
                    x.then_inc(s["moe_gt"], 1)
                    pe.wait_ge(s["moe_h"], it + 2)
                    pe.wait_ge(s["moe_htc"], it + 1)
                    for c in range(STEPS_DOWN):
                        x = tr(b4(2)[:, c, :], m_h[:, c * P:(c + 1) * P], ident[:])
                    x.then_inc(s["moe_ht"], 1)
                    pe.wait_ge(s["moe_htc"], it + 2)
                    pe.wait_ge(s["moe_acc"], it + 1)
                    for c in range(STEPS_DOWN):
                        w = wait_slot(q, STEPS_UP + c).rearrange("p (e n) -> p e n", e=QUAD)
                        for n in (0, 1):
                            for e in range(QUAD):
                                x = mm(bank[3 + n][CAP * e:CAP * (e + 1), :], m_ht[:, c * P + CAP * e:c * P + CAP * (e + 1)],
                                       w[:, e, n * BLK:(n + 1) * BLK], start=(c == 0), stop=(c == STEPS_DOWN - 1),
                                       tile_position=(0, CAP * e))
                        x.then_inc(release, 1)
                    pe.wait_ge(s["moe_gtc"], it + 2)
                    pe.wait_ge(s["moe_ya"], it + 1)
                    pe.wait_ge(s["moe_yd"], it + 1)
                    pe.wait_ge(s["moe_xg"], g + 2)
                    for k in range(4):
                        t, n = k // 2, k % 2
                        x = mm(bank[[5, 6, 3, 4][k]][:], m_gt[:, t * P:(t + 1) * P], m_y[:, n, :], start=True, stop=True)
                    x.then_inc(s["moe_scat"], 1)

                base = RING_BASE["moe"]

                def ring_slot(q, j):
                    i = (base + j) % SLOTS
                    pe.wait_ge(ready[i], q * (32 * MOE_STEPS // SLOTS) + slot_value(base + j))
                    return ring[:, i, :]

                gather(0, 1)
                with pe.Fori(0, NQ) as q:
                    pe_quad(q, q, q, ring_slot, s["ring_used"])
                passes = pe.value_load(count_i[0:1, 0:1], min_val=1, max_val=T // CAP)
                with pe.If(passes > 1):
                    with pe.Fori(1, passes) as p:
                        gather(p * (NQ + 1), p * NQ + 1)

                        def ov_slot(q, j):
                            pe.wait_ge(ov_ready, (p - 1) * (32 * NQ * MOE_STEPS) + q * (32 * MOE_STEPS) + 32 * (j + 1))
                            return ring[:, 0, :]

                        with pe.Fori(0, NQ) as q:
                            pe_quad(q, p * NQ + q, p * (NQ + 1) + q, ov_slot, ov_used)

            def turn_rows(use, name, pairs):
                pe.wait_ge(s["row_ready"], use)
                for k, (src, R) in enumerate(pairs):
                    x = tr(bank[5][:, T + R * k:T + R * k + R], src, ident[0:R, 0:R])
                x.then_inc(s["row_turned"], 1)

            def fox(occ, li, name):
                norm(name)
                normed(name)
                small(bank[5][0:FOX_H, 0:T], w_f[:, occ])
                split_ready(name)
                project(name, 0, 2)
                turn_rows(ROW_USE[name], name, [(rows[0:FOX_H, 3, t * P:(t + 1) * P], FOX_H) for t in range(NT)])
                for k in range(4):
                    project(name, 2 + k, 3 + k)
                    sum_squares(name, 16, lambda i: column(i, 16), [k])
                project(name, 6, 7)
                spread(name, 16, lambda i: [row_of(i, 16)])
                project(name, 7, 8)
                pe.wait_ge(s["proj_copied"], PROJ_BASE[name] + 16)
                pe.wait_ge(s["qk_ready"], occ + 1)

                def scores(h):
                    k = occ * FOX_H + h
                    if h >= 2:
                        pe.wait_ge(s["fox_l"], k - 1)
                    q, kk = cm[:, h, :], cm[:, 8 + h, :]
                    for t, (a, b) in enumerate(((0, P), (P, 3 * P))):
                        mm(bank[h % 2][:, a:b], q[:, t * P:(t + 1) * P], kk[:, 0:b - a], start=True, stop=False)
                        x = mm(bank[h % 2][:, a:b], row_of(h, FOX_H), rows[0:FOX_H, 2, 0:b - a], start=False, stop=True)
                    x.then_inc(s["fox_s"], 1)

                scores(0)
                for h in range(FOX_H):
                    k = occ * FOX_H + h
                    if h < FOX_H - 1:
                        scores(h + 1)
                    pe.wait_ge(s["fox_p"], k + 1)
                    if h >= 2:
                        pe.wait_ge(s["fox_tc"], k - 1)
                    for j in range(3):
                        x = tr(bank[2 + h % 2][:, j * P:(j + 1) * P], f_p[h % 2][:, j * P:(j + 1) * P], ident[:])
                    x.then_inc(s["fox_t"], 1)
                    pe.wait_ge(s["fox_tc"], k + 1)
                    if h >= 2:
                        pe.wait_ge(s["fox_oc"], k - 1)
                    o, pt = bank[6 + h % 2], f_pt[h % 2]
                    mm(o[:, 0:P], vtm[:, 0, h * P:(h + 1) * P], pt[:, 0:P], start=True, stop=True)
                    mm(o[:, P:T], vtm[:, 0, h * P:(h + 1) * P], pt[:, P:2 * P], start=True, stop=False)
                    mm(o[:, P:T], vtm[:, 1, h * P:(h + 1) * P], pt[:, 2 * P:3 * P], start=False, stop=True)\
                        .then_inc(s["fox_o"], 1)
                out_projection(name)

            def gla():
                norm("gla")
                normed("gla")
                small(bank[5][0:16, 0:T], w_low)
                split_ready("gla")
                project("gla", 0, 1)
                pe.wait_ge(s["gla_low"], 1)
                for h in range(GLA_H):
                    x = mm(b2(4 + h // 2)[:, h % 2, :], w_gup[:, h * P:(h + 1) * P], rows[0:16, 0], start=True, stop=True)
                x.then_inc(s["gla_gate"], 1)
                project("gla", 1, 6)
                pe.wait_ge(s["proj_copied"], PROJ_BASE["gla"] + 12)
                pe.wait_ge(s["gla_qk"], 1)
                for h in range(GLA_H):
                    for t in range(NT):
                        i, tt = 2 * h + t, slice(t * P, (t + 1) * P)
                        x = mm(b4(i // 4)[:, i % 4, :], cm[:, 4 + h, tt], cm[:, h, tt], start=True, stop=True)
                x.then_inc(s["gla_at"], 1)
                for t in range(NT):
                    for h in range(GLA_H):
                        x = tr(b4(2 + t)[:, h, :], cm[:, 28 + h, t * P:(t + 1) * P], ident[:])
                x.then_inc(s["gla_kt"], 1)

                kdec = [tf(40 + 2 * t, 2) for t in range(NT)]

                def update(c):
                    t, lo = c // 2, 64 * (c % 2)
                    for h in range(GLA_H):
                        x = mm(b2(2 * (c % 2) + h // 2)[:, h % 2, :], kdec[t][lo:lo + 64, h * P:(h + 1) * P],
                               vtm[lo:lo + 64, t, h * GLA_DV:(h + 1) * GLA_DV], start=True, stop=True)
                    x.then_inc(s["gla_st"], 1)

                pe.wait_ge(s["gla_atc"], 1)
                for h in range(GLA_H):
                    for j in (0, 1):
                        for t in range(NT):
                            i = 2 * h + t
                            mm(b2(4 + h)[:, j, t * P:(t + 1) * P], vtm[:, t, h * GLA_DV + j * P:h * GLA_DV + (j + 1) * P],
                               tiles(24, 4, P)[:, i, :], start=(j == 0 and t == 0), stop=False, skip_group_check=True)
                pe.wait_ge(s["gla_ktc"], 1)
                update(0)
                for c in range(1, 4):
                    pe.wait_ge(s["gla_stc"], c)
                    for h in range(GLA_H):
                        for j in (0, 1):
                            x = mm(b2(4 + h)[:, j, c * 64:(c + 1) * 64], tiles(16, 4, GLA_DV)[:, h, j * P:(j + 1) * P],
                                   cm[:, h, c * 64:(c + 1) * 64], start=False, stop=(c == 3 and j == 1), skip_group_check=True)
                    if c < 3:
                        update(c)
                x.then_inc(s["gla_o"], 1)
                sum_squares("gla", GLA_H, lambda i: column(i // 2, GLA_H))
                spread("gla", GLA_H, lambda i: [row_of(i // 2, GLA_H)])
                out_projection("gla")

            def gdn():
                norm("gdn")
                normed("gdn")
                small(bank[5][0:8, 0:T], w_ab[:, :, 0:8], last=False)
                small(bank[5][0:8, T:2 * T], w_ab[:, :, 8:16])
                split_ready("gdn")
                project("gdn", 0, 2)
                turn_rows(ROW_USE["gdn"], "gdn", [(rows[0:8, r, t * P:(t + 1) * P], 8) for r in (2, 0) for t in range(NT)])
                project("gdn", 2, 3)
                pe.wait_ge(s["col_ready"], 2)
                mm(bank[5][:, T + 32:T + 40], lastrow[:], tok[:, 0, 0:8], start=True, stop=True).then_inc(s["gdn_last"], 1)
                project("gdn", 3, 4)
                project("gdn", 4, 5)
                sum_squares("gdn_qk", 8, lambda i: column(i, 8), [0])
                project("gdn", 5, 6)
                sum_squares("gdn_qk", 8, lambda i: column(i, 8), [1])
                spread("gdn_qk", 8, lambda i: [row_of(i, 8)])
                pe.wait_ge(s["gdn_conv_done"], 4)
                pe.wait_ge(s["proj_copied"], PROJ_BASE["gdn"] + 12)
                for k in range(4):
                    c, hf = k // 2, k % 2
                    if k >= 2:
                        pe.wait_ge(s["gdn_xtc"], k - 1)
                    for j in range(4):
                        x = tr(b4(k % 2)[:, j, :], cm[:, 8 + 4 * hf + j, c * P:(c + 1) * P], ident[:])
                    x.then_inc(s["gdn_xt"], 1)
                pe.wait_ge(s["gdn_qk_ready"], 1)
                for c in range(NT):
                    for h in range(GDN_QH):
                        x = tr(b4(2 + c)[:, h, :], cm[:, 4 + h, c * P:(c + 1) * P], ident[:])
                x.then_inc(s["gdn_kt"], 1)
                pe.wait_ge(s["gdn_xtc"], 4)

                def blocks(a):
                    return a.rearrange("p (h d) -> p h d", d=P)

                for i in range(4):
                    c, hf = i // 2, i % 2
                    cc = slice(c * P, (c + 1) * P)
                    if i:
                        pe.wait_ge(s["gdn_exp"], i)
                        pe.wait_ge(s["gdn_x"], i)
                    for j in range(4):
                        mm(b4(0)[:, j, :], row_of(4 * hf + j, 8), rows[0:8, 2, cc], start=True, stop=True)
                    for j in range(2):
                        k = cm[:, 4 + 2 * hf + j, cc]
                        mm(b4(1)[:, j, :], k, k, start=True, stop=True)
                        x = mm(b4(1)[:, 2 + j, :], k, cm[:, 2 * hf + j, cc], start=True, stop=True)
                    x.then_inc(s["gdn_bc"], 1)
                    pe.wait_ge(s["gdn_x"], i + 1)
                    if i:
                        pe.wait_ge(s["gdn_r_ready"], 7 * i)
                    for j in range(4):
                        x = tr(b4(5)[:, j, :], blocks(g_QT)[:, j, :], ident[:])
                    x.then_inc(s["gdn_turned"], 1)
                    for j in range(6):
                        pe.wait_ge(s["gdn_q_ready"], 7 * i + j + 1)
                        if i or j:
                            pe.wait_ge(s["gdn_qt_ready"], 6 * i + j)
                        Q, QT, R = blocks(g_Q), blocks(g_QT), blocks(g_R)
                        for h in range(4):
                            mm(b4(6)[:, h, :], QT[:, h, :], Q[:, h, :], start=True, stop=True)
                            x = mm(b4(7)[:, h, :], Q[:, h, :], QT[:, h, :], start=True, stop=True)
                        x.then_inc(s["gdn_power"], 1)
                        pe.wait_ge(s["gdn_qt_ready"], 6 * i + j + 1)
                        pe.wait_ge(s["gdn_r_ready"], 7 * i + j + 1)
                        for h in range(4):
                            x = mm(b4(4)[:, h, :], QT[:, h, :], R[:, h, :], start=True, stop=True)
                        x.then_inc(s["gdn_r"], 1)
                    pe.wait_ge(s["gdn_r_ready"], 7 * i + 7)
                    if i:
                        pe.wait_ge(s["gdn_u_ready"], i)
                    if i == 3:
                        pe.wait_ge(s["gdn_w_ready"], 1)
                    if i == 0:
                        pe.wait_ge(s["gdn_ktc"], 1)
                    for h in range(4):
                        if c == 1:
                            mm(b4(3)[:, h, :], blocks(g_kbg)[:, 4 * hf + h, :], R[:, h, :], start=True, stop=True)
                        x = mm(b4(2)[:, h, :], R[:, h, :], vtm[:, c, (4 * hf + h) * P:(4 * hf + h + 1) * P], start=True, stop=True)
                    x.then_inc(s["gdn_uw"], 1)
                pe.wait_ge(s["gdn_u_ready"], 4)
                pe.wait_ge(s["gdn_w_ready"], 2)
                u = [blocks(g_u[i]) for i in range(4)]
                qkk = [blocks(g_qkk[i]) for i in range(4)]
                state = tiles(40, 4, P)
                for h in range(8):
                    x = mm(b4(h // 4)[:, h % 4, :], blocks(g_kdec)[:, h, :], u[h // 4][:, h % 4, :], start=True, stop=True)
                x.then_inc(s["gdn_s"], 1)
                for h in range(8):
                    mm(b2(4 + h // 2)[:, h % 2, 0:P], u[h // 4][:, h % 4, :], qkk[h // 4][:, h % 4, :], start=True, stop=True)
                pe.wait_ge(s["gdn_s_ready"], 1)
                for h in range(8):
                    x = mm(b4(2 + h // 4)[:, h % 4, :], blocks(g_w[h // 4])[:, h % 4, :], state[:, h, :], start=True, stop=True)
                x.then_inc(s["gdn_ws"], 1)
                pe.wait_ge(s["gdn_new"], 1)
                for h in range(8):
                    dst = b2(4 + h // 2)[:, h % 2, P:T]
                    mm(dst, state[:, h, :], blocks(g_qd[h // 4])[:, h % 4, :], start=True, stop=False)
                    x = mm(dst, u[2 + h // 4][:, h % 4, :], qkk[2 + h // 4][:, h % 4, :], start=False, stop=True)
                x.then_inc(s["gdn_o"], 1)
                sum_squares("gdn_o", 8, lambda i: column(i, 8))
                spread("gdn_o", 8, lambda i: [row_of(i, 8)])
                out_projection("gdn")

            if stop >= 2:
                fox(0, 1, "fox0")
            if stop >= 3:
                gla()
            if stop >= 4:
                gdn()
            if stop >= 5:
                fox(1, 4, "fox1")


_INS = ["x", "norm_mix", "w_in", "ssd_conv_w", "ssd_conv_b", "dt_bias", "a_log", "d_skip", "ssd_norm", "sc_conv_w",
        "sc_norm", "w_out", "norm_ffn", "w_router_group", "w_router_expert", "w_gate", "w_up", "w_down", "final_norm",
        "norm_w_2", "fox_w_in_2", "fox_b_f_2", "fox_q_gain_2", "fox_k_gain_2", "fox_w_out_2", "gla_w_in_2",
        "gla_w_gate_up_2", "gla_b_gate_2", "gla_o_gain_2", "gla_w_out_2", "gdn_w_in_2", "gdn_conv_w_2",
        "gdn_a_log_2", "gdn_dt_bias_2", "gdn_o_gain_2", "gdn_w_out_2"]
UPTO = "all"


def kernel(**inputs):
    import numpy as _np
    import concourse.bacc as _bacc
    from concourse.bass_utils import run_bass_kernel_spmd as _run

    nc = _bacc.Bacc("TRN2", target_bir_lowering=False, num_devices=1)
    arrays, args = {}, []
    for name in _INS:
        a = _np.ascontiguousarray(inputs[name])
        if name in ("w_gate", "w_up", "w_down"):
            a = a[0]
        arrays[f"in_{name}"] = a
        args.append(nc.dram_tensor(f"in_{name}", a.shape, F32, kind="ExternalInput").ap())
    out = nc.dram_tensor("out", (1, T, D), F32, kind="ExternalOutput").ap()
    build(nc, *args, out, upto=UPTO)
    r = _run(nc, [arrays], core_ids=[0])
    return r.results[0]["out"]
```

```python
from contextlib import ExitStack

import concourse.bass as bass
from concourse import mybir

F32 = mybir.dt.float32
F32R = mybir.dt.float32r
I32 = mybir.dt.int32
ALU = mybir.AluOpType
ACT = mybir.ActivationFunctionType
AX = mybir.AxisListType

P = 128
T = 256
NT = T // P
D = 1024
KD = D // P
BLK = 512
EPS = 1e-6
RSQRT_SEED = 1597463007.0

SLOTS = 4
SLOT = KD * BLK
UNITS = 4
UNIT = SLOT // UNITS
PARTS = 3

SSD_H, SSD_N = 16, 128
SSD_W, SSD_XBC = 1024, 1536
FOX_H = 8
GLA_H, GLA_DK, GLA_DV, GLA_CH = 4, 128, 256, 64
GDN_QH, GDN_VH = 4, 8
NG, EPG = 4, 8
NE = NG * EPG
QUAD = 4
CAP = P // QUAD
NQ = NE // QUAD
FF = 512
STEPS_UP, STEPS_DOWN = KD, FF // P
MOE_STEPS = STEPS_UP + STEPS_DOWN

VEC_A = [("ssd_conv_w", 48), ("ssd_conv_b", 12), ("ssd_norm", 8), ("sc_conv_w", 24), ("sc_norm", 8),
         ("norm_mix", 8), ("norm_ffn", 8), ("fox_q_gain", 2), ("fox_k_gain", 2), ("gla_o_gain", 2),
         ("gla_b_gate", 4), ("gdn_o_gain", 1)]
VEC_B = [("norm_w", 32), ("gdn_conv_w", 64)]
NA = sum(n for _, n in VEC_A)
NB = sum(n for _, n in VEC_B)
VCOL = {}
for _tab, _start in ((VEC_A, 0), (VEC_B, P)):
    for _name, _n in _tab:
        VCOL[_name] = _start
        _start += _n

LAYERS = ["ssd", "fox0", "gla", "gdn", "fox1"]
KINDS = {"ssd": ["channels"] * 11,
         "fox0": ["channels"] * 4 + ["tokens"] * 2 + ["channels"] * 2,
         "gla": ["channels"] * 2 + ["tokens"] * 2 + ["channels"] * 2,
         "gdn": ["channels"] * 6}
KINDS["fox1"] = KINDS["fox0"]
PROJ_BLOCKS = {_l: len(KINDS[_l]) for _l in LAYERS}
PROJ_BASE, _n = {}, 0
for _l in LAYERS:
    PROJ_BASE[_l] = _n
    _n += 2 * PROJ_BLOCKS[_l]

OUT_GROUPS = {_l: 2 if _l == "ssd" else 1 for _l in LAYERS}
UNIT_BASE, PAIR_BASE, _n, _m = {}, {}, 0, 0
for _l in LAYERS:
    UNIT_BASE[_l] = _n
    UNIT_BASE[_l + "_out"] = _n + UNITS * PROJ_BLOCKS[_l]
    _n += UNITS * (PROJ_BLOCKS[_l] + 2 * OUT_GROUPS[_l])
    PAIR_BASE[_l] = _m
    _m += 4 * OUT_GROUPS[_l]

RING_BASE, _n = {}, 0
for _l in LAYERS:
    RING_BASE[_l] = _n
    _n += PROJ_BLOCKS[_l]
    RING_BASE[_l + "_out"] = _n
    _n += 2 * OUT_GROUPS[_l]
    if _l == "ssd":
        RING_BASE["moe"] = _n
        _n += NQ * MOE_STEPS

ROWN = {}
_n = 0
for _name, _tiles in (("sc", 8), ("ssd", 8), ("fox0", 16), ("gla", 8), ("gdn_qk", 8), ("gdn_o", 8), ("fox1", 16)):
    ROWN[_name] = (len(ROWN), _n, _tiles)
    _n += _tiles

SOFT_USE = {"ssd": 1, "fox0": 2, "gdn": 3, "fox1": 4}
ROW_USE = {"ssd": 1, "fox0": 2, "gdn": 3, "fox1": 4}
SHARE = {"ssd": 4, "gla": 2}
SPREAD_BASE, SPREAD_END, _n = {}, [], 0
for _name in ROWN:
    SPREAD_BASE[_name] = _n
    _, _before, _tiles = ROWN[_name]
    for _i in range(_tiles // 2 // SHARE.get(_name, 1)):
        SPREAD_END.append(_before // 2 + (_i + 1) * SHARE.get(_name, 1))
        _n += 1

SUM_BANK = 4

X_BEFORE = {"moe": 4, "fox0": 6, "gla": 10, "gdn": 14, "fox1": 18, "end": 22}
NORMS = ["ssd", "moe", "fox0", "gla", "gdn", "fox1"]
SPLIT_NORMS = [_n for _n in NORMS if _n != "moe"]
SQS = ["ssd", "moe", "final", "fox0", "gla", "gdn", "fox1"]
HALVED = ("moe", "gla", "gdn", "fox1")
SQ_BEFORE, _n = {}, 0
for _name in SQS:
    SQ_BEFORE[_name] = _n
    _n += 4 if _name in HALVED else 2


def build(nc, x_in, norm_mix, w_in, ssd_conv_w, ssd_conv_b, dt_bias, a_log, d_skip, ssd_norm, sc_conv_w,
          sc_norm, w_out, norm_ffn, w_router_group, w_router_expert, w_gate, w_up, w_down, final_norm,
          norm_w, fox_w_in, fox_b_f, fox_q_gain, fox_k_gain, fox_w_out, gla_w_in, gla_w_gate_up, gla_b_gate,
          gla_o_gain, gla_w_out, gdn_w_in, gdn_conv_w, gdn_a_log, gdn_dt_bias, gdn_o_gain, gdn_w_out, out):
    ctx = ExitStack()
    with ctx:
        def sb(name, shape, dt=F32):
            return ctx.enter_context(nc.sbuf_tensor(name, shape, dt))

        def sem(name):
            return ctx.enter_context(nc.semaphore(name))

        ring = sb("ring", [P, SLOTS, SLOT])
        x_res = sb("x_res", [P, NT, D])
        hn = sb("hn", [P, NT, D])
        hnT = sb("hnT", [P, KD, T])
        hnT_h, hnT_l = sb("hnT_h", [P, KD, T], F32R), sb("hnT_l", [P, KD, T], F32R)
        w_h, w_l = sb("w_h", [P, PARTS, UNIT], F32R), sb("w_l", [P, PARTS, UNIT], F32R)
        cm = sb("cm", [P, 44, T])
        vtm = sb("vtm", [P, NT, D])
        sq = sb("sq", [P, 2, 4, T])
        onehot = sb("onehot", [P, 32])
        colsel64 = sb("colsel64", [P, 8, 16])
        ident = sb("ident", [P, P])
        ones = sb("ones", [P, P])
        qgain = sb("qgain", [P, 1])
        upper = sb("upper", [P, P])
        supper = sb("supper", [P, P])
        slower = sb("slower", [P, P])
        upper64 = sb("upper64", [P, P])
        negmask = sb("negmask", [P, 2, P])
        iota_i = sb("iota_i", [P, CAP], I32)
        iota = sb("iota", [P, CAP])
        vec = sb("vec", [P, 2 * P])
        ss = sb("ss", [P, 12])
        w_dt = sb("w_dt", [P, KD, SSD_H])
        w_f = sb("w_f", [P, 2, KD, FOX_H])
        w_low = sb("w_low", [P, KD, 16])
        w_ab = sb("w_ab", [P, KD, 16])
        w_rt = sb("w_rt", [P, KD, NG + NE])
        w_gup = sb("w_gup", [16, BLK])
        cols = sb("cols", [16, 8])
        ncols = sb("ncols", [16, 2])
        dsk = sb("dsk", [P, 8])
        heads = sb("heads", [P, 3, 2 * 16])
        rows = sb("rows", [16, 4, T])
        tok = sb("tok", [P, 8, 16])
        count_i = sb("count_i", [1, 1], I32)

        bank = [ctx.enter_context(nc.psum_tensor(f"bank{i}", [P, 512], F32)) for i in range(8)]

        cmf = cm[:].rearrange("p a b -> p (a b)")
        hnTf = hnT[:].rearrange("p a b -> p (a b)")

        def tiles(a, n, inner=T):
            return cmf[:, a * T:(a + n) * T].rearrange("p (n i) -> p n i", i=inner)

        def b2(i):
            return bank[i][:].rearrange("p (a b) -> p a b", b=T)

        def b4(i):
            return bank[i][:].rearrange("p (a b) -> p a b", b=P)

        s = {n: sem(n) for n in (
            "x_loaded", "vec_loaded", "small_loaded", "late_loaded", "fnorm_loaded", "out_stored", "ring_used",
            "pool_chain", "ident_ready", "consts_ready",
            "dve_chain", "act_chain", "moe_chain", "pass_chain", "sp_turn",
            "vec_turned", "vec_ready", "cols_ready",
            "ss_ready", "xn_ready", "turned", "hnT_act", "hnT_dve", "x_ready", "gained",
            "hnT_high", "hnT_own", "hnT_split", "high_ready", "low_ready", "unit_done", "proj_copied", "small_done",
            "sq_ready", "sq_summed", "rownorm_ready", "spread_done", "spread_used",
            "out_high", "out_low",
            "lin_ready", "tanh_ready", "z_tanh", "z_ready",
            "row_arg", "qk_ready", "row_ln", "row_ready", "row_turned", "col_ready",
            "ssd_conv_done", "ssd_xt_done", "ssd_xt_used", "ssd_g_done", "ssd_bc", "ssd_seg", "ssd_exp",
            "ssd_m", "ssd_y", "ssd_dte_arg", "ssd_dte", "ssd_xdte", "ssd_state", "ssd_state_used", "ssd_yready",
            "rt_done", "rt_arg", "rt_exp", "rt_mask", "rt_rank", "rt_passes", "moe_sel", "moe_sg", "moe_gath", "moe_xg", "moe_tanh",
            "moe_h", "moe_gt", "moe_gtc", "moe_ht", "moe_htc", "moe_ya", "moe_yd", "moe_scat", "moe_acc", "moe_done",
            "fox_s", "fox_l", "fox_e", "fox_p", "fox_t", "fox_tc", "fox_o", "fox_oc",
            "gla_low", "gla_gate", "gla_arg", "gla_ln", "gla_dec", "gla_exp", "gla_qk", "gla_at", "gla_atc", "gla_kt",
            "gla_ktc", "gla_st", "gla_stc", "gla_o", "gla_oc",
            "gdn_row_free", "gdn_beta_exp", "gdn_last", "gdn_col_arg", "gdn_col_exp", "gdn_conv_done", "gdn_qk_ready",
            "gdn_xt", "gdn_xtc", "gdn_kt", "gdn_ktc", "gdn_bc", "gdn_arg", "gdn_exp", "gdn_x", "gdn_turned", "gdn_q_ready",
            "gdn_qt_ready", "gdn_power", "gdn_r", "gdn_r_ready", "gdn_uw", "gdn_u_ready", "gdn_w_ready", "gdn_s",
            "gdn_s_ready", "gdn_ws", "gdn_new", "gdn_o", "gdn_oc",
        )}
        ready = [sem(f"slot_ready{i}") for i in range(SLOTS)]
        ov_ready, ov_used = sem("ov_ready"), sem("ov_used")

        earlier = sb("earlier", [P, 8, 8])

        def column(r, R):
            return onehot[:, 15 - r:15 - r + R]

        def row_of(r, R, n=P):
            return ident[0:R, r:r + 1].to_broadcast([R, n])

        def tf(a, n):
            return cmf[:, a * T:(a + n) * T]

        used_floats = [0]

        def view(*shape):
            size = 1
            for k in shape:
                size *= k
            a = cmf[:, used_floats[0]:used_floats[0] + size]
            used_floats[0] += size
            if len(shape) == 2:
                return a.rearrange("p (a b) -> p a b", a=shape[0])
            return a

        m_xg, m_S, m_SG, m_gt = view(KD, P), view(NT, P), view(NT, P), view(T)
        m_tanh, m_silu, m_h, m_ht, m_y = view(FF), view(FF), view(FF), view(FF), view(2, BLK)
        r_lg, r_eg, r_n, r_gs, r_es, r_ex = (view(NT, NG + NE), view(NT, NG), view(NT, 2), view(NT, 1), view(NT, EPG),
                                             view(NT, EPG))
        r_c1, r_c2, r_gsel, r_sel, r_sum = view(NT * EPG * EPG), view(NT * EPG * EPG), view(NT, NG), view(NT, EPG), view(NT, 4)
        r_mask, r_gate, r_pm, r_pass = view(NT, NE), view(NT, NE + QUAD), view(NT, NE + QUAD), view(2, 16)
        r_prod = view(NT * NG * EPG).rearrange("p (t g e) -> p t g e", t=NT, g=NG)
        assert used_floats[0] <= 40 * T
        N_EARLY, N_LATE = 8, 6 + NG

        f_l = [cmf[:, 24 * T + i * 384:24 * T + (i + 1) * 384] for i in (0, 1)]
        f_p = [cmf[:, 27 * T + i * 384:27 * T + (i + 1) * 384] for i in (0, 1)]
        f_pt = [cmf[:, 30 * T + i * 384:30 * T + (i + 1) * 384] for i in (0, 1)]
        f_banks = (0, 1, 4)
        f_n = tiles(33, 1, 2)[:, 0:2, :]
        f_s = tiles(33, 1, 2)[:, 2:4, :]
        f_r = tiles(33, 1, 2)[:, 4:6, :]

        gla_states = (tiles(16, 4, GLA_DV), tiles(28, 4, GLA_DV))

        sqf = sq[:].rearrange("p a b c -> p (a b c)")
        g_Q, g_QT, g_R, g_dt = ([a[:, i * 512:(i + 1) * 512] for a in (hnTf, sqf)] for i in range(4))
        g_d = g_R
        g_km, g_qm = [tiles(42, 1, P), tiles(40, 1, P)], [tiles(43, 1, P), tiles(41, 1, P)]
        g_banks = [(0, 1, 4, 6, 7), (5, 4, 5, 2, 3)]
        g_w = [hn[:, 0, i * 512:(i + 1) * 512] for i in (0, 1)]
        g_qd = [hn[:, 1, i * 512:(i + 1) * 512] for i in (0, 1)]
        g_u = [tf(8 + 2 * i, 2) for i in range(4)]
        g_qkk = [tf(24 + 2 * i, 2) for i in range(4)]
        g_kbg, g_kdec = tf(32, 4), tf(36, 4)

        def slot_value(n):
            return 32 * (n // SLOTS + 1)

        def released(n):
            for l in LAYERS:
                b = RING_BASE[l]
                if b <= n < b + PROJ_BLOCKS[l] + 2 * OUT_GROUPS[l]:
                    return s["low_ready"], UNIT_BASE[l] + UNITS * (n - b + 1)
            return s["ring_used"], n - RING_BASE["moe"] + 1

        def unit_of(u):
            for l in LAYERS:
                i, m = (u - UNIT_BASE[l]) // UNITS, (u - UNIT_BASE[l]) % UNITS
                if 0 <= i < PROJ_BLOCKS[l] + 2 * OUT_GROUPS[l]:
                    n = RING_BASE[l] + i
                    w = ring[:, n % SLOTS, :].rearrange("p (c n) -> p c n", n=BLK)
                    if i < PROJ_BLOCKS[l] and KINDS[l][i] == "channels":
                        return n, w[:, :, m * P:(m + 1) * P], P
                    return n, w[:, 2 * m:2 * m + 2, :], BLK

        def part(x, u, width):
            return x[:, u % PARTS, :].rearrange("p (c n) -> p c n", n=width)

        def bank_units(layer, b):
            if KINDS[layer][b // 2] == "channels":
                return UNIT_BASE[layer] + 2 * b + 2
            return UNIT_BASE[layer] + UNITS * (b // 2 + 1)

        def block_halves(w, col):
            v = w[:, col:col + BLK].rearrange("(c p) n -> p c n", p=P)
            return [v[:, 0:4, :], v[:, 4:8, :]]

        up_v = [w.rearrange("(q j) (c p) f -> q c p j f", j=QUAD, p=P) for w in (w_gate, w_up)]
        down_v = w_down.rearrange("(q j) (c p) n -> q c p j n", j=QUAD, p=P)

        def slot_half(i, h):
            return ring[:, i, h * (SLOT // 2):(h + 1) * (SLOT // 2)]

        def moe_halves(i, q, j):
            if j < STEPS_UP:
                return [(slot_half(i, h).rearrange("p (e f) -> p e f", e=QUAD), up_v[h][q, j]) for h in (0, 1)]
            return [(slot_half(i, h).rearrange("p (e f) -> p e f", e=QUAD // 2),
                     down_v[q, j - STEPS_UP][:, 2 * h:2 * h + 2, :]) for h in (0, 1)]

        col_of = {
            "ssd": [SSD_W + BLK * i for i in range(3)] +
                   [SSD_W + SSD_XBC + SSD_H + D + BLK * i for i in range(4)] +
                   [SSD_W + SSD_XBC + SSD_H + BLK * i for i in range(2)] +
                   [BLK * i for i in range(2)],
            "fox0": [BLK * i for i in range(8)], "fox1": [BLK * i for i in range(8)],
            "gla": [BLK * i for i in range(6)],
            "gdn": [BLK * i for i in range(6)],
        }
        w_of = {"ssd": w_in[0], "fox0": fox_w_in[0], "gla": gla_w_in[0], "gdn": gdn_w_in[0], "fox1": fox_w_in[1]}
        wo_of = {"ssd": w_out[0], "fox0": fox_w_out[0], "gla": gla_w_out[0], "gdn": gdn_w_out[0], "fox1": fox_w_out[1]}

        block = ctx.enter_context(nc.Block())

        @block.sync
        def _(sp):
            def by_chunks(w):
                return w.rearrange("(c p) n -> p c n", p=P)

            early = ((w_dt[:], by_chunks(w_in[0][:, SSD_W + SSD_XBC:SSD_W + SSD_XBC + SSD_H])),
                     (cols[0:16, 0:1], a_log.rearrange("a h -> h a")), (cols[0:16, 1:2], dt_bias.rearrange("a h -> h a")),
                     (cols[0:8, 2:4], fox_b_f.rearrange("a h -> h a")),
                     (cols[0:8, 4:5], gdn_a_log.rearrange("a h -> h a")),
                     (cols[0:8, 5:6], gdn_dt_bias.rearrange("a h -> h a"))) + tuple(
                (dsk[64 * h:64 * h + 64, :], d_skip[0].rearrange("(i two) -> two i", two=2)[h:h + 1, :].to_broadcast([64, 8]))
                for h in (0, 1))
            late = ((w_f[:, 0], by_chunks(fox_w_in[0][:, 4 * D:4 * D + FOX_H])),
                    (w_f[:, 1], by_chunks(fox_w_in[1][:, 4 * D:4 * D + FOX_H])),
                    (w_low[:], by_chunks(gla_w_in[0][:, 3 * D:3 * D + 16])),
                    (w_ab[:], by_chunks(gdn_w_in[0][:, 3 * D:3 * D + 16])),
                    (w_rt[:, :, 0:NG], by_chunks(w_router_group[0])), (w_gup[:], gla_w_gate_up[0])) + tuple(
                (w_rt[:, :, NG + EPG * g:NG + EPG * (g + 1)], by_chunks(w_router_expert[0, g])) for g in range(NG))
            assert len(early) == N_EARLY and len(late) == N_LATE

            def load_small(loads, done):
                for dst, src in loads:
                    sp.dma_start(dst, src, allow_slow_non_contiguous=True).then_inc(done, 16)

            for t in range(NT):
                sp.dma_start(x_res[:, t, :], x_in[0, t * P:(t + 1) * P, :]).then_inc(s["x_loaded"], 16)

            def put(n, halves):
                i = n % SLOTS
                if n >= SLOTS:
                    sp.wait_ge(*released(n - SLOTS))
                for dst, src in halves:
                    sp.dma_start(dst, src).then_inc(ready[i], 16)

            def put_block(n, w, col):
                halves = block_halves(w, col)
                put(n, [(slot_half(n % SLOTS, h).rearrange("p (c n) -> p c n", c=4), halves[h]) for h in (0, 1)])

            sp.wait_ge(s["vec_loaded"], 16 * (len(VEC_A) + len(VEC_B)))
            for l in LAYERS:
                for i, col in enumerate(col_of[l]):
                    if l == "ssd" and i == 1:
                        load_small(early, s["small_loaded"])
                    if l == "ssd" and i == SLOTS:
                        load_small(late, s["late_loaded"])
                    put_block(RING_BASE[l] + i, w_of[l], col)
                groups = wo_of[l].shape[0] // D
                for i in range(2 * groups):
                    g = groups - 1 - i // 2
                    put_block(RING_BASE[l + "_out"] + i, wo_of[l][g * D:(g + 1) * D, :], BLK * (i % 2))
                if l == "ssd":
                    base = RING_BASE["moe"]
                    for j in range(MOE_STEPS):
                        put(base + j, moe_halves((base + j) % SLOTS, 0, j))
                    with sp.Fori(1, NQ) as q:
                        for j in range(MOE_STEPS):
                            i = (base + j) % SLOTS
                            sp.wait_ge(s["ring_used"], q * MOE_STEPS + (j - SLOTS + 1))
                            sp.sem_inc(s["sp_turn"], 1)
                            for dst, src in moe_halves(i, q, j):
                                sp.dma_start(dst, src).then_inc(ready[i], 16)
                    sp.wait_ge(s["rt_passes"], 1)
                    passes = sp.value_load(count_i[0:1, 0:1], min_val=1, max_val=T // CAP)
                    with sp.If(passes > 1):
                        sp.wait_ge(s["ring_used"], NQ * MOE_STEPS)
                        with sp.Fori(1, passes) as p:
                            with sp.Fori(0, NQ) as q:
                                for j in range(MOE_STEPS):
                                    for dst, src in moe_halves(0, q, j):
                                        sp.dma_start(dst, src).then_inc(ov_ready, 16)
                                    sp.wait_ge(ov_used, (p - 1) * (NQ * MOE_STEPS) + q * MOE_STEPS + (j + 1))
                                    sp.sem_inc(s["sp_turn"], 1)
            for k in range(4):
                n, t = k // 2, k % 2
                sp.wait_ge(s["x_ready"], X_BEFORE["end"] - 3 + k)
                c = slice(n * BLK, (n + 1) * BLK)
                sp.dma_start(out[0, t * P:(t + 1) * P, c], x_res[:, t, c]).then_inc(s["out_stored"], 16)
            sp.wait_ge(s["out_stored"], 16 * 4)

        @block.gpsimd
        def _(pool):
            n = [0]

            def link(ins):
                n[0] += 1
                ins.then_inc(s["pool_chain"], 1)
                pool.wait_ge(s["pool_chain"], n[0])

            link(nc.gpsimd.memset(ident[:], 0.0))
            link(nc.gpsimd.affine_select(out=ident[:], in_=ident[:], compare_op=ALU.not_equal, fill=1.0, base=0,
                                         pattern=[[-1, P]], channel_multiplier=1))
            pool.sem_inc(s["ident_ready"], 1)
            for t in (onehot, colsel64, negmask):
                link(nc.gpsimd.memset(t[:], 0.0))
            for t in (ones, upper, supper, slower, upper64, earlier):
                link(nc.gpsimd.memset(t[:], 1.0))
            link(nc.gpsimd.iota(iota_i[:], pattern=[[1, CAP]], base=0, channel_multiplier=0))
            link(nc.gpsimd.tensor_copy(iota[:], iota_i[:]))

            def select(a, op, fill, base, pattern, cmul):
                link(nc.gpsimd.affine_select(out=a, in_=a, compare_op=op, fill=fill, base=base,
                                             pattern=pattern, channel_multiplier=cmul))

            select(onehot[:], ALU.not_equal, 1.0, -15, [[1, 32]], 0)
            for half in (0, 1):
                select(colsel64[64 * half:64 * half + 64], ALU.not_equal, 1.0, half, [[2, 8], [-1, 16]], 0)
            select(upper[:], ALU.is_ge, 0.0, 0, [[1, P]], -1)
            select(supper[:], ALU.is_ge, 0.0, -1, [[1, P]], -1)
            select(slower[:], ALU.is_ge, 0.0, -1, [[-1, P]], 1)
            select(earlier[:], ALU.is_ge, 0.0, -1, [[1, 8], [-1, 8]], 0)
            select(negmask[:, 1, :], ALU.is_ge, -1e30, 0, [[-1, P]], 1)
            select(upper64[:], ALU.is_ge, 0.0, 0, [[1, P]], -1)
            select(upper64[:, 64:P], ALU.is_ge, 0.0, -64, [[0, 64]], 1)
            pool.sem_inc(s["consts_ready"], 1)
            for u in range(UNIT_BASE[LAYERS[-1] + "_out"] + 2 * UNITS * OUT_GROUPS[LAYERS[-1]]):
                _, w, width = unit_of(u)
                pool.wait_ge(s["high_ready"], u + 1)
                nc.gpsimd.tensor_tensor(part(w_l, u, width), w, part(w_h, u, width).bitcast(F32),
                                        ALU.subtract).then_inc(s["low_ready"], 1)

        @block.scalar
        def _(act):
            n_link = [0]

            def link(ins):
                n_link[0] += 1
                ins.then_inc(s["act_chain"], 1)
                act.wait_ge(s["act_chain"], n_link[0])

            af = nc.scalar.activation

            staged = [tiles(0, 1)[0:NA, 0, 0:P], tiles(1, 1)[0:NB, 0, 0:P]]
            srcs = {"ssd_conv_w": ssd_conv_w, "ssd_conv_b": ssd_conv_b, "ssd_norm": ssd_norm, "sc_conv_w": sc_conv_w,
                    "sc_norm": sc_norm, "norm_mix": norm_mix, "norm_ffn": norm_ffn, "fox_q_gain": fox_q_gain,
                    "fox_k_gain": fox_k_gain, "gla_o_gain": gla_o_gain, "gla_b_gate": gla_b_gate,
                    "gdn_o_gain": gdn_o_gain, "norm_w": norm_w, "gdn_conv_w": gdn_conv_w}
            for tab, dst in zip((VEC_A, VEC_B), staged):
                at = 0
                for name, k in tab:
                    src = srcs[name]
                    flat = src.rearrange("a b c -> (a b c)") if len(src.shape) == 3 else src.rearrange("a b -> (a b)")
                    act.dma_start(dst[at:at + k, :], flat.rearrange("(r p) -> r p", p=P)).then_inc(s["vec_loaded"], 16)
                    at += k

            def square_sum(name):
                for t in range(NT):
                    af(hn[:, t, :], x_res[:, t, :], ACT.Square, accum_out=ss[:, t:t + 1]).then_inc(s["ss_ready"], 1)

            def half_sum(name, n):
                for t in range(NT):
                    act.wait_ge(s["x_ready"], X_BEFORE[name] - 3 + 2 * n + t)
                    c = slice(n * BLK, (n + 1) * BLK)
                    af(hn[:, t, c], x_res[:, t, c], ACT.Square,
                       accum_out=ss[:, 8 * (1 - n) + t:8 * (1 - n) + t + 1]).then_inc(s["ss_ready"], 1)

            n_high = [0]

            def high(end):
                for u in range(n_high[0], end):
                    n, w, width = unit_of(u)
                    act.wait_ge(ready[n % SLOTS], slot_value(n))
                    if u >= PARTS:
                        act.wait_ge(s["unit_done"], u - PARTS + 1)
                    af(part(w_h, u, width), w, ACT.Copy).then_inc(s["high_ready"], 1)
                n_high[0] = max(n_high[0], end)

            def layer_start(name):
                if name == "ssd":
                    act.wait_ge(s["x_loaded"], 16 * NT)
                    square_sum(name)
                elif name == "fox0":
                    for t in range(NT):
                        act.wait_ge(s["gained"], t + 1)
                        af(sqf[:, t * D:(t + 1) * D], vtm[:, t, :], ACT.Square, accum_out=ss[:, 8 + t:9 + t]).then_inc(s["ss_ready"], 1)
                else:
                    half_sum(name, 0)
                    if name != "moe":
                        high(UNIT_BASE[name] + 2)
                    half_sum(name, 1)
                if name not in ("ssd", "moe"):
                    high(UNIT_BASE[name] + 3)

            def out_high(name, pair, src, n=1):
                k = 2 * (pair % 4)
                if pair >= 4:
                    act.wait_ge(s["unit_done"], UNIT_BASE[name + "_out"] + UNITS + pair % 4 + 1)
                af(hnT_h[:, k:k + 2 * n, :], src, ACT.Copy).then_inc(s["out_high"], n)

            def norm_copies(u, col, split=True):
                for b in (0, 2):
                    act.wait_ge(s["turned"], 4 * u + b + 1)
                    for j in (0, 1):
                        i = af(hnT[:, 2 * b + j, :], b2(4 if b and not split else 6)[:, j, :], ACT.Copy,
                               scale=vec[:, col + 2 * b + j:col + 2 * b + j + 1])
                    i.then_inc(s["hnT_act"], 1)
                    if split:
                        act.wait_ge(s["hnT_act"], 2 * u + b // 2 + 1)
                        af(hnT_h[:, 2 * b:2 * b + 2, :], hnT[:, 2 * b:2 * b + 2, :], ACT.Copy).then_inc(s["hnT_high"], 1)

            def copy_bank(layer, b, dst, scale=1.0):
                g = PROJ_BASE[layer] + b
                done = bank_units(layer, b)
                high(min(done + PARTS, UNIT_BASE[layer + "_out"] + PARTS))
                act.wait_ge(s["unit_done"], done)
                af(dst, bank[g % 4][:], ACT.Copy, scale=scale).then_inc(s["proj_copied"], 1)

            def own_copies(layer, banks):
                act.wait_ge(s["proj_copied"], PROJ_BASE[layer] + banks)

            def squares(name, k, src):
                _, before, _ = ROWN[name]
                g = before // 4 + k
                if g >= 2:
                    act.wait_ge(s["sq_summed"], g - 1)
                af(sq[:, g % 2].rearrange("p a b -> p (a b)"), src, ACT.Square).then_inc(s["sq_ready"], 1)

            def silu_z(li, z0, summed):
                act.wait_ge(s["sq_summed"], summed)
                for b in (0, 1):
                    af(sq[:, b].rearrange("p a b -> p (a b)"), cmf[:, (z0 + 4 * b) * T:(z0 + 4 * b + 4) * T],
                       ACT.Tanh).then_inc(s["z_tanh"], 1)

            def softplus_row(k, src, dst, parts):
                act.wait_ge(s["row_arg"], k)
                link(af(dst[0:parts], src[0:parts], ACT.Exp, scale=-1.0))
                af(dst[0:parts], dst[0:parts], ACT.Ln, bias=1.0).then_inc(s["row_ln"], 1)

            layer_start("ssd")
            act.wait_ge(s["small_loaded"], 16 * N_EARLY)
            af(ncols[0:16, 0:1], cols[0:16, 0:1], ACT.Exp)
            af(ncols[0:8, 1:2], cols[0:8, 4:5], ACT.Exp).then_inc(s["cols_ready"], 1)
            act.wait_ge(s["vec_ready"], 1)
            norm_copies(0, VCOL["norm_mix"])
            high(PARTS)
            softplus_row(1, rows[:, 1, :], rows[:, 2, :], 16)
            for b in range(6):
                copy_bank("ssd", b, cmf[:, (8 + 2 * b) * T:(10 + 2 * b) * T])
            dst = [28 + 2 * i for i in range(4)] + [36 + 2 * i for i in range(4)] + [20 + 2 * i for i in range(4)] + \
                  [2 * i for i in range(4)]
            for b in range(16):
                copy_bank("ssd", 6 + b, cmf[:, dst[b] * T:(dst[b] + 2) * T], 0.5 if b >= 12 else 1.0)
                if b in (0, 3, 6):
                    k = b // 3
                    act.wait_ge(s["lin_ready"], k + 1)
                    af(vtm[:, 1, :], vtm[:, 0, :], ACT.Tanh).then_inc(s["tanh_ready"], 1)
            for k in range(2):
                act.wait_ge(s["ssd_conv_done"], 3 + k + 1)
                squares("sc", k, cmf[:, (36 + 4 * k) * T:(40 + 4 * k) * T])
            own_copies("ssd", 22)
            silu_z(0, 0, 2)
            act.wait_ge(s["spread_used"], 4)
            out_high("ssd", 0, tiles(36, 8), 4)
            act.wait_ge(s["ssd_dte_arg"], 1)
            af(tok[:, 4, :], tok[:, 4, :], ACT.Exp).then_inc(s["ssd_dte"], 1)
            for i in range(8):
                c, hq = i // 4, i % 4
                act.wait_ge(s["ssd_seg"], i + 1)
                m = hnTf[:, (i % 2) * 512:(i % 2) * 512 + 512]
                if c == 1:
                    ce = hnTf[:, 1024 + (i % 2) * 512:1536 + (i % 2) * 512]
                    if i >= 6:
                        act.wait_ge(s["ssd_y"], i - 1)
                    af(ce, bank[i % 2][:], ACT.Exp)
                af(m, m, ACT.Exp).then_inc(s["ssd_exp"], 1)
            for k in range(2):
                act.wait_ge(s["ssd_yready"], k + 1)
                act.wait_ge(s["z_ready"], 2)
                if k == 0:
                    high(UNIT_BASE["ssd_out"] + UNITS)
                squares("ssd", k, cmf[:, (8 + 4 * k) * T:(12 + 4 * k) * T])
            high(UNIT_BASE["ssd_out"] + 2 * UNITS + PARTS)
            for b in range(4):
                act.wait_ge(s["spread_used"], 4 + b + 1)
                out_high("ssd", 4 + b, tiles(8 + 2 * b, 2))
            high(UNIT_BASE["ssd_out"] + 4 * UNITS)

            layer_start("moe")
            act.dma_start(cmf[:, 40 * T:44 * T], final_norm.rearrange("(a d) -> a d", a=1).to_broadcast([P, D]))\
               .then_inc(s["fnorm_loaded"], 16)
            norm_copies(1, VCOL["norm_ffn"], False)
            act.wait_ge(s["rt_arg"], 1)
            for t in range(NT):
                af(r_eg[:, t, :], r_lg[:, t, 0:NG], ACT.Exp, bias=r_n[:, t, 0:1], accum_out=r_gs[:, t, :])
                x = af(r_ex[:, t, :], r_es[:, t, :], ACT.Exp, bias=r_n[:, t, 1:2])
            x.then_inc(s["rt_exp"], 1)

            def act_quad(it, used, base):
                act.wait_ge(used, base + STEPS_UP)
                af(m_tanh, bank[0][:], ACT.Tanh, scale=0.5).then_inc(s["moe_tanh"], 1)
                act.wait_ge(s["moe_gt"], it + 1)
                af(m_gt, bank[7][:, 0:T], ACT.Copy).then_inc(s["moe_gtc"], 1)
                act.wait_ge(s["moe_ht"], it + 1)
                af(m_ht, bank[2][:], ACT.Copy, scale=0.5).then_inc(s["moe_htc"], 1)
                act.wait_ge(used, base + MOE_STEPS)
                af(m_y[:, 0, :], bank[3][:], ACT.Copy).then_inc(s["moe_ya"], 1)

            for name in ("moe_gtc", "moe_htc"):
                act.sem_inc(s[name], 1)
            with act.Fori(0, NQ) as q:
                act_quad(q, s["ring_used"], q * MOE_STEPS)
            act.wait_ge(s["rt_passes"], 1)
            passes = act.value_load(count_i[0:1, 0:1], min_val=1, max_val=T // CAP)
            with act.If(passes > 1):
                with act.Fori(1, passes) as p:
                    with act.Fori(0, NQ) as q:
                        act_quad(p * NQ + q, ov_used, (p - 1) * (NQ * MOE_STEPS) + q * MOE_STEPS)
            act.wait_ge(s["moe_done"], 1)
            for t in range(NT):
                af(hn[:, t, :], x_res[:, t, :], ACT.Square, accum_out=ss[:, t:t + 1]).then_inc(s["ss_ready"], 1)

            def fox(occ, li, name):
                u = NORMS.index(name)
                layer_start(name)
                norm_copies(u, VCOL["norm_w"] + 8 * (0 if occ == 0 else 3))
                softplus_row(SOFT_USE[name], rows[:, 1, :], rows[:, 2, :], 8)
                for b in range(8):
                    copy_bank(name, b, cmf[:, 2 * b * T:(2 * b + 2) * T])
                    if b % 2:
                        own_copies(name, b + 1)
                        squares(name, b // 2, cmf[:, (2 * b - 2) * T:(2 * b + 2) * T])
                for b in range(4):
                    copy_bank(name, 8 + b, vtm[:, b % 2, (b // 2) * BLK:(b // 2 + 1) * BLK])
                for b in range(4):
                    copy_bank(name, 12 + b, cmf[:, (16 + 2 * b) * T:(18 + 2 * b) * T], 0.5)
                own_copies(name, 16)
                silu_z(li, 16, ROWN[name][1] // 4 + 4)

                def exponentials(h):
                    act.wait_ge(s["fox_l"], occ * FOX_H + h + 1)
                    for t, (a, b) in enumerate(((0, P), (P, 3 * P))):
                        i = af(f_p[h % 2][:, a:b], f_l[h % 2][:, a:b], ACT.Exp, bias=f_n[:, h % 2, t:t + 1],
                               accum_out=f_s[:, h % 2, t:t + 1])
                    i.then_inc(s["fox_e"], 1)

                exponentials(0)
                for h in range(FOX_H):
                    k = occ * FOX_H + h
                    if h < FOX_H - 1:
                        exponentials(h + 1)
                    act.wait_ge(s["fox_t"], k + 1)
                    af(f_pt[h % 2], bank[2 + h % 2][:, 0:3 * P], ACT.Copy).then_inc(s["fox_tc"], 1)
                    if h >= 2 and h % 2 == 0:
                        act.wait_ge(s["fox_oc"], k)
                        out_high(name, h // 2 - 1, tiles(14 + h, 2))
                act.wait_ge(s["fox_oc"], (occ + 1) * FOX_H)
                out_high(name, 3, tiles(22, 2))
                high(UNIT_BASE[name + "_out"] + 2 * UNITS)

            def gla():
                layer_start("gla")
                norm_copies(NORMS.index("gla"), VCOL["norm_w"] + 8)
                for b in range(4):
                    copy_bank("gla", b, cmf[:, 2 * b * T:(2 * b + 2) * T])
                    if b == 2:
                        act.wait_ge(s["gla_arg"], 1)
                        link(af(tf(20, 4), tf(20, 4), ACT.Exp, scale=-1.0))
                        af(tf(20, 4), tf(20, 4), ACT.Ln, bias=1.0).then_inc(s["gla_ln"], 1)
                for b in range(4):
                    copy_bank("gla", 4 + b, vtm[:, b % 2, (b // 2) * BLK:(b // 2 + 1) * BLK])
                    if b:
                        act.wait_ge(s["gla_dec"], 1)
                        dst, src, scale = ((20, 16, 1.0), (24, 16, -1.0), (28, 28, 1.0))[b - 1]
                        af(tf(dst, 4), tf(src, 4), ACT.Exp, scale=scale / 16).then_inc(s["gla_exp"], 1)
                for b in range(4):
                    copy_bank("gla", 8 + b, cmf[:, (8 + 2 * b) * T:(10 + 2 * b) * T], 0.5)
                own_copies("gla", 12)
                silu_z(2, 8, ROWN["fox0"][1] // 4 + 4)
                act.wait_ge(s["gla_kt"], 1)
                for k in (0, 1):
                    i = af(tf(40 + 2 * k, 2), bank[2 + k][:], ACT.Copy)
                i.then_inc(s["gla_ktc"], 1)
                act.wait_ge(s["z_ready"], 6)
                for k in range(2):
                    act.wait_ge(s["gla_oc"], 2 * k + 2)
                    squares("gla", k, tf(32 + 4 * k, 4))
                for b in range(4):
                    act.wait_ge(s["spread_used"], ROWN["gla"][1] // 2 + b + 1)
                    out_high("gla", b, tiles(8 + 2 * b, 2))
                high(UNIT_BASE["gla_out"] + 2 * UNITS)

            def gdn():
                layer_start("gdn")
                norm_copies(NORMS.index("gdn"), VCOL["norm_w"] + 16)
                softplus_row(SOFT_USE["gdn"], rows[:, 1, :], rows[:, 2, :], 8)
                act.wait_ge(s["gdn_row_free"], 1)
                af(rows[0:8, 0], bank[5][0:8, T:2 * T], ACT.Exp, scale=-1.0).then_inc(s["gdn_beta_exp"], 1)
                for b in range(12):
                    copy_bank("gdn", b, tf(2 * b, 2), 0.5 if b >= 8 else 1.0)
                    if b in (4, 6, 8, 10):
                        k = (b - 4) // 2
                        act.wait_ge(s["lin_ready"], 3 + k + 1)
                        af(vtm[:, 1, :], vtm[:, 0, :], ACT.Tanh).then_inc(s["tanh_ready"], 1)
                        if 1 <= k <= 2:
                            act.wait_ge(s["gdn_conv_done"], k)
                            squares("gdn_qk", k - 1, tf(4 * (k - 1), 4))
                own_copies("gdn", 12)
                silu_z(3, 16, ROWN["gdn_qk"][1] // 4 + 2)
                act.wait_ge(s["gdn_col_arg"], 1)
                af(tok[:, 4:6, 0:8], tok[:, 4:6, 0:8], ACT.Exp).then_inc(s["gdn_col_exp"], 1)
                for c in range(NT):
                    for hf in (0, 1):
                        act.wait_ge(s["gdn_arg"], 2 * c + hf + 1)
                        if c == 1:
                            af(g_qd[hf], bank[g_banks[hf][0]][:], ACT.Exp)
                        af(g_dt[hf], g_dt[hf], ACT.Exp)
                        af(g_d[hf], g_d[hf], ACT.Exp, scale=-1.0).then_inc(s["gdn_exp"], 1)
                    for hf in (0, 1):
                        act.wait_ge(s["gdn_turned"], 2 * c + hf + 1)
                        af(g_Q[hf], bank[g_banks[hf][3]][:], ACT.Copy).then_inc(s["gdn_q_ready"], 1)
                    for j in range(5):
                        for hf in (0, 1):
                            act.wait_ge(s["gdn_power"], 12 * c + 2 * j + hf + 1)
                            if j == 0:
                                act.wait_ge(s["gdn_r_ready"], 14 * c + hf + 1)
                            af(g_Q[hf], bank[g_banks[hf][3]][:], ACT.Copy).then_inc(s["gdn_q_ready"], 1)
                    for hf in (0, 1):
                        act.wait_ge(s["gdn_uw"], 2 * c + hf + 1)
                        af(g_u[2 * c + hf], bank[g_banks[hf][3]][:], ACT.Copy).then_inc(s["gdn_u_ready"], 1)
                act.wait_ge(s["z_ready"], 8)
                for k in range(2):
                    act.wait_ge(s["gdn_oc"], 2 * k + 2)
                    squares("gdn_o", k, tf(4 * k, 4))
                for b in range(4):
                    act.wait_ge(s["spread_used"], ROWN["gdn_o"][1] // 2 + b + 1)
                    out_high("gdn", b, tiles(16 + 2 * b, 2))
                high(UNIT_BASE["gdn_out"] + 2 * UNITS)

            fox(0, 1, "fox0")
            gla()
            gdn()
            fox(1, 4, "fox1")

        @block.vector
        def _(dve):
            v = nc.vector
            n_link = [0]

            def link(ins):
                n_link[0] += 1
                ins.then_inc(s["dve_chain"], 1)
                dve.wait_ge(s["dve_chain"], n_link[0])

            def inverse_root(dst, x, t, done=None):
                link(v.tensor_scalar(dst.bitcast(I32), x.bitcast(I32), -0.5, RSQRT_SEED, ALU.mult, ALU.add))
                for k in range(3):
                    link(v.tensor_tensor(t, dst, dst, ALU.mult))
                    link(v.scalar_tensor_tensor(out=t, in0=t, scalar=-0.5, in1=x, op0=ALU.mult, op1=ALU.mult))
                    i = v.scalar_tensor_tensor(out=dst, in0=t, scalar=1.5, in1=dst, op0=ALU.add, op1=ALU.mult)
                    if k == 2 and done is not None:
                        i.then_inc(done[0], 1)
                        dve.wait_ge(done[0], done[1])
                    else:
                        link(i)

            def token_scale(name):
                if name == "fox0":
                    link(v.tensor_tensor(ss[:, 6:8], ss[:, 4:6], ss[:, 4:6], ALU.mult))
                    dve.wait_ge(s["ss_ready"], SQ_BEFORE[name] + 2)
                    link(v.scalar_tensor_tensor(out=ss[:, 2:4], in0=ss[:, 8:10], scalar=1.0 / D, in1=ss[:, 6:8],
                                                op0=ALU.mult, op1=ALU.mult))
                    link(v.tensor_scalar(ss[:, 2:4], ss[:, 2:4], EPS, None, ALU.add))
                    inverse_root(ss[:, 8:10], ss[:, 2:4], ss[:, 6:8])
                    link(v.tensor_tensor(ss[:, 4:6], ss[:, 4:6], ss[:, 8:10], ALU.mult))
                    return
                if name in HALVED:
                    dve.wait_ge(s["ss_ready"], SQ_BEFORE[name] + 4)
                    link(v.scalar_tensor_tensor(out=ss[:, 2:4], in0=ss[:, 0:2], scalar=1.0 / D, in1=ss[:, 10:12],
                                                op0=ALU.mult, op1=ALU.add))
                else:
                    dve.wait_ge(s["ss_ready"], SQ_BEFORE[name] + 2)
                    link(v.tensor_scalar(ss[:, 2:4], ss[:, 0:2], 1.0 / D, EPS, ALU.mult, ALU.add))
                inverse_root(ss[:, 4:6], ss[:, 2:4], ss[:, 6:8])

            def out_low(name, pair, src, n=1):
                k = 2 * (pair % 4)
                dve.wait_ge(s["out_high"], PAIR_BASE[name] + pair + n)
                v.tensor_tensor(hnT_l[:, k:k + 2 * n, :], src, hnT_h[:, k:k + 2 * n, :].bitcast(F32),
                                ALU.subtract).then_inc(s["out_low"], n)

            def moe_norm(col):
                u = NORMS.index("moe")
                for b, src in ((1, 7), (3, 0)):
                    dve.wait_ge(s["turned"], 4 * u + b + 1)
                    for j in (0, 1):
                        i = v.tensor_scalar(hnT[:, 2 * b + j, :], b2(src)[:, j, :],
                                            vec[:, col + 2 * b + j:col + 2 * b + j + 1], None, ALU.mult)
                    i.then_inc(s["hnT_dve"], 1)
                token_scale("moe")
                for t in range(NT):
                    v.tensor_scalar(hn[:, t, :], x_res[:, t, :], ss[:, 4 + t:5 + t], None,
                                    ALU.mult).then_inc(s["xn_ready"], 1)

            def norm(name, col):
                u = NORMS.index(name)
                token_scale(name)
                for t in range(NT):
                    src = vtm if name == "fox0" else x_res
                    v.tensor_scalar(hn[:, t, :], src[:, t, :], ss[:, 4 + t:5 + t], None,
                                    ALU.mult).then_inc(s["xn_ready"], 1)
                for b in (1, 3):
                    dve.wait_ge(s["turned"], 4 * u + b + 1)
                    for j in (0, 1):
                        i = v.tensor_scalar(hnT[:, 2 * b + j, :], b2(7)[:, j, :],
                                            vec[:, col + 2 * b + j:col + 2 * b + j + 1], None, ALU.mult)
                    i.then_inc(s["hnT_dve"], 1)
                    w = SPLIT_NORMS.index(name)
                    dve.wait_ge(s["hnT_dve"], 2 * u + b // 2 + 1)
                    v.tensor_copy(hnT_h[:, 2 * b:2 * b + 2, :], hnT[:, 2 * b:2 * b + 2, :]).then_inc(s["hnT_own"], 1)
                    dve.wait_ge(s["hnT_own"], 2 * w + b // 2 + 1)
                    dve.wait_ge(s["hnT_high"], 2 * w + b // 2 + 1)
                    c = slice(2 * b - 2, 2 * b + 2)
                    v.tensor_tensor(hnT_l[:, c, :], hnT[:, c, :], hnT_h[:, c, :].bitcast(F32),
                                    ALU.subtract).then_inc(s["hnT_split"], 1)

            def row_roots(name, R, scale):
                r, before, n = ROWN[name]
                dve.wait_ge(s["sq_summed"], (before + n) // 4)
                n = NT * R
                link(v.tensor_scalar(heads[:, 0, 0:n], bank[SUM_BANK][:, 0:n], scale, EPS, ALU.mult, ALU.add))
                inverse_root(heads[:, 1, 0:n], heads[:, 0, 0:n], heads[:, 2, 0:n], (s["rownorm_ready"], r + 1))

            def rownorm(name, R, scale, use, split=None, roots=True):
                if roots:
                    row_roots(name, R, scale)
                _, before, n = ROWN[name]
                share = SHARE.get(name, 1)
                for b in range(n // 2):
                    g = SPREAD_BASE[name] + b // share
                    dve.wait_ge(s["spread_done"], g + 1)
                    for j in (0, 1):
                        i = 2 * b + j
                        x = use(i, b2(6 + g % 2)[:, (i // share) % 2, :])
                    x.then_inc(s["spread_used"], 1)
                    if split and b:
                        out_low(split[0], split[1] + b - 1, tiles(split[2] + 2 * b - 2, 2))
                if split:
                    out_low(split[0], split[1] + n // 2 - 1, tiles(split[2] + n - 2, 2))
                dve.wait_ge(s["spread_used"], (before + n) // 2)

            def add_projection(li):
                done = UNIT_BASE[LAYERS[li] + "_out"] + 2 * UNITS * (OUT_GROUPS[LAYERS[li]] - 1)
                following = ["moe", "gla", "gdn", "fox1", None][li]
                for k in range(4):
                    n, t = k // 2, k % 2
                    if k == 2 and following:
                        dve.wait_ge(s["ss_ready"], SQ_BEFORE[following] + 2)
                        link(v.tensor_scalar(ss[:, 10:12], ss[:, 8:10], 1.0 / D, EPS, ALU.mult, ALU.add))
                    dve.wait_ge(s["unit_done"], done + UNITS * (n + 1))
                    dst = x_res[:, t, n * BLK:(n + 1) * BLK]
                    v.tensor_tensor(dst, bank[t + 2 * n][:], dst, ALU.add).then_inc(s["x_ready"], 1)

            def silu_z(li, z0):
                for b in (0, 1):
                    dve.wait_ge(s["z_tanh"], 2 * li + b + 1)
                    z = tf(z0 + 4 * b, 4)
                    v.scalar_tensor_tensor(out=z, in0=sq[:, b].rearrange("p a b -> p (a b)"), scalar=1.0, in1=z,
                                           op0=ALU.add, op1=ALU.mult).then_inc(s["z_ready"], 1)
                dve.wait_ge(s["z_ready"], 2 * li + 2)

            def conv(src, dst, weights, stride, taps, bias=None):
                n = len(src)
                for d in range(taps):
                    tap = taps - 1 - d
                    for i in range(n):
                        w = vec[:, weights + stride * tap + i:weights + stride * tap + i + 1]
                        if d == 0 and bias is None:
                            x = v.tensor_scalar(dst[i], src[i], w, None, ALU.mult)
                        elif d == 0:
                            x = v.tensor_scalar(dst[i], src[i], w, vec[:, bias + i:bias + i + 1], ALU.mult, ALU.add)
                        else:
                            x = v.scalar_tensor_tensor(out=dst[i][:, d:T], in0=src[i][:, 0:T - d], scalar=w,
                                                       in1=dst[i][:, d:T], op0=ALU.mult, op1=ALU.add)
                    if d < taps - 1:
                        link(x)
                return x

            def conv_silu(k, t0, weights, stride, bias, done):
                lin = [vtm[:, 0, i * T:(i + 1) * T] for i in range(4)]
                conv([cm[:, t0 + i, :] for i in range(4)], lin, weights, stride, 4, bias).then_inc(s["lin_ready"], 1)
                dve.wait_ge(s["lin_ready"], k + 1)
                dve.wait_ge(s["tanh_ready"], k + 1)
                v.scalar_tensor_tensor(out=tf(t0, 4), in0=vtm[:, 1, :], scalar=1.0, in1=vtm[:, 0, :],
                                       op0=ALU.add, op1=ALU.mult).then_inc(done[0], 1)
                dve.wait_ge(*done)

            dve.wait_ge(s["vec_turned"], 2)
            v.tensor_copy(vec[:, 0:NA], bank[5][:, 0:NA])
            link(v.tensor_copy(vec[:, P:P + NB], bank[5][:, P:P + NB]))
            v.tensor_scalar(vec[:, 0:60], vec[:, 0:60], 0.5, None, ALU.mult)
            v.tensor_scalar(vec[:, P + 32:P + 96], vec[:, P + 32:P + 96], 0.5, None, ALU.mult).then_inc(s["vec_ready"], 1)
            dve.wait_ge(s["vec_ready"], 1)
            norm("ssd", VCOL["norm_mix"])
            dve.wait_ge(s["cols_ready"], 1)
            v.tensor_scalar(ncols[0:16, 0:1], ncols[0:16, 0:1], -1.0, None, ALU.mult)
            link(v.tensor_scalar(ncols[0:8, 1:2], ncols[0:8, 1:2], -1.0, None, ALU.mult))

            def softplus_args(k, R, src, bias, sign):
                link(v.tensor_scalar(rows[0:R, 0], src, bias, sign, ALU.add, ALU.mult))
                v.scalar_tensor_tensor(out=rows[0:R, 1], in0=rows[0:R, 0], scalar=-1.0, in1=rows[0:R, 0],
                                       op0=ALU.mult, op1=ALU.max).then_inc(s["row_arg"], 1)
                dve.wait_ge(s["row_ln"], k)

            def softplus_tail(R, dst):
                link(v.scalar_tensor_tensor(out=dst, in0=rows[0:R, 0], scalar=0.0, in1=rows[0:R, 2],
                                            op0=ALU.max, op1=ALU.add))

            dve.wait_ge(s["small_done"], 1)
            dve.wait_ge(s["consts_ready"], 1)
            softplus_args(1, 16, bank[5][0:16, 0:T], cols[0:16, 1:2], 1.0)
            softplus_tail(16, rows[0:16, 3])
            link(v.tensor_scalar(rows[0:16, 1], rows[0:16, 3], ncols[0:16, 0:1], None, ALU.mult))
            for c in range(NT):
                x = v.tensor_tensor_scan(rows[0:16, 2, c * P:(c + 1) * P], ones[0:16, :], rows[0:16, 1, c * P:(c + 1) * P],
                                         0.0, ALU.mult, ALU.add)
            x.then_inc(s["row_ready"], 1)
            dve.wait_ge(s["row_turned"], 1)
            v.tensor_copy(tok[:, 0:4, :], bank[5][:, T:T + 64].rearrange("p (a b) -> p a b", a=4)).then_inc(s["col_ready"], 1)
            dve.wait_ge(s["col_ready"], 1)

            for k in range(3):
                dve.wait_ge(s["proj_copied"], 2 * k + 2)
                conv_silu(k, 8 + 4 * k, VCOL["ssd_conv_w"] + 4 * k, 12, VCOL["ssd_conv_b"] + 4 * k,
                          (s["ssd_conv_done"], k + 1))
            for k in range(2):
                dve.wait_ge(s["proj_copied"], 10 + 2 * k + 2)
                link(v.tensor_tensor(tf(28 + 4 * k, 4), tf(28 + 4 * k, 4), tf(36 + 4 * k, 4), ALU.mult))
                dve.wait_ge(s["proj_copied"], 14 + 2 * k + 2)
                link(conv([cm[:, 28 + 4 * k + i, :] for i in range(4)], [cm[:, 36 + 4 * k + i, :] for i in range(4)],
                          VCOL["sc_conv_w"] + 4 * k, 8, 3))
                v.tensor_tensor(tf(36 + 4 * k, 4), tf(36 + 4 * k, 4), tf(20 + 4 * k, 4),
                                ALU.mult).then_inc(s["ssd_conv_done"], 1)
                dve.wait_ge(s["ssd_conv_done"], 3 + k + 1)

            def sc_out(i, spread):
                return v.scalar_tensor_tensor(out=cm[:, 36 + i, :], in0=spread, scalar=vec[:, VCOL["sc_norm"] + i:VCOL["sc_norm"] + i + 1],
                                              in1=cm[:, 36 + i, :], op0=ALU.mult, op1=ALU.mult)

            xdt = vtm
            for k in range(4):
                c, hf = k // 2, k % 2
                dve.wait_ge(s["ssd_xt_done"], k + 1)
                dst = xdt[:, c, hf * BLK:(hf + 1) * BLK].rearrange("p (h d) -> p h d", d=64)
                dtc = tok[:, 2 + c, 8 * hf:8 * hf + 8].unsqueeze(2).to_broadcast([P, 8, 64])
                v.tensor_tensor(dst, bank[k % 2][:].rearrange("p (h d) -> p h d", d=64), dtc,
                                ALU.mult).then_inc(s["ssd_xt_used"], 1)
                if k == 1:
                    row_roots("sc", 16, 1.0 / 64)
            rownorm("sc", 16, 1.0 / 64, sc_out, roots=False)
            dve.wait_ge(s["ssd_xt_used"], 4)
            dve.wait_ge(s["ssd_g_done"], 1)
            v.tensor_tensor(tok[:, 4, :], bank[3][:, 2 * P:2 * P + 16], tok[:, 0, :], ALU.subtract).then_inc(s["ssd_dte_arg"], 1)
            v.tensor_copy(tiles(30, 1, P)[:, :, :], b4(3)[:, 0:2, :])
            for j in range(4):
                x = v.tensor_tensor(tf(28, 2)[:, j * P:(j + 1) * P], b4(2)[:, j, :], upper[:], ALU.mult)
            link(x)
            dve.wait_ge(s["ssd_dte"], 1)
            v.tensor_tensor(hn[:, 0, :].rearrange("p (h d) -> p h d", d=64), xdt[:, 0, :].rearrange("p (h d) -> p h d", d=64),
                            tok[:, 4, :].unsqueeze(2).to_broadcast([P, 16, 64]), ALU.mult).then_inc(s["ssd_xdte"], 1)
            silu_z(0, 0)
            out_low("ssd", 0, tiles(36, 8), 4)
            dve.wait_ge(s["ssd_state"], 1)
            for g in range(2):
                x = v.tensor_copy(hn[:, 1, g * BLK:(g + 1) * BLK], bank[g + 6][:])
            x.then_inc(s["ssd_state_used"], 1)
            for i in range(8):
                c, hq = i // 4, i % 4
                g = hq // 2
                m = hnTf[:, (i % 2) * 512:(i % 2) * 512 + 512]
                dve.wait_ge(s["ssd_bc"], i + 1)
                if i >= 2:
                    dve.wait_ge(s["ssd_y"], i - 1)
                for j in range(4):
                    h = 4 * hq + j
                    x = v.tensor_scalar(m[:, j * P:(j + 1) * P], b4(i % 2)[:, j, :], tok[:, c, h:h + 1], 0.0,
                                        ALU.subtract, ALU.min)
                x.then_inc(s["ssd_seg"], 1)
                dve.wait_ge(s["ssd_exp"], i + 1)
                m4 = m.rearrange("p (a b) -> p a b", b=P)
                gm = tf(28, 2)[:, (2 * c + g) * P:(2 * c + g + 1) * P].unsqueeze(1).to_broadcast([P, 4, P])
                if c == 1:
                    ce = hnTf[:, 1024 + (i % 2) * 512:1536 + (i % 2) * 512].rearrange("p (a b) -> p a b", b=P)
                    v.tensor_tensor(ce, ce, cm[:, 18 + g, P:T].unsqueeze(1).to_broadcast([P, 4, P]), ALU.mult)
                v.tensor_tensor(m4, m4, gm, ALU.mult).then_inc(s["ssd_m"], 1)
            for k in range(2):
                dve.wait_ge(s["ssd_y"], 4 + 2 * k + 2)
                for i in range(4 * k, 4 * k + 4):
                    x = v.scalar_tensor_tensor(out=cm[:, 8 + i, :], in0=cm[:, 8 + i, :], scalar=dsk[:, i:i + 1],
                                               in1=b2(2 + i // 2)[:, i % 2, :], op0=ALU.mult, op1=ALU.add)
                link(x)
                v.tensor_tensor(tf(8 + 4 * k, 4), tf(8 + 4 * k, 4), tf(4 * k, 4), ALU.mult).then_inc(s["ssd_yready"], 1)
                dve.wait_ge(s["ssd_yready"], k + 1)

            def ssd_out(i, spread):
                return v.scalar_tensor_tensor(out=cm[:, 8 + i, :], in0=spread, scalar=vec[:, VCOL["ssd_norm"] + i:VCOL["ssd_norm"] + i + 1],
                                              in1=cm[:, 8 + i, :], op0=ALU.mult, op1=ALU.mult)

            rownorm("ssd", 2, 1.0 / BLK, ssd_out, ("ssd", 4, 8))
            add_projection(0)

            moe_norm(VCOL["norm_ffn"])
            dve.wait_ge(s["rt_done"], 1)
            for t in range(NT):
                x = v.tensor_scalar(r_lg[:, t, :], bank[5][:, t * (NG + NE):(t + 1) * (NG + NE)], ss[:, 4 + t:5 + t],
                                    None, ALU.mult)
            link(x)

            def rank(x, n, limit, dst):
                c1, c2 = (c[:, 0:NT * n * n].rearrange("p (t i j) -> p t i j", t=NT, i=n) for c in (r_c1, r_c2))
                other = x.unsqueeze(2).to_broadcast([P, NT, n, n])
                own = x.unsqueeze(3).to_broadcast([P, NT, n, n])
                v.tensor_tensor(c1, other, own, ALU.is_gt)
                link(v.tensor_tensor(c2, other, own, ALU.is_equal))
                link(v.tensor_tensor(c2, c2, earlier[:, 0:n, 0:n].unsqueeze(1).to_broadcast([P, NT, n, n]), ALU.mult))
                link(v.tensor_tensor(c1, c1, c2, ALU.add))
                link(v.tensor_reduce(dst, c1, AX.X, ALU.add))
                link(v.tensor_scalar(dst, dst, limit - 0.5, None, ALU.is_lt))

            gl, el = r_lg[:, :, 0:NG], r_lg[:, :, NG:NG + NE].rearrange("p t (g e) -> p t g e", g=NG)
            grid = [P, NT, NG, EPG]
            rank(gl, NG, 1, r_gsel)
            in_group = r_gsel.unsqueeze(3).to_broadcast(grid)
            v.tensor_reduce(r_n[:, :, 0:1], gl, AX.X, ALU.max, negate=True)
            link(v.tensor_tensor(r_prod, el, in_group, ALU.mult))
            link(v.tensor_reduce(r_es, r_prod.rearrange("p t g e -> p t e g"), AX.X, ALU.add))
            v.tensor_reduce(r_n[:, :, 1:2], r_es, AX.X, ALU.max, negate=True).then_inc(s["rt_arg"], 1)
            rank(r_es, EPG, 2, r_sel)
            v.tensor_tensor(r_mask.rearrange("p t (g e) -> p t g e", g=NG), r_sel.unsqueeze(2).to_broadcast(grid),
                            in_group, ALU.mult).then_inc(s["rt_mask"], 1)
            v.memset(r_gate, 0.0)
            link(v.memset(r_pm, -1.0))
            dve.wait_ge(s["rt_exp"], 1)
            link(v.tensor_tensor(r_ex, r_ex, r_sel, ALU.mult))
            link(v.tensor_reduce(r_sum[:, :, 0:1], r_ex, AX.X, ALU.add))
            link(v.tensor_tensor(r_sum[:, :, 1:2], r_sum[:, :, 0:1], r_gs, ALU.mult))
            link(v.reciprocal(r_sum[:, :, 2:3], r_sum[:, :, 1:2]))
            link(v.tensor_tensor(r_ex, r_ex, r_sum[:, :, 2:3].to_broadcast([P, NT, EPG]), ALU.mult))
            link(v.tensor_tensor(r_gate[:, :, 0:NE].rearrange("p t (g e) -> p t g e", g=NG),
                                 r_ex.unsqueeze(2).to_broadcast(grid), in_group, ALU.mult))
            dve.wait_ge(s["rt_mask"], 1)
            dve.wait_ge(s["rt_rank"], 1)
            pm = r_pm[:, :, 0:NE]
            link(v.scalar_tensor_tensor(out=pm, in0=bank[5][:, P:P + NT * NE].rearrange("p (t e) -> p t e", t=NT),
                                        scalar=1.0, in1=r_mask, op0=ALU.add, op1=ALU.mult))
            link(v.tensor_scalar(pm, pm, -1.0, None, ALU.add))
            link(v.tensor_reduce(r_pass[0:1, 0, 0:1], bank[5][0:1, T:T + NE], AX.X, ALU.max))
            link(v.tensor_scalar(r_pass[0:1, 1, 0:8], iota[0:1, 0:8], float(CAP), r_pass[0:1, 0, 0:1], ALU.mult, ALU.is_lt))
            link(v.tensor_reduce(r_pass[0:1, 0, 1:2], r_pass[0:1, 1, 0:8], AX.X, ALU.add))
            v.tensor_copy(count_i[0:1, 0:1], r_pass[0:1, 0, 1:2]).then_inc(s["rt_passes"], 1)

            iota4 = iota[:].unsqueeze(1).to_broadcast([P, QUAD, CAP])

            def select_tokens(q):
                for t in range(NT):
                    place = r_pm[:, t, bass.ds(q * QUAD, QUAD)].unsqueeze(2).to_broadcast([P, QUAD, CAP])
                    x = v.tensor_tensor(m_S[:, t, :].rearrange("p (e c) -> p e c", e=QUAD), iota4, place, ALU.is_equal)
                x.then_inc(s["moe_sel"], 1)

            def gathered(g):
                dve.wait_ge(s["moe_gath"], g + 1)
                for half in (0, 1):
                    gain = vec[:, VCOL["norm_ffn"] + 4 * half:VCOL["norm_ffn"] + 4 * half + 4]
                    x = v.tensor_tensor(m_xg[:, 4 * half:4 * half + 4, :], b4(5 + half)[:],
                                        gain.unsqueeze(2).to_broadcast([P, 4, P]), ALU.mult)
                x.then_inc(s["moe_xg"], 1)

            def dve_quad(q, it, g):
                dve.wait_ge(s["moe_sel"], g + 1)
                for t in range(NT):
                    gate = r_gate[:, t, bass.ds(q * QUAD, QUAD)].unsqueeze(2).to_broadcast([P, QUAD, CAP])
                    x = v.tensor_tensor(m_SG[:, t, :].rearrange("p (e c) -> p e c", e=QUAD),
                                        m_S[:, t, :].rearrange("p (e c) -> p e c", e=QUAD), gate, ALU.mult)
                x.then_inc(s["moe_sg"], 1)
                dve.wait_ge(s["moe_sg"], it + 1)
                select_tokens(q + 1)
                dve.wait_ge(s["moe_tanh"], it + 1)
                v.scalar_tensor_tensor(out=m_silu, in0=m_tanh, scalar=1.0, in1=bank[0][:], op0=ALU.add,
                                       op1=ALU.mult).then_inc(s["moe_chain"], 1)
                dve.wait_ge(s["moe_chain"], it + 1)
                v.tensor_tensor(m_h, m_silu, bank[1][:], ALU.mult).then_inc(s["moe_h"], 1)
                gathered(g + 1)
                return

            def dve_quad_end(it, used, base):
                dve.wait_ge(used, base + MOE_STEPS)
                v.tensor_copy(m_y[:, 1, :], bank[4][:]).then_inc(s["moe_yd"], 1)
                dve.wait_ge(s["moe_scat"], it + 1)
                for k in range(4):
                    t, n = k // 2, k % 2
                    dst = x_res[:, t, n * BLK:(n + 1) * BLK]
                    x = v.tensor_tensor(dst, bank[[5, 6, 3, 4][k]][:], dst, ALU.add)
                x.then_inc(s["moe_acc"], 1)

            dve.sem_inc(s["moe_h"], 1)
            dve.sem_inc(s["moe_acc"], 1)
            dve.wait_ge(s["rt_passes"], 1)
            select_tokens(0)
            gathered(0)
            with dve.Fori(0, NQ) as q:
                dve_quad(q, q, q)
                dve_quad_end(q, s["ring_used"], q * MOE_STEPS)
            passes = dve.value_load(count_i[0:1, 0:1], min_val=1, max_val=T // CAP)
            with dve.If(passes > 1):
                with dve.Fori(1, passes) as p:
                    for t in range(NT):
                        x = v.tensor_scalar(r_pm[:, t, :], r_pm[:, t, :], -float(CAP), None, ALU.add)
                    x.then_inc(s["pass_chain"], 1)
                    dve.wait_ge(s["pass_chain"], p)
                    select_tokens(0)
                    gathered(p * (NQ + 1))
                    with dve.Fori(0, NQ) as q:
                        dve_quad(q, p * NQ + q, p * (NQ + 1) + q)
                        dve_quad_end(p * NQ + q, ov_used, (p - 1) * (NQ * MOE_STEPS) + q * MOE_STEPS)
            v.drain().then_inc(s["moe_done"], 1)
            dve.wait_ge(s["fnorm_loaded"], 16)
            for t in range(NT):
                v.tensor_tensor(vtm[:, t, :], x_res[:, t, :], tf(40, 4), ALU.mult).then_inc(s["gained"], 1)
            token_scale("final")
            dve.wait_ge(s["gained"], NT)
            for t in range(NT):
                v.tensor_scalar(x_res[:, t, :], vtm[:, t, :], ss[:, 4 + t:5 + t], None, ALU.mult).then_inc(s["x_ready"], 1)
            dve.wait_ge(s["x_ready"], X_BEFORE["fox0"])

            def fox(occ, li, name):
                norm(name, VCOL["norm_w"] + 8 * (0 if occ == 0 else 3))
                dve.wait_ge(s["small_done"], li + 1)
                softplus_args(SOFT_USE[name], FOX_H, bank[5][0:FOX_H, 0:T], cols[0:FOX_H, 2 + occ:3 + occ], -1.0)
                softplus_tail(FOX_H, rows[0:FOX_H, 1])
                link(v.tensor_tensor_scan(rows[0:FOX_H, 3], ones[0:FOX_H, 0:1].to_broadcast([FOX_H, T]), rows[0:FOX_H, 1], 0.0, ALU.mult, ALU.subtract))
                v.tensor_scalar(rows[0:FOX_H, 2], rows[0:FOX_H, 3], -1.0, None, ALU.mult).then_inc(s["row_ready"], 1)
                dve.wait_ge(s["row_turned"], ROW_USE[name])
                link(v.tensor_copy(tok[:, 5:7, 0:FOX_H], bank[5][:, T:T + 16].rearrange("p (a b) -> p a b", a=2)))

                def qk_out(i, spread):
                    gain = VCOL["fox_q_gain"] + occ if i < 8 else VCOL["fox_k_gain"] + occ
                    if i < 8:
                        return v.scalar_tensor_tensor(out=cm[:, i, :], in0=spread, scalar=qgain[:, 0:1], in1=cm[:, i, :],
                                                      op0=ALU.mult, op1=ALU.mult)
                    return v.scalar_tensor_tensor(out=cm[:, i, :], in0=spread, scalar=vec[:, gain:gain + 1], in1=cm[:, i, :],
                                                  op0=ALU.mult, op1=ALU.mult)

                qcol = VCOL["fox_q_gain"] + occ
                link(v.tensor_scalar(qgain[:, 0:1], vec[:, qcol:qcol + 1], float(P) ** -0.5, None, ALU.mult))
                rownorm(name, 16, 1.0 / P, qk_out)
                dve.sem_inc(s["qk_ready"], 1)
                silu_z(li, 16)

                def logits(h):
                    dve.wait_ge(s["fox_s"], occ * FOX_H + h + 1)
                    src = bank[f_banks[h % 3]]
                    v.scalar_tensor_tensor(out=f_l[h % 2][:, 0:P], in0=src[:, 0:P], scalar=tok[:, 5, h:h + 1],
                                           in1=negmask[:, 1, :], op0=ALU.add, op1=ALU.add)
                    link(v.scalar_tensor_tensor(out=f_l[h % 2][:, P:3 * P], in0=src[:, P:3 * P],
                                                scalar=tok[:, 6, h:h + 1], in1=negmask[:].rearrange("p a b -> p (a b)"),
                                                op0=ALU.add, op1=ALU.add))
                    v.tensor_reduce(f_n[:, h % 2, 0:1], f_l[h % 2][:, 0:P], AX.X, ALU.max, negate=True)
                    v.tensor_reduce(f_n[:, h % 2, 1:2], f_l[h % 2][:, P:3 * P], AX.X, ALU.max,
                                    negate=True).then_inc(s["fox_l"], 1)

                logits(0)
                logits(1)
                for h in range(FOX_H + 1):
                    k = occ * FOX_H + h
                    if h < FOX_H:
                        dve.wait_ge(s["fox_e"], k + 1)
                        link(v.reciprocal(f_r[:, h % 2, :], f_s[:, h % 2, :]))
                        v.tensor_scalar(f_p[h % 2][:, 0:P], f_p[h % 2][:, 0:P], f_r[:, h % 2, 0:1], None, ALU.mult)
                        v.tensor_scalar(f_p[h % 2][:, P:3 * P], f_p[h % 2][:, P:3 * P], f_r[:, h % 2, 1:2], None,
                                        ALU.mult).then_inc(s["fox_p"], 1)
                    if h >= 1:
                        dve.wait_ge(s["fox_o"], k)
                        z = cm[:, 16 + h - 1, :]
                        v.tensor_tensor(z, bank[6 + (h - 1) % 2][:, 0:T], z, ALU.mult).then_inc(s["fox_oc"], 1)
                    if h < FOX_H - 2:
                        logits(h + 2)
                    if h >= 3 and h % 2:
                        out_low(name, (h - 3) // 2, tiles(13 + h, 2))
                out_low(name, 3, tiles(22, 2))
                add_projection(li)

            def ones_free(R, n):
                return ones[0:R, 0:1].to_broadcast([R, n])

            def gla():
                norm("gla", VCOL["norm_w"] + 8)
                dve.wait_ge(s["small_done"], 3)
                v.tensor_copy(rows[0:16, 0], bank[5][0:16, 0:T]).then_inc(s["gla_low"], 1)
                dve.wait_ge(s["gla_gate"], 1)
                for h in range(GLA_H):
                    x = v.tensor_scalar(cm[:, 16 + h, :], b2(4 + h // 2)[:, h % 2, :],
                                        vec[:, VCOL["gla_b_gate"] + h:VCOL["gla_b_gate"] + h + 1], -1.0, ALU.add, ALU.mult)
                link(x)
                v.scalar_tensor_tensor(out=tf(20, 4), in0=tf(16, 4), scalar=-1.0, in1=tf(16, 4), op0=ALU.mult,
                                       op1=ALU.max).then_inc(s["gla_arg"], 1)
                dve.wait_ge(s["gla_ln"], 1)
                link(v.scalar_tensor_tensor(out=tf(20, 4), in0=tf(16, 4), scalar=0.0, in1=tf(20, 4), op0=ALU.max,
                                            op1=ALU.add))
                for k in range(GLA_H * T // GLA_CH):
                    x = v.tensor_tensor_scan(tf(16, 4)[:, k * 64:(k + 1) * 64], ones[:, 0:64], tf(20, 4)[:, k * 64:(k + 1) * 64],
                                             0.0, ALU.mult, ALU.subtract)
                link(x)
                cum = tiles(16, 4, 64)
                v.tensor_tensor(tiles(28, 4, 64), cum[:, :, 63:64].to_broadcast([P, 16, 64]), cum,
                                ALU.subtract).then_inc(s["gla_dec"], 1)
                dve.wait_ge(s["gla_exp"], 3)
                dve.wait_ge(s["proj_copied"], PROJ_BASE["gla"] + 4)
                v.scalar_tensor_tensor(out=tf(0, 4), in0=tf(0, 4), scalar=float(GLA_DK) ** -0.5, in1=tf(20, 4),
                                       op0=ALU.mult, op1=ALU.mult)
                link(v.tensor_tensor(tf(28, 4), tf(4, 4), tf(28, 4), ALU.mult))
                v.tensor_tensor(tf(4, 4), tf(4, 4), tf(24, 4), ALU.mult).then_inc(s["gla_qk"], 1)
                silu_z(2, 8)
                dve.wait_ge(s["gla_qk"], 1)
                dve.wait_ge(s["gla_at"], 1)
                for k in (0, 1):
                    x = v.tensor_tensor(tiles(24 + 2 * k, 2, P), b4(k), upper64[:].unsqueeze(1).to_broadcast([P, 4, P]),
                                        ALU.mult)
                x.then_inc(s["gla_atc"], 1)
                for c in range(3):
                    state, before = gla_states[c % 2], gla_states[(c + 1) % 2]
                    dve.wait_ge(s["gla_st"], c + 1)
                    if c:
                        dve.wait_ge(s["gla_stc"], c)
                    for h in range(GLA_H):
                        new = b2(2 * (c % 2) + h // 2)[:, h % 2, :]
                        if c == 0:
                            x = v.tensor_copy(state[:, h, :], new)
                        else:
                            a = h * T + c * 64 + 63
                            x = v.scalar_tensor_tensor(out=state[:, h, :], in0=before[:, h, :], scalar=tf(20, 4)[:, a:a + 1],
                                                       in1=new, op0=ALU.mult, op1=ALU.add)
                    x.then_inc(s["gla_stc"], 1)
                dve.wait_ge(s["gla_o"], 1)
                for h in range(GLA_H):
                    v.tensor_copy(tf(32 + 2 * h, 2), bank[4 + h][:]).then_inc(s["gla_oc"], 1)
                dve.wait_ge(s["gla_oc"], 4)
                link(v.tensor_tensor(tf(8, 8), tf(8, 8), tf(32, 8), ALU.mult))

                def out(i, spread):
                    gain = VCOL["gla_o_gain"] + i % 2
                    return v.scalar_tensor_tensor(out=cm[:, 8 + i, :], in0=spread, scalar=vec[:, gain:gain + 1],
                                                  in1=cm[:, 8 + i, :], op0=ALU.mult, op1=ALU.mult)

                rownorm("gla", GLA_H, 1.0 / GLA_DV, out, ("gla", 0, 8))
                add_projection(2)

            def gdn():
                norm("gdn", VCOL["norm_w"] + 16)
                dve.wait_ge(s["small_done"], 4)
                softplus_args(SOFT_USE["gdn"], 8, bank[5][0:8, 0:T], cols[0:8, 5:6], 1.0)
                softplus_tail(8, rows[0:8, 3])
                v.tensor_scalar(rows[0:8, 1], rows[0:8, 3], ncols[0:8, 1:2], None, ALU.mult).then_inc(s["gdn_row_free"], 1)
                dve.wait_ge(s["gdn_row_free"], 1)
                for c in range(NT):
                    x = v.tensor_tensor_scan(rows[0:8, 2, c * P:(c + 1) * P], ones[0:8, :], rows[0:8, 1, c * P:(c + 1) * P],
                                             0.0, ALU.mult, ALU.add)
                dve.wait_ge(s["gdn_beta_exp"], 1)
                link(v.tensor_scalar(rows[0:8, 0], rows[0:8, 0], 1.0, None, ALU.add))
                v.reciprocal(rows[0:8, 0], rows[0:8, 0]).then_inc(s["row_ready"], 1)

                def gdn_conv(k):
                    dve.wait_ge(s["proj_copied"], PROJ_BASE["gdn"] + 2 * k + 2)
                    conv_silu(3 + k, 4 * k, VCOL["gdn_conv_w"] + 4 * k, 16, None, (s["gdn_conv_done"], k + 1))

                gdn_conv(0)
                dve.wait_ge(s["row_turned"], ROW_USE["gdn"])
                v.tensor_copy(tok[:, 0:4, 0:8], bank[5][:, T:T + 32].rearrange("p (a b) -> p a b", a=4)).then_inc(s["col_ready"], 1)
                dve.wait_ge(s["col_ready"], 2)
                v.tensor_scalar(tok[:, 6:8, 0:8], tok[:, 2:4, 0:8], -1.0, None, ALU.mult)
                v.tensor_copy(tok[:, 5, 0:8], tok[:, 1, 0:8])
                for k in (1, 2, 3):
                    gdn_conv(k)
                dve.wait_ge(s["gdn_last"], 1)
                v.tensor_tensor(tok[:, 4, 0:8], bank[5][:, T + 32:T + 40], tok[:, 0, 0:8],
                                ALU.subtract).then_inc(s["gdn_col_arg"], 1)

                def qk_out(i, spread):
                    return v.scalar_tensor_tensor(out=cm[:, i, :], in0=spread, scalar=float(P) ** -0.5 if i < 4 else 1.0,
                                                  in1=cm[:, i, :], op0=ALU.mult, op1=ALU.mult)

                rownorm("gdn_qk", 8, 1.0, qk_out)
                dve.sem_inc(s["gdn_qk_ready"], 1)
                silu_z(3, 16)
                for k in range(4):
                    c, hf = k // 2, k % 2
                    dve.wait_ge(s["gdn_xt"], k + 1)
                    v.tensor_tensor(vtm[:, c, hf * BLK:(hf + 1) * BLK].rearrange("p (h d) -> p h d", h=4), b4(k % 2),
                                    tok[:, 2 + c, 4 * hf:4 * hf + 4].unsqueeze(2).to_broadcast([P, 4, P]),
                                    ALU.mult).then_inc(s["gdn_xtc"], 1)
                dve.wait_ge(s["gdn_xtc"], 4)
                dve.wait_ge(s["gdn_col_exp"], 1)
                link(v.tensor_tensor(tok[:, 5, 0:8], tok[:, 5, 0:8], tok[:, 3, 0:8], ALU.mult))
                dve.wait_ge(s["gdn_kt"], 1)
                for dst, b, col in ((g_kdec, 2, 4), (g_kbg, 3, 5)):
                    x = v.tensor_tensor(dst.rearrange("p (h r d) -> p h r d", h=4, r=2), b4(b).unsqueeze(2).to_broadcast([P, 4, 2, P]),
                                        tok[:, col, 0:8].rearrange("p (h r) -> p h r", r=2).unsqueeze(3).to_broadcast([P, 4, 2, P]),
                                        ALU.mult)
                x.then_inc(s["gdn_ktc"], 1)
                dve.wait_ge(s["gdn_ktc"], 1)
                for c in range(NT):
                    for hf in (0, 1):
                        b = g_banks[hf]
                        dve.wait_ge(s["gdn_bc"], 2 * c + hf + 1)
                        if c:
                            dve.wait_ge(s["gdn_uw"], hf + 1)
                        for j in range(4):
                            col = tok[:, c, 4 * hf + j:4 * hf + j + 1]
                            v.tensor_scalar(g_dt[hf][:, j * P:(j + 1) * P], b4(b[0])[:, j, :], col, 0.0, ALU.subtract, ALU.min)
                            x = v.tensor_scalar(g_d[hf][:, j * P:(j + 1) * P], b4(b[0])[:, j, :], col, 0.0,
                                                ALU.subtract, ALU.max)
                        x.then_inc(s["gdn_arg"], 1)
                        v.tensor_tensor(g_km[hf], b4(b[1])[:, 0:2, :], slower[:].unsqueeze(1).to_broadcast([P, 2, P]), ALU.mult)
                        link(v.tensor_tensor(g_qm[hf], b4(b[1])[:, 2:4, :], upper[:].unsqueeze(1).to_broadcast([P, 2, P]), ALU.mult))
                    for hf in (0, 1):
                        dve.wait_ge(s["gdn_exp"], 2 * c + hf + 1)
                        for j in range(4):
                            h = 4 * hf + j
                            x = v.scalar_tensor_tensor(out=g_QT[hf][:, j * P:(j + 1) * P], in0=g_km[hf][:, j // 2, :],
                                                       scalar=tok[:, 6 + c, h:h + 1], in1=g_d[hf][:, j * P:(j + 1) * P],
                                                       op0=ALU.mult, op1=ALU.mult)
                        x.then_inc(s["gdn_x"], 1)

                    def pairs(a):
                        return a.rearrange("p (h r d) -> p h r d", h=2, r=2)

                    for hf in (0, 1):
                        dve.wait_ge(s["gdn_q_ready"], 12 * c + hf + 1)
                        v.tensor_tensor(g_R[hf].rearrange("p (h d) -> p h d", h=4), g_Q[hf].rearrange("p (h d) -> p h d", h=4),
                                        ident[:].unsqueeze(1).to_broadcast([P, 4, P]), ALU.add).then_inc(s["gdn_r_ready"], 1)
                    for j in range(6):
                        for hf in (0, 1):
                            dve.wait_ge(s["gdn_power"], 12 * c + 2 * j + hf + 1)
                            v.tensor_copy(g_QT[hf], bank[g_banks[hf][4]][:]).then_inc(s["gdn_qt_ready"], 1)
                        for hf in (0, 1):
                            dve.wait_ge(s["gdn_r"], 12 * c + 2 * j + hf + 1)
                            dve.wait_ge(s["gdn_r_ready"], 14 * c + 2 * j + hf + 1)
                            v.tensor_tensor(g_R[hf], g_R[hf], bank[g_banks[hf][2]][:], ALU.add).then_inc(s["gdn_r_ready"], 1)
                        if j < 2:
                            v.tensor_tensor(pairs(g_qkk[2 * c + j]), pairs(g_dt[j]), g_qm[j].unsqueeze(2).to_broadcast([P, 2, 2, P]),
                                            ALU.mult)
                            if c == 1:
                                v.tensor_tensor(pairs(g_qd[j]), pairs(g_qd[j]),
                                                cm[:, 2 * j:2 * j + 2, P:T].unsqueeze(2).to_broadcast([P, 2, 2, P]), ALU.mult)
                    if c == 1:
                        for hf in (0, 1):
                            dve.wait_ge(s["gdn_uw"], 2 * c + hf + 1)
                            v.tensor_copy(g_w[hf], bank[g_banks[hf][4]][:]).then_inc(s["gdn_w_ready"], 1)
                dve.wait_ge(s["gdn_s"], 1)
                for k in (0, 1):
                    x = v.tensor_copy(tf(40 + 2 * k, 2), bank[k][:])
                x.then_inc(s["gdn_s_ready"], 1)
                dve.wait_ge(s["gdn_ws"], 1)
                for k in (0, 1):
                    x = v.tensor_tensor(g_u[2 + k], g_u[2 + k], bank[2 + k][:], ALU.subtract)
                x.then_inc(s["gdn_new"], 1)
                dve.wait_ge(s["gdn_o"], 1)
                for k in range(4):
                    v.tensor_copy(tf(2 * k, 2), bank[4 + k][:]).then_inc(s["gdn_oc"], 1)
                dve.wait_ge(s["gdn_oc"], 4)
                link(v.tensor_tensor(tf(16, 8), tf(16, 8), tf(0, 8), ALU.mult))

                def out(i, spread):
                    gain = VCOL["gdn_o_gain"]
                    return v.scalar_tensor_tensor(out=cm[:, 16 + i, :], in0=spread, scalar=vec[:, gain:gain + 1],
                                                  in1=cm[:, 16 + i, :], op0=ALU.mult, op1=ALU.mult)

                rownorm("gdn_o", 8, 1.0 / P, out, ("gdn", 0, 16))
                add_projection(3)

            fox(0, 1, "fox0")
            gla()
            gdn()
            fox(1, 4, "fox1")

        @block.tensor
        def _(pe):
            mm, tr = nc.tensor.matmul, nc.tensor.transpose

            def norm(name):
                u = NORMS.index(name)
                for t in range(NT):
                    pe.wait_ge(s["xn_ready"], NT * u + t + 1)
                    for k in range(4):
                        x = tr(b2(6 + k // 2)[:, k % 2, t * P:(t + 1) * P], hn[:, t, k * P:(k + 1) * P], ident[:])
                        if t == NT - 1 and k % 2:
                            x.then_inc(s["turned"], 1)
                for b in (2, 3):
                    pe.wait_ge(s["hnT_act"] if b == 2 else s["hnT_dve"], 2 * u + 1)
                    for j in (0, 1):
                        for t in range(NT):
                            k = 2 * b + j
                            x = tr(b2(6 + b % 2)[:, j, t * P:(t + 1) * P], hn[:, t, k * P:(k + 1) * P], ident[:])
                    x.then_inc(s["turned"], 1)

            def normed(name):
                u = NORMS.index(name)
                pe.wait_ge(s["hnT_act"], 2 * u + 2)
                pe.wait_ge(s["hnT_dve"], 2 * u + 2)

            def split_ready(name):
                pe.wait_ge(s["hnT_split"], 2 * SPLIT_NORMS.index(name) + 2)

            def small(dst, w, last=True):
                for k in range(KD):
                    x = mm(dst, w[:, k, :], hnT[:, k, :], start=(k == 0), stop=(k == KD - 1))
                if last:
                    x.then_inc(s["small_done"], 1)

            def products(dst, stationary, moving, start, stop):
                (sh, sl), (mh, ml) = stationary, moving
                mm(dst, sh, mh, start=start, stop=False)
                mm(dst, sh, ml, start=False, stop=False)
                return mm(dst, sl, mh, start=False, stop=stop)

            def project(name, first, end):
                for i in range(first, end):
                    kind = KINDS[name][i]
                    for m in range(UNITS):
                        u, g = UNIT_BASE[name] + UNITS * i + m, PROJ_BASE[name] + 2 * i
                        if m == 0 and g >= 4:
                            pe.wait_ge(s["proj_copied"], g - 3)
                        if m == (2 if kind == "channels" else 0) and g >= 4:
                            pe.wait_ge(s["proj_copied"], g - 2)
                        pe.wait_ge(s["low_ready"], u + 1)
                        if kind == "channels":
                            wh, wl = part(w_h, u, P), part(w_l, u, P)
                            for k in range(KD):
                                x = products(b2((g + m // 2) % 4)[:, m % 2, :], (wh[:, k, :], wl[:, k, :]),
                                             (hnT_h[:, k, :], hnT_l[:, k, :]), k == 0, k == KD - 1)
                        else:
                            wh, wl = part(w_h, u, BLK), part(w_l, u, BLK)
                            for t in range(NT):
                                for j in (0, 1):
                                    k, tt = 2 * m + j, slice(t * P, (t + 1) * P)
                                    x = products(bank[(g + t) % 4][:], (hnT_h[:, k, tt], hnT_l[:, k, tt]),
                                                 (wh[:, j, :], wl[:, j, :]), k == 0, k == KD - 1)
                        x.then_inc(s["unit_done"], 1)

            def sum_squares(name, R, pick, batches=None):
                _, before, n = ROWN[name]
                for i in range(n):
                    if batches is not None and i // 4 not in batches:
                        continue
                    g = (before + i) // 4
                    if i % 4 == 0:
                        pe.wait_ge(s["sq_ready"], g + 1)
                    for t in range(NT):
                        x = mm(bank[SUM_BANK][:, t * R:(t + 1) * R], sq[:, g % 2, i % 4, t * P:(t + 1) * P], pick(i),
                               start=(i == 0 and t == 0), stop=(i == n - 1 and t == NT - 1), skip_group_check=True)
                    if i % 4 == 3:
                        x.then_inc(s["sq_summed"], 1)

            def spread(name, R, pick):
                r, _, n = ROWN[name]
                pe.wait_ge(s["rownorm_ready"], r + 1)
                for b in range(n // 2 // SHARE.get(name, 1)):
                    g = SPREAD_BASE[name] + b
                    if g >= 2:
                        pe.wait_ge(s["spread_used"], SPREAD_END[g - 2])
                    for j in (0, 1):
                        picked = pick(2 * b + j)
                        m = P // len(picked)
                        for i, head in enumerate(picked):
                            for t in range(NT):
                                a = t * R + head
                                x = mm(b2(6 + g % 2)[m * i:m * i + m, j, t * P:(t + 1) * P],
                                       heads[:, 1, a:a + 1].to_broadcast([P, m]), ident[:], start=True, stop=True)
                    x.then_inc(s["spread_done"], 1)

            def out_projection(name, groups=None):
                for g in (range(OUT_GROUPS[name]) if groups is None else groups):
                    for n in (0, 1):
                        if name == "ssd" and g == 0 and n == 1:
                            pe.wait_ge(s["ssd_yready"], 1)
                        for m in range(UNITS):
                            u = UNIT_BASE[name + "_out"] + UNITS * (2 * g + n) + m
                            if n == 0:
                                pe.wait_ge(s["out_low"], PAIR_BASE[name] + 4 * g + m + 1)
                            pe.wait_ge(s["low_ready"], u + 1)
                            wh, wl = part(w_h, u, BLK), part(w_l, u, BLK)
                            for t in range(NT):
                                for j in (0, 1):
                                    k, tt = 2 * m + j, slice(t * P, (t + 1) * P)
                                    x = products(bank[t + 2 * n][:], (hnT_h[:, k, tt], hnT_l[:, k, tt]),
                                                 (wh[:, j, :], wl[:, j, :]), g == 0 and k == 0,
                                                 g == OUT_GROUPS[name] - 1 and k == KD - 1)
                            x.then_inc(s["unit_done"], 1)

            pe.wait_ge(s["ident_ready"], 1)
            pe.wait_ge(s["vec_loaded"], 16 * (len(VEC_A) + len(VEC_B)))
            tr(bank[5][:, 0:NA], cm[0:NA, 0, 0:P], ident[0:NA, 0:NA]).then_inc(s["vec_turned"], 1)
            tr(bank[5][:, P:P + NB], cm[0:NB, 1, 0:P], ident[0:NB, 0:NB]).then_inc(s["vec_turned"], 1)
            norm("ssd")
            pe.wait_ge(s["small_loaded"], 16 * N_EARLY)
            normed("ssd")
            pe.wait_ge(s["vec_ready"], 1)
            small(bank[5][0:16, 0:T], w_dt)
            pe.wait_ge(s["consts_ready"], 1)
            split_ready("ssd")
            project("ssd", 0, 3)
            pe.wait_ge(s["row_ready"], 1)
            for k in range(4):
                c = k % 2
                x = tr(bank[5][:, T + 16 * k:T + 16 * k + 16], rows[0:16, 2 + k // 2, c * P:(c + 1) * P], ident[0:16, 0:16])
            x.then_inc(s["row_turned"], 1)
            project("ssd", 3, 11)
            pe.wait_ge(s["ssd_conv_done"], 3)
            pe.wait_ge(s["proj_copied"], 22)
            for k in range(4):
                c, hf = k // 2, k % 2
                if k >= 2:
                    pe.wait_ge(s["ssd_xt_used"], k - 1)
                for j in range(4):
                    x = tr(b4(k % 2)[:, j, :], cm[:, 8 + 4 * hf + j, c * P:(c + 1) * P], ident[:])
                x.then_inc(s["ssd_xt_done"], 1)
                if k == 1:
                    sum_squares("sc", 16, lambda i: colsel64[:, i, :])
            pe.wait_ge(s["col_ready"], 1)
            for g in range(2):
                tr(b4(3)[:, g, :], cm[:, 16 + g, 0:P], ident[:])
            mm(bank[3][:, 2 * P:2 * P + 16], row_of(P - 1, P), tok[:, 0, :], start=True, stop=True)
            for j in range(4):
                c, g = j // 2, j % 2
                x = mm(b4(2)[:, j, :], cm[:, 16 + g, c * P:(c + 1) * P], cm[:, 18 + g, c * P:(c + 1) * P], start=True, stop=True)
            x.then_inc(s["ssd_g_done"], 1)
            spread("sc", 16, lambda i: [2 * i, 2 * i + 1])
            pe.wait_ge(s["ssd_xdte"], 1)
            pe.wait_ge(s["spread_used"], 4)
            for g in range(2):
                x = mm(bank[6 + g][:], tiles(30, 1, P)[:, g, :], hn[:, 0, g * BLK:(g + 1) * BLK], start=True, stop=True)
            x.then_inc(s["ssd_state"], 1)

            def ssd_spread(i):
                c, hq = i // 4, i % 4
                if i >= 2:
                    pe.wait_ge(s["ssd_exp"], i - 1)
                for j in range(4):
                    x = mm(b4(i % 2)[:, j, :], row_of(4 * hq + j, 16), rows[0:16, 2, c * P:(c + 1) * P], start=True, stop=True)
                x.then_inc(s["ssd_bc"], 1)

            pe.wait_ge(s["ssd_xt_used"], 4)
            ssd_spread(0)
            for i in range(8):
                c, hq = i // 4, i % 4
                if i < 7:
                    ssd_spread(i + 1)
                pe.wait_ge(s["ssd_m"], i + 1)
                if c == 1:
                    pe.wait_ge(s["ssd_state_used"], 1)
                for j in range(4):
                    h = 4 * hq + j
                    dst = b2(2 + hq)[64 * (h % 2):64 * (h % 2) + 64, j // 2, c * P:(c + 1) * P]
                    m = hnTf[:, (i % 2) * 512 + j * P:(i % 2) * 512 + (j + 1) * P]
                    x = mm(dst, vtm[:, c, 64 * h:64 * h + 64], m, start=True, stop=(c == 0))
                    if c == 1:
                        ce = hnTf[:, 1024 + (i % 2) * 512 + j * P:1024 + (i % 2) * 512 + (j + 1) * P]
                        x = mm(dst, hn[:, 1, 64 * h:64 * h + 64], ce, start=False, stop=True)
                x.then_inc(s["ssd_y"], 1)
            out_projection("ssd", [0])
            pe.wait_ge(s["ssd_yready"], 2)
            sum_squares("ssd", 2, lambda i: column(i // 4, 2))
            spread("ssd", 2, lambda i: [i])
            out_projection("ssd", [1])

            u = NORMS.index("moe")
            for t in range(NT):
                pe.wait_ge(s["x_ready"], X_BEFORE["moe"] - 1 + t)
                for k in range(KD):
                    b = [6, 7, 4, 0][k // 2]
                    x = tr(b2(b)[:, k % 2, t * P:(t + 1) * P], x_res[:, t, k * P:(k + 1) * P], ident[:])
                    if t == NT - 1 and k % 2:
                        x.then_inc(s["turned"], 1)
            normed("moe")
            pe.wait_ge(s["late_loaded"], 16 * N_LATE)
            for t in range(NT):
                for k in range(KD):
                    x = mm(bank[5][:, t * (NG + NE):(t + 1) * (NG + NE)], hnT[:, k, t * P:(t + 1) * P], w_rt[:, k, :],
                           start=(k == 0), stop=(k == KD - 1))
            x.then_inc(s["rt_done"], 1)
            pe.wait_ge(s["rt_mask"], 1)
            mm(bank[5][:, P:P + NE], supper[:], r_mask[:, 0, :], start=True, stop=True)
            mm(bank[5][:, P + NE:P + 2 * NE], ones[:], r_mask[:, 0, :], start=True, stop=False)
            mm(bank[5][:, P + NE:P + 2 * NE], supper[:], r_mask[:, 1, :], start=False, stop=True)
            for t in range(NT):
                x = mm(bank[5][:, T:T + NE], ones[:], r_mask[:, t, :], start=(t == 0), stop=(t == 1))
            x.then_inc(s["rt_rank"], 1)

            def gather(g, acc):
                pe.wait_ge(s["moe_sel"], g + 1)
                pe.wait_ge(s["moe_acc"], acc)
                for k in range(KD):
                    for t in range(NT):
                        x = mm(b4(5 + k // 4)[:, k % 4, :], hn[:, t, k * P:(k + 1) * P], m_S[:, t, :],
                               start=(t == 0), stop=(t == NT - 1))
                x.then_inc(s["moe_gath"], 1)

            def pe_quad(q, it, g, wait_slot, release):
                pe.wait_ge(s["moe_xg"], g + 1)
                pe.wait_ge(s["moe_h"], it + 1)
                for j in range(STEPS_UP):
                    w = wait_slot(q, j).rearrange("p (a e f) -> p a e f", a=2, e=QUAD)
                    for a in (0, 1):
                        for e in range(QUAD):
                            x = mm(bank[a][CAP * e:CAP * (e + 1), :], m_xg[:, j, CAP * e:CAP * (e + 1)], w[:, a, e, :],
                                   start=(j == 0), stop=(j == STEPS_UP - 1), tile_position=(0, CAP * e))
                    x.then_inc(release, 1)
                gather(g + 1, it + 1)
                pe.wait_ge(s["moe_sg"], it + 1)
                pe.wait_ge(s["moe_gtc"], it + 1)
                for t in range(NT):
                    x = tr(bank[7][:, t * P:(t + 1) * P], m_SG[:, t, :], ident[:])
                x.then_inc(s["moe_gt"], 1)
                pe.wait_ge(s["moe_h"], it + 2)
                pe.wait_ge(s["moe_htc"], it + 1)
                for c in range(STEPS_DOWN):
                    x = tr(b4(2)[:, c, :], m_h[:, c * P:(c + 1) * P], ident[:])
                x.then_inc(s["moe_ht"], 1)
                pe.wait_ge(s["moe_htc"], it + 2)
                pe.wait_ge(s["moe_acc"], it + 1)
                for c in range(STEPS_DOWN):
                    w = wait_slot(q, STEPS_UP + c).rearrange("p (e n) -> p e n", e=QUAD)
                    for n in (0, 1):
                        for e in range(QUAD):
                            x = mm(bank[3 + n][CAP * e:CAP * (e + 1), :], m_ht[:, c * P + CAP * e:c * P + CAP * (e + 1)],
                                   w[:, e, n * BLK:(n + 1) * BLK], start=(c == 0), stop=(c == STEPS_DOWN - 1),
                                   tile_position=(0, CAP * e))
                    x.then_inc(release, 1)
                pe.wait_ge(s["moe_gtc"], it + 2)
                pe.wait_ge(s["moe_ya"], it + 1)
                pe.wait_ge(s["moe_yd"], it + 1)
                pe.wait_ge(s["moe_xg"], g + 2)
                for k in range(4):
                    t, n = k // 2, k % 2
                    x = mm(bank[[5, 6, 3, 4][k]][:], m_gt[:, t * P:(t + 1) * P], m_y[:, n, :], start=True, stop=True)
                x.then_inc(s["moe_scat"], 1)

            base = RING_BASE["moe"]

            def ring_slot(q, j):
                i = (base + j) % SLOTS
                pe.wait_ge(ready[i], q * (32 * MOE_STEPS // SLOTS) + slot_value(base + j))
                return ring[:, i, :]

            gather(0, 1)
            with pe.Fori(0, NQ) as q:
                pe_quad(q, q, q, ring_slot, s["ring_used"])
            passes = pe.value_load(count_i[0:1, 0:1], min_val=1, max_val=T // CAP)
            with pe.If(passes > 1):
                with pe.Fori(1, passes) as p:
                    gather(p * (NQ + 1), p * NQ + 1)

                    def ov_slot(q, j):
                        pe.wait_ge(ov_ready, (p - 1) * (32 * NQ * MOE_STEPS) + q * (32 * MOE_STEPS) + 32 * (j + 1))
                        return ring[:, 0, :]

                    with pe.Fori(0, NQ) as q:
                        pe_quad(q, p * NQ + q, p * (NQ + 1) + q, ov_slot, ov_used)

            def turn_rows(use, name, pairs):
                pe.wait_ge(s["row_ready"], use)
                for k, (src, R) in enumerate(pairs):
                    x = tr(bank[5][:, T + R * k:T + R * k + R], src, ident[0:R, 0:R])
                x.then_inc(s["row_turned"], 1)

            def fox(occ, li, name):
                norm(name)
                normed(name)
                small(bank[5][0:FOX_H, 0:T], w_f[:, occ])
                split_ready(name)
                project(name, 0, 2)
                turn_rows(ROW_USE[name], name, [(rows[0:FOX_H, 3, t * P:(t + 1) * P], FOX_H) for t in range(NT)])
                for k in range(4):
                    project(name, 2 + k, 3 + k)
                    sum_squares(name, 16, lambda i: column(i, 16), [k])
                project(name, 6, 7)
                spread(name, 16, lambda i: [i])
                project(name, 7, 8)
                pe.wait_ge(s["proj_copied"], PROJ_BASE[name] + 16)
                pe.wait_ge(s["qk_ready"], occ + 1)

                def scores(h):
                    k = occ * FOX_H + h
                    if h >= 3:
                        pe.wait_ge(s["fox_l"], k - 2)
                    q, kk = cm[:, h, :], cm[:, 8 + h, :]
                    for t, (a, b) in enumerate(((0, P), (P, 3 * P))):
                        mm(bank[f_banks[h % 3]][:, a:b], q[:, t * P:(t + 1) * P], kk[:, 0:b - a], start=True, stop=False)
                        x = mm(bank[f_banks[h % 3]][:, a:b], row_of(h, FOX_H), rows[0:FOX_H, 2, 0:b - a], start=False, stop=True)
                    x.then_inc(s["fox_s"], 1)

                for h in range(3):
                    scores(h)
                for h in range(FOX_H):
                    k = occ * FOX_H + h
                    pe.wait_ge(s["fox_p"], k + 1)
                    if h >= 2:
                        pe.wait_ge(s["fox_tc"], k - 1)
                    for j in range(3):
                        x = tr(bank[2 + h % 2][:, j * P:(j + 1) * P], f_p[h % 2][:, j * P:(j + 1) * P], ident[:])
                    x.then_inc(s["fox_t"], 1)
                    if h < FOX_H - 3:
                        scores(h + 3)
                    pe.wait_ge(s["fox_tc"], k + 1)
                    if h >= 2:
                        pe.wait_ge(s["fox_oc"], k - 1)
                    o, pt = bank[6 + h % 2], f_pt[h % 2]
                    mm(o[:, 0:P], vtm[:, 0, h * P:(h + 1) * P], pt[:, 0:P], start=True, stop=True)
                    mm(o[:, P:T], vtm[:, 0, h * P:(h + 1) * P], pt[:, P:2 * P], start=True, stop=False)
                    mm(o[:, P:T], vtm[:, 1, h * P:(h + 1) * P], pt[:, 2 * P:3 * P], start=False, stop=True)\
                        .then_inc(s["fox_o"], 1)
                out_projection(name)

            def gla():
                norm("gla")
                normed("gla")
                small(bank[5][0:16, 0:T], w_low)
                split_ready("gla")
                project("gla", 0, 1)
                pe.wait_ge(s["gla_low"], 1)
                for h in range(GLA_H):
                    x = mm(b2(4 + h // 2)[:, h % 2, :], w_gup[:, h * P:(h + 1) * P], rows[0:16, 0], start=True, stop=True)
                x.then_inc(s["gla_gate"], 1)
                project("gla", 1, 6)
                pe.wait_ge(s["proj_copied"], PROJ_BASE["gla"] + 12)
                pe.wait_ge(s["gla_qk"], 1)
                for h in range(GLA_H):
                    for t in range(NT):
                        i, tt = 2 * h + t, slice(t * P, (t + 1) * P)
                        x = mm(b4(i // 4)[:, i % 4, :], cm[:, 4 + h, tt], cm[:, h, tt], start=True, stop=True)
                x.then_inc(s["gla_at"], 1)
                for t in range(NT):
                    for h in range(GLA_H):
                        x = tr(b4(2 + t)[:, h, :], cm[:, 28 + h, t * P:(t + 1) * P], ident[:])
                x.then_inc(s["gla_kt"], 1)

                kdec = [tf(40 + 2 * t, 2) for t in range(NT)]

                def update(c):
                    t, lo = c // 2, 64 * (c % 2)
                    for h in range(GLA_H):
                        x = mm(b2(2 * (c % 2) + h // 2)[:, h % 2, :], kdec[t][lo:lo + 64, h * P:(h + 1) * P],
                               vtm[lo:lo + 64, t, h * GLA_DV:(h + 1) * GLA_DV], start=True, stop=True)
                    x.then_inc(s["gla_st"], 1)

                pe.wait_ge(s["gla_atc"], 1)
                for h in range(GLA_H):
                    for j in (0, 1):
                        for t in range(NT):
                            i = 2 * h + t
                            mm(b2(4 + h)[:, j, t * P:(t + 1) * P], vtm[:, t, h * GLA_DV + j * P:h * GLA_DV + (j + 1) * P],
                               tiles(24, 4, P)[:, i, :], start=(j == 0 and t == 0), stop=False, skip_group_check=True)
                pe.wait_ge(s["gla_ktc"], 1)
                update(0)
                update(1)
                for c in range(1, 4):
                    pe.wait_ge(s["gla_stc"], c)
                    for h in range(GLA_H):
                        for j in (0, 1):
                            x = mm(b2(4 + h)[:, j, c * 64:(c + 1) * 64], gla_states[(c - 1) % 2][:, h, j * P:(j + 1) * P],
                                   cm[:, h, c * 64:(c + 1) * 64], start=False, stop=(c == 3 and j == 1), skip_group_check=True)
                    if c == 1:
                        update(2)
                x.then_inc(s["gla_o"], 1)
                sum_squares("gla", GLA_H, lambda i: column(i // 2, GLA_H))
                spread("gla", GLA_H, lambda i: [i])
                out_projection("gla")

            def gdn():
                norm("gdn")
                normed("gdn")
                small(bank[5][0:8, 0:T], w_ab[:, :, 0:8], last=False)
                small(bank[5][0:8, T:2 * T], w_ab[:, :, 8:16])
                split_ready("gdn")
                project("gdn", 0, 2)
                turn_rows(ROW_USE["gdn"], "gdn", [(rows[0:8, r, t * P:(t + 1) * P], 8) for r in (2, 0) for t in range(NT)])
                project("gdn", 2, 3)
                pe.wait_ge(s["col_ready"], 2)
                mm(bank[5][:, T + 32:T + 40], row_of(P - 1, P), tok[:, 0, 0:8], start=True, stop=True).then_inc(s["gdn_last"], 1)
                project("gdn", 3, 4)
                project("gdn", 4, 5)
                sum_squares("gdn_qk", 8, lambda i: column(i, 8), [0])
                project("gdn", 5, 6)
                sum_squares("gdn_qk", 8, lambda i: column(i, 8), [1])
                spread("gdn_qk", 8, lambda i: [i])
                pe.wait_ge(s["gdn_conv_done"], 4)
                pe.wait_ge(s["proj_copied"], PROJ_BASE["gdn"] + 12)
                for k in range(4):
                    c, hf = k // 2, k % 2
                    if k >= 2:
                        pe.wait_ge(s["gdn_xtc"], k - 1)
                    for j in range(4):
                        x = tr(b4(k % 2)[:, j, :], cm[:, 8 + 4 * hf + j, c * P:(c + 1) * P], ident[:])
                    x.then_inc(s["gdn_xt"], 1)
                pe.wait_ge(s["gdn_qk_ready"], 1)
                for c in range(NT):
                    for h in range(GDN_QH):
                        x = tr(b4(2 + c)[:, h, :], cm[:, 4 + h, c * P:(c + 1) * P], ident[:])
                x.then_inc(s["gdn_kt"], 1)
                pe.wait_ge(s["gdn_xtc"], 4)

                def blocks(a):
                    return a.rearrange("p (h d) -> p h d", d=P)

                def decays(c, hf):
                    b, cc = g_banks[hf], slice(c * P, (c + 1) * P)
                    for j in range(4):
                        mm(b4(b[0])[:, j, :], row_of(4 * hf + j, 8), rows[0:8, 2, cc], start=True, stop=True)
                    for j in range(2):
                        k = cm[:, 4 + 2 * hf + j, cc]
                        mm(b4(b[1])[:, j, :], k, k, start=True, stop=True)
                        x = mm(b4(b[1])[:, 2 + j, :], k, cm[:, 2 * hf + j, cc], start=True, stop=True)
                    x.then_inc(s["gdn_bc"], 1)

                decays(0, 0)
                for c in range(NT):
                    decays(c, 1)
                    if c == 0:
                        pe.wait_ge(s["gdn_ktc"], 1)
                    for hf in (0, 1):
                        pe.wait_ge(s["gdn_x"], 2 * c + hf + 1)
                        if c:
                            pe.wait_ge(s["gdn_u_ready"], hf + 1)
                        for j in range(4):
                            x = tr(b4(g_banks[hf][3])[:, j, :], blocks(g_QT[hf])[:, j, :], ident[:])
                        x.then_inc(s["gdn_turned"], 1)
                    for j in range(6):
                        for hf in (0, 1):
                            Q, QT = blocks(g_Q[hf]), blocks(g_QT[hf])
                            pe.wait_ge(s["gdn_q_ready"], 12 * c + 2 * j + hf + 1)
                            if c or j:
                                pe.wait_ge(s["gdn_qt_ready"], 12 * c + 2 * j + hf - 1)
                            for h in range(4):
                                if j < 5:
                                    mm(b4(g_banks[hf][3])[:, h, :], QT[:, h, :], Q[:, h, :], start=True, stop=True)
                                x = mm(b4(g_banks[hf][4])[:, h, :], Q[:, h, :], QT[:, h, :], start=True, stop=True)
                            x.then_inc(s["gdn_power"], 1)
                        for hf in (0, 1):
                            QT, R = blocks(g_QT[hf]), blocks(g_R[hf])
                            pe.wait_ge(s["gdn_qt_ready"], 12 * c + 2 * j + hf + 1)
                            pe.wait_ge(s["gdn_r_ready"], 14 * c + 2 * j + hf + 1)
                            for h in range(4):
                                x = mm(b4(g_banks[hf][2])[:, h, :], QT[:, h, :], R[:, h, :], start=True, stop=True)
                            x.then_inc(s["gdn_r"], 1)
                    if c == 0:
                        decays(1, 0)
                    for hf in (0, 1):
                        pe.wait_ge(s["gdn_r_ready"], 14 * c + 13 + hf)
                        R = blocks(g_R[hf])
                        for h in range(4):
                            if c == 1:
                                mm(b4(g_banks[hf][4])[:, h, :], blocks(g_kbg)[:, 4 * hf + h, :], R[:, h, :], start=True, stop=True)
                            x = mm(b4(g_banks[hf][3])[:, h, :], R[:, h, :], vtm[:, c, (4 * hf + h) * P:(4 * hf + h + 1) * P],
                                   start=True, stop=True)
                        x.then_inc(s["gdn_uw"], 1)
                pe.wait_ge(s["gdn_u_ready"], 4)
                pe.wait_ge(s["gdn_w_ready"], 2)
                u = [blocks(g_u[i]) for i in range(4)]
                qkk = [blocks(g_qkk[i]) for i in range(4)]
                state = tiles(40, 4, P)
                for h in range(8):
                    x = mm(b4(h // 4)[:, h % 4, :], blocks(g_kdec)[:, h, :], u[h // 4][:, h % 4, :], start=True, stop=True)
                x.then_inc(s["gdn_s"], 1)
                for h in range(8):
                    mm(b2(4 + h // 2)[:, h % 2, 0:P], u[h // 4][:, h % 4, :], qkk[h // 4][:, h % 4, :], start=True, stop=True)
                pe.wait_ge(s["gdn_s_ready"], 1)
                for h in range(8):
                    x = mm(b4(2 + h // 4)[:, h % 4, :], blocks(g_w[h // 4])[:, h % 4, :], state[:, h, :], start=True, stop=True)
                x.then_inc(s["gdn_ws"], 1)
                pe.wait_ge(s["gdn_new"], 1)
                for h in range(8):
                    dst = b2(4 + h // 2)[:, h % 2, P:T]
                    mm(dst, state[:, h, :], blocks(g_qd[h // 4])[:, h % 4, :], start=True, stop=False)
                    x = mm(dst, u[2 + h // 4][:, h % 4, :], qkk[2 + h // 4][:, h % 4, :], start=False, stop=True)
                x.then_inc(s["gdn_o"], 1)
                sum_squares("gdn_o", 8, lambda i: column(i, 8))
                spread("gdn_o", 8, lambda i: [i])
                out_projection("gdn")

            fox(0, 1, "fox0")
            gla()
            gdn()
            fox(1, 4, "fox1")


_INS = ["x", "norm_mix", "w_in", "ssd_conv_w", "ssd_conv_b", "dt_bias", "a_log", "d_skip", "ssd_norm", "sc_conv_w",
        "sc_norm", "w_out", "norm_ffn", "w_router_group", "w_router_expert", "w_gate", "w_up", "w_down", "final_norm",
        "norm_w_2", "fox_w_in_2", "fox_b_f_2", "fox_q_gain_2", "fox_k_gain_2", "fox_w_out_2", "gla_w_in_2",
        "gla_w_gate_up_2", "gla_b_gate_2", "gla_o_gain_2", "gla_w_out_2", "gdn_w_in_2", "gdn_conv_w_2",
        "gdn_a_log_2", "gdn_dt_bias_2", "gdn_o_gain_2", "gdn_w_out_2"]


def kernel(**inputs):
    import numpy as _np
    import concourse.bacc as _bacc
    from concourse.bass_utils import run_bass_kernel_spmd as _run

    nc = _bacc.Bacc("TRN2", target_bir_lowering=False, num_devices=1)
    arrays, args = {}, []
    for name in _INS:
        a = _np.ascontiguousarray(inputs[name])
        if name in ("w_gate", "w_up", "w_down"):
            a = a[0]
        arrays[f"in_{name}"] = a
        args.append(nc.dram_tensor(f"in_{name}", a.shape, F32, kind="ExternalInput").ap())
    out = nc.dram_tensor("out", (1, T, D), F32, kind="ExternalOutput").ap()
    build(nc, *args, out)
    r = _run(nc, [arrays], core_ids=[0])
    return r.results[0]["out"]
```
